# Optimizing a Trainium2 kernel written in Bass

```python
import math
import jax, jax.numpy as jnp
from jax import lax
import numpy as np

D_MODEL = 1024
BATCH = 1
SEQ = 512
DEPTH = 2

EPS = 1e-6
D_FF = 2816
GLA_HEADS = 4
GLA_DK = 128
GLA_DV = 256
GLA_GATE_RANK = 16
GLA_GATE_TAU = 16.0
GLA_CHUNK = 64
GLA_QK = GLA_HEADS * GLA_DK
GLA_V = GLA_HEADS * GLA_DV
SSD_HEADS = 16
SSD_HEADDIM = 64
SSD_STATE = 128
SSD_GROUPS = 2
SSD_CONV = 4
SSD_CHUNK = 128
SSD_INNER = SSD_HEADS * SSD_HEADDIM
SSD_BC = SSD_GROUPS * SSD_STATE
SSD_CONV_CH = SSD_INNER + 2 * SSD_BC
HY_IN_SIZES = (GLA_QK, GLA_QK, GLA_V, GLA_V, GLA_GATE_RANK, SSD_INNER, SSD_CONV_CH, SSD_HEADS)
HY_IN_WIDTH = 2 * GLA_QK + 2 * GLA_V + GLA_GATE_RANK + SSD_INNER + SSD_CONV_CH + SSD_HEADS
MIX_WIDTH = GLA_V + SSD_INNER
DSA_HEADS = 16
DSA_Q_RANK = 256
DSA_LATENT = 128
DSA_VDIM = 64
IDX_HEADS = 16
IDX_DIM = 64
TOPK_MAX = 256
Q_BLOCK = 128
REL_BUCKETS = 32
REL_MAX_DIST = 128

kernel_name = 'hybrid_gla_ssd_dsa_macaron'

def rmsnorm(x, g):
    xf = x.astype(jnp.float32)
    y = xf * lax.rsqrt(jnp.mean(xf * xf, axis=-1, keepdims=True) + EPS)
    return (y * g.astype(jnp.float32)).astype(x.dtype)

def layernorm(x, g, b):
    xf = x.astype(jnp.float32)
    mu = jnp.mean(xf, axis=-1, keepdims=True)
    var = jnp.mean(jnp.square(xf - mu), axis=-1, keepdims=True)
    y = (xf - mu) * lax.rsqrt(var + EPS)
    return (y * g.astype(jnp.float32) + b.astype(jnp.float32)).astype(x.dtype)

def swiglu(h, wg, wu, wd):
    return (jax.nn.silu(h @ wg) * (h @ wu)) @ wd

def split_cols(t, sizes):
    idx = np.cumsum(np.array(sizes))[:-1].tolist()
    return jnp.split(t, idx, axis=-1)

def to_chunks(t, c):
    b, s = t.shape[0], t.shape[1]
    return jnp.moveaxis(t.reshape(b, s // c, c, *t.shape[2:]), 1, 0)

def from_chunks(t):
    t = jnp.moveaxis(t, 0, 1)
    return t.reshape(t.shape[0], t.shape[1] * t.shape[2], *t.shape[3:])

def causal_depthwise_conv(x, w, b):
    k, ch = w.shape
    y = lax.conv_general_dilated(x, w.reshape(k, 1, ch).astype(x.dtype), window_strides=(1,),
                                 padding=[(k - 1, 0)], dimension_numbers=('NWC', 'WIO', 'NWC'),
                                 feature_group_count=ch)
    return y + b.astype(x.dtype)

def gla_chunked(q, k, v, log_a):
    bsz, _, h, dk = q.shape
    dv = v.shape[-1]
    c = GLA_CHUNK
    mask = jnp.tril(jnp.ones((c, c), dtype=bool))[None, :, :, None, None]

    def step(state, inp):
        qc, kc, vc, gc = [t.astype(jnp.float32) for t in inp]
        b = jnp.cumsum(gc, axis=1)
        o_inter = jnp.einsum('bihk,bhkv->bihv', qc * jnp.exp(b), state)
        diff = b[:, :, None] - b[:, None]
        decay = jnp.exp(jnp.where(mask, diff, -jnp.inf))
        attn = jnp.einsum('bijhk,bjhk->bijh', qc[:, :, None] * decay, kc)
        o_intra = jnp.einsum('bijh,bjhv->bihv', attn, vc)
        b_last = b[:, -1]
        k_dec = kc * jnp.exp(b_last[:, None] - b)
        state = state * jnp.exp(b_last)[..., None] + jnp.einsum('bjhk,bjhv->bhkv', k_dec, vc)
        return state, o_inter + o_intra

    state0 = jnp.zeros((bsz, h, dk, dv), jnp.float32)
    _, o = lax.scan(step, state0, (to_chunks(q, c), to_chunks(k, c), to_chunks(v, c), to_chunks(log_a, c)))
    return from_chunks(o).astype(v.dtype)

def ssd_chunked(x, dt, a, bm, cm):
    bsz, _, h, p = x.shape
    n = bm.shape[-1]
    rep = h // bm.shape[2]
    c = SSD_CHUNK
    mask = jnp.tril(jnp.ones((c, c), dtype=bool))[None, :, :, None]

    def step(state, inp):
        xc, dtc, bc, cc = [t.astype(jnp.float32) for t in inp]
        bc = jnp.repeat(bc, rep, axis=2)
        cc = jnp.repeat(cc, rep, axis=2)
        acum = jnp.cumsum(dtc * a.astype(jnp.float32), axis=1)
        diff = acum[:, :, None] - acum[:, None]
        seg = jnp.exp(jnp.where(mask, diff, -jnp.inf))
        xdt = xc * dtc[..., None]
        scores = jnp.einsum('bihn,bjhn->bijh', cc, bc) * seg
        y_intra = jnp.einsum('bijh,bjhp->bihp', scores, xdt)
        y_inter = jnp.einsum('bihn,bhpn->bihp', cc * jnp.exp(acum)[..., None], state)
        a_last = acum[:, -1]
        w = jnp.exp(a_last[:, None] - acum)[..., None]
        state = state * jnp.exp(a_last)[..., None, None] + jnp.einsum('bjhn,bjhp->bhpn', bc * w, xdt)
        return state, y_intra + y_inter

    state0 = jnp.zeros((bsz, h, p, n), jnp.float32)
    _, y = lax.scan(step, state0, (to_chunks(x, c), to_chunks(dt, c), to_chunks(bm, c), to_chunks(cm, c)))
    return from_chunks(y).astype(x.dtype)

def gla_ssd_mixer(h, w_in, gla_w_gate2, gla_b_gate, gla_norm_g, ssd_conv_w, ssd_conv_b,
                  ssd_dt_bias, ssd_a_log, ssd_d, ssd_norm_g, w_out):
    bsz, s, _ = h.shape
    q, k, v, r, g_lr, z, xbc, dt = split_cols(h @ w_in, HY_IN_SIZES)
    q = q.reshape(bsz, s, GLA_HEADS, GLA_DK) * (GLA_DK ** -0.5)
    k = k.reshape(bsz, s, GLA_HEADS, GLA_DK)
    v = v.reshape(bsz, s, GLA_HEADS, GLA_DV)
    log_a = jax.nn.log_sigmoid((g_lr @ gla_w_gate2 + gla_b_gate).astype(jnp.float32)) / GLA_GATE_TAU
    o_gla = gla_chunked(q, k, v, log_a.reshape(bsz, s, GLA_HEADS, GLA_DK))
    o_gla = rmsnorm(o_gla, gla_norm_g.reshape(GLA_HEADS, GLA_DV)).reshape(bsz, s, GLA_V)
    o_gla = o_gla * jax.nn.silu(r)
    xbc = jax.nn.silu(causal_depthwise_conv(xbc, ssd_conv_w, ssd_conv_b))
    xs, bm, cm = split_cols(xbc, (SSD_INNER, SSD_BC, SSD_BC))
    xs = xs.reshape(bsz, s, SSD_HEADS, SSD_HEADDIM)
    dt = jax.nn.softplus((dt + ssd_dt_bias).astype(jnp.float32))
    a = -jnp.exp(ssd_a_log.astype(jnp.float32))
    y = ssd_chunked(xs, dt, a, bm.reshape(bsz, s, SSD_GROUPS, SSD_STATE), cm.reshape(bsz, s, SSD_GROUPS, SSD_STATE))
    y = (y + ssd_d[:, None].astype(y.dtype) * xs).reshape(bsz, s, SSD_INNER) * jax.nn.silu(z)
    y = rmsnorm(y.reshape(bsz, s, SSD_GROUPS, SSD_INNER // SSD_GROUPS),
                ssd_norm_g.reshape(SSD_GROUPS, SSD_INNER // SSD_GROUPS)).reshape(bsz, s, SSD_INNER)
    return jnp.concatenate([o_gla, y], axis=-1) @ w_out

def t5_bucket(rel):
    max_exact = REL_BUCKETS // 2
    relf = jnp.maximum(rel, 1).astype(jnp.float32)
    large = max_exact + (jnp.log(relf / max_exact) / math.log(REL_MAX_DIST / max_exact)
                         * (REL_BUCKETS - max_exact)).astype(jnp.int32)
    large = jnp.minimum(large, REL_BUCKETS - 1)
    return jnp.where(rel < max_exact, rel, large)

def dsa_mixer(h, w_dq, q_norm_g, w_uq, w_dkv, kv_norm_g, w_uv, w_o,
              idx_w_q, idx_w_k, idx_ln_g, idx_ln_b, idx_w_w, rel_bias):
    bsz, s, _ = h.shape
    q_lat = rmsnorm(h @ w_dq, q_norm_g)
    q = (q_lat @ w_uq).reshape(bsz, s, DSA_HEADS, DSA_LATENT)
    kv = rmsnorm(h @ w_dkv, kv_norm_g)
    q_idx = (q_lat @ idx_w_q).reshape(bsz, s, IDX_HEADS, IDX_DIM)
    k_idx = layernorm(h @ idx_w_k, idx_ln_g, idx_ln_b)
    w_idx = (h @ idx_w_w) * (IDX_HEADS ** -0.5 * IDX_DIM ** -0.5)
    topk = min(TOPK_MAX, s // 4)
    nb = s // Q_BLOCK
    key_pos = jnp.arange(s)

    def one_block(inp):
        qb, qib, wb, start = inp
        qpos = start + jnp.arange(Q_BLOCK)
        idx_logits = jnp.einsum('bqhd,bsd->bqhs', qib, k_idx).astype(jnp.float32)
        score = jnp.einsum('bqhs,bqh->bqs', jax.nn.relu(idx_logits), wb.astype(jnp.float32))
        score = jnp.where((key_pos[None, :] <= qpos[:, None])[None], score, -jnp.inf)
        _, sel = lax.top_k(score, topk)
        valid = sel <= qpos[None, :, None]
        kv_sel = jax.vmap(lambda kvb, ib: kvb[ib])(kv, sel)
        logits = jnp.einsum('bqhc,bqkc->bqhk', qb, kv_sel).astype(jnp.float32) * (DSA_LATENT ** -0.5)
        bias = rel_bias[t5_bucket(jnp.maximum(qpos[None, :, None] - sel, 0))]
        logits = logits + jnp.moveaxis(bias, 3, 2).astype(jnp.float32)
        logits = jnp.where(valid[:, :, None, :], logits, -jnp.inf)
        p = jax.nn.softmax(logits, axis=-1).astype(kv.dtype)
        return jnp.einsum('bqhk,bqkc->bqhc', p, kv_sel)

    o_lat = lax.map(one_block, (to_chunks(q, Q_BLOCK), to_chunks(q_idx, Q_BLOCK),
                                to_chunks(w_idx, Q_BLOCK), jnp.arange(nb) * Q_BLOCK))
    o_lat = from_chunks(o_lat)
    o = jnp.einsum('bshc,hcd->bshd', o_lat, w_uv).reshape(bsz, s, DSA_HEADS * DSA_VDIM)
    return o @ w_o

def setup_inputs(seed: int = 0) -> dict:
    key = jax.random.key(seed)
    keys = jax.random.split(key, 64)
    counter = [0]

    def nk():
        counter[0] += 1
        return keys[counter[0] - 1]

    def w(shape, fan_in):
        return jax.random.normal(nk(), shape, jnp.float32) * (fan_in ** -0.5)

    def gain(shape):
        return 1.0 + 0.02 * jax.random.normal(nk(), shape, jnp.float32)

    def small(shape, scale=0.02):
        return scale * jax.random.normal(nk(), shape, jnp.float32)

    ne, no = (DEPTH + 1) // 2, DEPTH // 2
    x = jax.random.normal(nk(), (BATCH, SEQ, D_MODEL), jnp.float32)
    dt0 = jnp.exp(jax.random.uniform(nk(), (ne, SSD_HEADS), jnp.float32, math.log(1e-3), math.log(1e-1)))
    ssd_dt_bias = dt0 + jnp.log(-jnp.expm1(-dt0))
    ssd_a_log = jnp.log(jax.random.uniform(nk(), (ne, SSD_HEADS), jnp.float32, 1.0, 16.0))
    return {
        'x': x,
        'ffn_norm_g': gain((DEPTH, 2, D_MODEL)),
        'ffn_w_gate': w((DEPTH, 2, D_MODEL, D_FF), D_MODEL),
        'ffn_w_up': w((DEPTH, 2, D_MODEL, D_FF), D_MODEL),
        'ffn_w_down': w((DEPTH, 2, D_FF, D_MODEL), D_FF),
        'mix_norm_g': gain((DEPTH, D_MODEL)),
        'hy_w_in': w((ne, D_MODEL, HY_IN_WIDTH), D_MODEL),
        'gla_w_gate2': w((ne, GLA_GATE_RANK, GLA_QK), GLA_GATE_RANK),
        'gla_b_gate': small((ne, GLA_QK), 0.1),
        'gla_norm_g': gain((ne, GLA_V)),
        'ssd_conv_w': w((ne, SSD_CONV, SSD_CONV_CH), SSD_CONV),
        'ssd_conv_b': small((ne, SSD_CONV_CH)),
        'ssd_dt_bias': ssd_dt_bias,
        'ssd_a_log': ssd_a_log,
        'ssd_d': gain((ne, SSD_HEADS)),
        'ssd_norm_g': gain((ne, SSD_INNER)),
        'hy_w_out': w((ne, MIX_WIDTH, D_MODEL), MIX_WIDTH),
        'dsa_w_dq': w((no, D_MODEL, DSA_Q_RANK), D_MODEL),
        'dsa_q_norm_g': gain((no, DSA_Q_RANK)),
        'dsa_w_uq': w((no, DSA_Q_RANK, DSA_HEADS * DSA_LATENT), DSA_Q_RANK),
        'dsa_w_dkv': w((no, D_MODEL, DSA_LATENT), D_MODEL),
        'dsa_kv_norm_g': gain((no, DSA_LATENT)),
        'dsa_w_uv': w((no, DSA_HEADS, DSA_LATENT, DSA_VDIM), DSA_LATENT),
        'dsa_w_o': w((no, DSA_HEADS * DSA_VDIM, D_MODEL), DSA_HEADS * DSA_VDIM),
        'idx_w_q': w((no, DSA_Q_RANK, IDX_HEADS * IDX_DIM), DSA_Q_RANK),
        'idx_w_k': w((no, D_MODEL, IDX_DIM), D_MODEL),
        'idx_ln_g': gain((no, IDX_DIM)),
        'idx_ln_b': small((no, IDX_DIM)),
        'idx_w_w': w((no, D_MODEL, IDX_HEADS), D_MODEL),
        'rel_bias': small((REL_BUCKETS, DSA_HEADS), 0.5),
        'final_norm_g': gain((D_MODEL,)),
    }

def reference(x, ffn_norm_g, ffn_w_gate, ffn_w_up, ffn_w_down, mix_norm_g,
              hy_w_in, gla_w_gate2, gla_b_gate, gla_norm_g, ssd_conv_w, ssd_conv_b,
              ssd_dt_bias, ssd_a_log, ssd_d, ssd_norm_g, hy_w_out,
              dsa_w_dq, dsa_q_norm_g, dsa_w_uq, dsa_w_dkv, dsa_kv_norm_g, dsa_w_uv, dsa_w_o,
              idx_w_q, idx_w_k, idx_ln_g, idx_ln_b, idx_w_w, rel_bias, final_norm_g):
    for layer in range(DEPTH):
        h = rmsnorm(x, ffn_norm_g[layer, 0])
        x = x + 0.5 * swiglu(h, ffn_w_gate[layer, 0], ffn_w_up[layer, 0], ffn_w_down[layer, 0])
        h = rmsnorm(x, mix_norm_g[layer])
        i = layer // 2
        if layer % 2 == 0:
            x = x + gla_ssd_mixer(h, hy_w_in[i], gla_w_gate2[i], gla_b_gate[i], gla_norm_g[i],
                                  ssd_conv_w[i], ssd_conv_b[i], ssd_dt_bias[i], ssd_a_log[i],
                                  ssd_d[i], ssd_norm_g[i], hy_w_out[i])
        else:
            x = x + dsa_mixer(h, dsa_w_dq[i], dsa_q_norm_g[i], dsa_w_uq[i], dsa_w_dkv[i],
                              dsa_kv_norm_g[i], dsa_w_uv[i], dsa_w_o[i], idx_w_q[i], idx_w_k[i],
                              idx_ln_g[i], idx_ln_b[i], idx_w_w[i], rel_bias)
        h = rmsnorm(x, ffn_norm_g[layer, 1])
        x = x + 0.5 * swiglu(h, ffn_w_gate[layer, 1], ffn_w_up[layer, 1], ffn_w_down[layer, 1])
    return rmsnorm(x, final_norm_g)


_drawn_inputs = setup_inputs


def setup_inputs(seed=0):
    import zlib

    import numpy as np

    out = dict(_drawn_inputs(seed))
    spreads = {}
    factors = {'ffn_norm_g': 2.902,
     'gla_b_gate': 2.834,
     'gla_norm_g': 5.303,
     'ssd_conv_b': 2.781,
     'ssd_d': 3.588,
     'ssd_norm_g': 3.74,
     'dsa_q_norm_g': 5.105,
     'dsa_kv_norm_g': 8.0,
     'idx_ln_g': 5.681,
     'idx_ln_b': 6.356,
     'final_norm_g': 2.773}
    for name, (base, spread) in spreads.items():
        noise = np.random.default_rng([zlib.crc32(name.encode()), seed]).standard_normal(out[name].shape)
        drawn = base * np.exp(spread * noise) if base else spread * noise
        out[name] = __import__('jax').numpy.asarray(drawn.astype(out[name].dtype))
    for name, factor in factors.items():
        out[name] = (out[name] * factor).astype(out[name].dtype)
    return out
```

```python
from contextlib import ExitStack

import concourse.bass as bass
from concourse import mybir

F32 = mybir.dt.float32
F32R = mybir.dt.float32r
I32 = mybir.dt.int32
I8 = mybir.dt.int8
ALU = mybir.AluOpType
ACT = mybir.ActivationFunctionType
KB = 1024

P = 128
TOK = 512
D = 1024
KT = D // P
TT = TOK // P
D_FF = 2816
FT = D_FF // P
EPS = 1e-6
GH, GDK, GDV, GRANK, GTAU = 4, 128, 256, 16, 16.0
GVT = GH * GDV // P
SH, SHD, SN, SG, TAPS = 16, 64, 128, 2, 4
SI = SH * SHD
XT = (SI + 2 * SG * SN) // P
HY_Q, HY_K, HY_V = 0, GH * GDK, 2 * GH * GDK
HY_R = HY_V + GH * GDV
HY_G = HY_R + GH * GDV
HY_Z = HY_G + GRANK
HY_XBC = HY_Z + SI
HY_DT = HY_XBC + XT * P
DT0 = 64
LEVELS = 7
AH, AL, AV, AQR = 16, 128, 64, 256
IH, IDIM, TOPK = 16, 64, min(256, TOK // 4)
REL_BUCKETS, REL_MAX_DIST = 32, 128
LINE = TOK + P
MASKED, TAKEN = -1e30, -3e38

SLOTS = 4
UC = KT * P
PHASES = ((0, 8), (8, 8), (16, 6))
STAGES = ["ffn0", "mix0", "ffn1", "ffn2", "mix1", "ffn3"]


def build_program(nc, a, out):
    ctx = ExitStack()
    with ctx:
        def sb(name, shape, dt=F32):
            return ctx.enter_context(nc.sbuf_tensor(name, shape, dt))

        def sem(name):
            return ctx.enter_context(nc.semaphore(name))

        x = sb("x", [P, KT, TOK])
        H0 = nc.sbuf_base
        h_hi = sb("h_hi", [P, KT, TOK], F32R)
        h_lo = sb("h_lo", [P, KT, TOK], F32R)
        w_raw = sb("w_raw", [P, SLOTS, UC])
        w_hi = sb("w_hi", [P, SLOTS, UC], F32R)
        w_lo = sb("w_lo", [P, SLOTS, UC], F32R)
        ident = sb("ident", [P, P])
        ones = sb("ones", [P, P])
        sq = sb("sq", [P, 4, TOK])
        rs = sb("rs", [P, 4, 16])
        gains = sb("gains", [P, 176])
        pcols = sb("pcols", [P, 16])
        ps = ctx.enter_context(nc.psum_tensor("ps", [P, 8, 512], F32))
        ARENA = 100
        sb("arena", [P, ARENA * 256])
        A0 = nc.sbuf_base - ARENA * KB

        def at(name, shape, kb, dt=F32):
            return nc.alloc_sbuf_tensor_at(name, shape, dt, offset=A0 + int(kb * KB))
        act_hi = at("act_hi", [P, 8, TOK], 0, F32R)
        act_lo = at("act_lo", [P, 8, TOK], 16, F32R)
        sg = at("sg", [P, 2, TOK], 32)
        prod = at("prod", [P, 2, TOK], 36)
        x_in = at("x_in", [P, TT, D], 40)
        prow = at("prow", [P, 2, P], 56)
        ij = at("ij", [P, 4, P], 57, I32)
        gfin = at("gfin", [P, D], 60)
        otile = at("otile", [P, 2, D], 64)
        gq = at("gq", [P, GH, TOK], 0)
        gk = at("gk", [P, GH, TOK], 8)
        gv = at("gv", [P, TT, GH * GDV], 16)
        o_hi = at("o_hi", [P, KT, TOK], 0, F32R)
        o_lo = at("o_lo", [P, KT, TOK], 16, F32R)
        gb = at("gb", [P, GH, TOK], 32)
        gm = at("gm", [P, 2, GH, TOK], 40)
        gattn = at("gattn", [P, TT, GH, P], 56)
        gr = at("gr", [P, GVT, TOK], 64)
        gvT = at("gvT", [P, GVT, TOK], 80)
        small = at("small", [P, TOK], 96)
        masks = at("masks", [P, LEVELS + 1, P], 98, I8)
        tri = at("tri", [P, P], 99)
        gS = gm[:, 0, 0:2, :].rearrange("p a b -> p (a b)").rearrange("p (h v) -> p h v", h=GH)
        dt_tmp = gb[:, 0:3, :]
        gkd = gm[:, 1, :, :].rearrange("p c (h k) -> p c h k", h=GH)
        el = sb("el", [P, GH, TT])
        xbc = at("xbc", [P, XT, TOK], 0)
        sz = at("sz", [P, SI // P, TOK], 24)
        acb = at("acb", [P, 2, SH, P], 40)
        pm = at("pm", [P, SH, P], 56)
        ce = at("ce", [P, SH, P], 64)
        xdt = at("xdt", [P, SI], 72)
        xdtw = at("xdtw", [P, SI], 76)
        sB = at("sB", [P, SG, P], 80)
        cb = at("cb", [P, SG, P], 81)
        sS = at("sS", [P, SI], 82)
        xp = at("xp", [P, 2, TOK + 8], 86)
        toks = sb("toks", [P, 2, TT, SH])
        wtok = sb("wtok", [P, 2, SH])
        acum_dram = nc.dram_tensor("acum_scratch", (SH, TOK), F32).ap()

        aT = at("aT", [P, AH, TOK], 64)
        aq = at("aq", [P, AH, TOK], 0)
        kvT = at("kvT", [P, TOK], 32)
        kvtok = at("kvtok", [P, TT, AL], 34)
        amask = at("amask", [P, TT, TOK], 36, F32R)
        kvr = at("kvr", [P, TOK], 36)
        kx = at("kx", [P, TOK], 38)
        kc = at("kc", [IDIM, TOK], 40)
        lp = at("lp", [P, 4, TOK], 44)
        qlr = at("qlr", [P, 2, TOK], 44)
        ql_hi = at("ql_hi", [P, 2, TOK], 48, F32R)
        ql_lo = at("ql_lo", [P, 2, TOK], 52, F32R)
        pt = at("pt", [P, 2, TOK], 52)
        olat = at("olat", [P, 2, TOK], 56)
        wuv = at("wuv", [P, AH, AV], 60)
        kn = at("kn", [P, TOK], 96)
        cneg = at("cneg", [P, P], 98)
        identr = at("identr", [P, P], 98.5, F32R)
        cmat = at("cmat", [IDIM, IDIM], 99)
        wtk = at("wtk", [P, TT, IH], 99.25)
        stat = at("stat", [P, 4, 8], 99.5)
        qix = nc.alloc_sbuf_tensor_at("qix", [P, KT, TOK], F32, offset=H0)
        ao = nc.alloc_sbuf_tensor_at("ao", [P, KT, TOK], F32, offset=H0)
        sc = nc.alloc_sbuf_tensor_at("sc", [P, TT - 1, TOK], F32, offset=H0 + 16 * KB)
        relb = at("relb", [REL_BUCKETS, AH], 72)
        hot = at("hot", [REL_BUCKETS, LINE], 73)
        line = at("line", [AH, LINE], 76)
        line_dram = nc.dram_tensor("line_scratch", (AH, P, LINE), F32).ap()

        NU = {"ffn": 2 * FT + 3 * KT, "mix0": 1 + 8 + 2 * GVT + KT + SI // P + XT + KT, "mix1": 18}
        NX = {"ffn": 3 * KT, "mix0": 2 * KT, "mix1": KT}
        UB, XB, un, xn = {}, {}, 0, KT
        for st in STAGES:
            UB[st], XB[st] = un, xn
            un += NU.get(st, NU["ffn"])
            xn += NX.get(st, NX["ffn"])
        NUNITS = un
        OPS, NORMS = {}, {}
        for st in STAGES:
            OPS[st] = 8 * len(OPS)
            NORMS[st] = len(NORMS)
            if st == "mix0":
                for e in ("gla", "ssd"):
                    OPS[e] = 8 * len(OPS)
                    NORMS[e] = len(NORMS)
            if st == "mix1":
                OPS["dsa"] = 8 * len(OPS)
        NORMS["final"] = len(NORMS)
        parts = [1] * NUNITS
        if "mix0" in UB:
            parts[UB["mix0"]] = 3
        if "mix1" in UB:
            parts[UB["mix1"] + 3] = 3
        LAND, acc = [], [0] * SLOTS
        for n in range(NUNITS):
            acc[n % SLOTS] += 16 * parts[n]
            LAND.append(acc[n % SLOTS])

        raw_landed = [sem(f"raw_landed{s}") for s in range(SLOTS)]
        hi_ready, lo_ready, unit_used = sem("hi_ready"), sem("lo_ready"), sem("unit_used")
        consts_ready, iota_ready, mask_steps = sem("consts_ready"), sem("iota_ready"), sem("mask_steps")
        x_landed, par_landed, gfin_landed = sem("x_landed"), sem("par_landed"), sem("gfin_landed")
        xt_done, par_done, gains_ready = sem("xt_done"), sem("par_done"), sem("gains_ready")
        x_upd = sem("x_upd")
        wg2_landed = sem("wg2_landed")
        silu_done, mul_done, ahi_done, alo_done = sem("silu_done"), sem("mul_done"), sem("ahi_done"), sem("alo_done")
        sq_ready, ss_done = sem("sq_ready"), sem("ss_done")
        rsq_steps, rstd_ready, bc_done = sem("rsq_steps"), sem("rstd_ready"), sem("bc_done")
        omul_done, ohi_done, opnd_ready = sem("omul_done"), sem("ohi_done"), sem("opnd_ready")
        fin_t, fin_ready = sem("fin_t"), sem("fin_ready")
        stored = [sem("stored_even"), sem("stored_odd")]
        tile_out = sem("tile_out")
        g_glr, g_gate_mm, g_gate_b, g_abs, g_scan = sem("g_glr"), sem("g_gate_mm"), sem("g_gate_b"), sem("g_abs"), sem("g_scan")
        g_diff, g_exp, g_mul, g_lvl, g_mask = sem("g_diff"), sem("g_exp"), sem("g_mul"), sem("g_lvl"), sem("g_mask")
        g_zero, g_vt, g_vev = sem("g_zero"), sem("g_vt"), sem("g_vev")
        g_dec, g_decm, g_kt, g_kev, g_o, g_oev, g_st, g_S = (sem(n) for n in (
            "g_dec", "g_decm", "g_kt", "g_kev", "g_o", "g_oev", "g_st", "g_S"))
        g_gated = sem("g_gated")
        s_dt, s_dta, s_acum, s_scr, s_tok, s_tokev = (sem(n) for n in ("s_dt", "s_dta", "s_acum", "s_scr", "s_tok", "s_tokev"))
        s_acb = [sem("s_acb_even"), sem("s_acb_odd")]
        s_conv, s_conved, s_silu, s_pad = sem("s_conv"), sem("s_conved"), sem("s_silu"), sem("s_pad")
        s_ea, s_pexp, s_wd, s_w, s_D, s_P, s_C = (sem(n) for n in ("s_ea", "s_pexp", "s_wd", "s_w", "s_D", "s_P", "s_C"))
        s_cb, s_cbm, s_tr, s_trB, s_Bev, s_xdt, s_xdtw = (sem(n) for n in ("s_cb", "s_cbm", "s_tr", "s_trB", "s_Bev", "s_xdt", "s_xdtw"))
        s_y, s_yev, s_st, s_S1, s_S2, s_gate = (sem(n) for n in ("s_y", "s_yev", "s_st", "s_S1", "s_S2", "s_gate"))

        l_landed, l_mm, l_ev, l_scr, t_landed = (sem(n) for n in ("l_landed", "l_mm", "l_ev", "l_scr", "t_landed"))
        uv_landed, a_cneg, a_const = sem("uv_landed"), sem("a_cneg"), sem("a_const")
        d_raw, d_kx, d_cen, d_kc, d_sq, d_ss, d_rs, d_bc = (sem("d_" + n) for n in ("raw", "kx", "cen", "kc", "sq", "ss", "rs", "bc"))
        d_mul, d_hi, d_ql, d_kv, d_kn, d_dup, d_tr, d_trev = (sem("d_" + n) for n in ("mul", "hi", "ql", "kv", "kn", "dup", "tr", "trev"))
        d_tile, d_ix, d_relu, d_acc = sem("d_tile"), sem("d_ix"), sem("d_relu"), sem("d_acc")
        a_log, a_max, a_exp, a_rec, a_nrm, a_tr, a_pt, a_pv, a_ol, a_uv, a_o = (sem("a_" + n) for n in (
            "log", "max", "exp", "rec", "nrm", "tr", "pt", "pv", "ol", "uv", "o"))
        k_top, k_mask = sem("k_top"), sem("k_mask")
        T1 = 25 + SI // P + XT if "mix0" in STAGES else 0

        wg, wu, wd = a["ffn_w_gate"], a["ffn_w_up"], a["ffn_w_down"]
        w_in, w_out = a["hy_w_in"][0], a["hy_w_out"][0]
        GB_B, GB_N, GB_CB, GB_SN, GB_Q, GB_KV, GB_CW = 48, 52, 60, 72, 80, 82, 128

        block = ctx.enter_context(nc.Block())

        @block.sync
        def _(sp):
            def load(n, i, srcs):
                if n >= SLOTS or not isinstance(i, int):
                    sp.wait_ge(lo_ready, n - SLOTS + 1 + 4 * i)
                for dst, src in srcs:
                    sp.dma_start(dst, src).then_inc(raw_landed[n % SLOTS], 16)

            def slot(n, kt=KT, c=P):
                return w_raw[:, n % SLOTS, 0:kt * c].rearrange("p (k n) -> p k n", k=kt)

            def kp(w):
                return w.rearrange("(k p) n -> p k n", p=P)

            def columns(n, w, c0, tiles, kt=KT):
                with sp.Fori(0, tiles // 4) as i:
                    for j in range(4):
                        load(n + j, i, [(slot(n + j, kt), w[:, :, bass.ds(i * (4 * P) + (c0 + j * P), P)])])
                return n + tiles

            with nc.allow_non_contiguous_dma(reason="a few hundred parameters, one number each"):
                sp.dma_start(x_in[:, :, :], a["x"][0].rearrange("(t p) d -> p t d", p=P)).then_inc(x_landed, 16)
                rows = [(0, 0, a["ffn_norm_g"].rearrange("l a (k p) -> (l a k) p", p=P), 32),
                        (0, 32, a["mix_norm_g"].rearrange("l (k p) -> (l k) p", p=P), 16),
                        (0, GB_B, a["gla_b_gate"].rearrange("l (k p) -> (l k) p", p=P), 4),
                        (0, GB_N, a["gla_norm_g"].rearrange("l (k p) -> (l k) p", p=P), 8),
                        (0, GB_CB, a["ssd_conv_b"].rearrange("l (k p) -> (l k) p", p=P), 12),
                        (0, GB_SN, a["ssd_norm_g"].rearrange("l (k p) -> (l k) p", p=P), 8),
                        (0, GB_Q, a["dsa_q_norm_g"].rearrange("l (k p) -> (l k) p", p=P), 2),
                        (0, GB_KV, a["dsa_kv_norm_g"], 1),
                        (1, 0, a["ssd_conv_w"].rearrange("l w (k p) -> (l w k) p", p=P), 48)]
                for c, r, src, cnt in rows:
                    sp.dma_start(prow[r:r + cnt, c, :], src).then_inc(par_landed, 16)
                dv = a["ssd_d"].rearrange("l (t two) -> (l two) t", two=2)
                for h in range(2):
                    sp.dma_start(pcols[h * 64:(h + 1) * 64, 0:8], dv[h:h + 1, :].to_broadcast([64, 8])).then_inc(par_landed, 16)
                sp.dma_start(pcols[DT0:DT0 + SH, 8:9], a["ssd_dt_bias"].rearrange("l h -> h l")).then_inc(par_landed, 16)
                sp.dma_start(pcols[DT0:DT0 + SH, 9:10], a["ssd_a_log"].rearrange("l h -> h l")).then_inc(par_landed, 16)
                sp.dma_start(pcols[0:IDIM, 11:12], a["idx_ln_g"].rearrange("l h -> h l")).then_inc(par_landed, 16)
                sp.dma_start(pcols[0:IDIM, 12:13], a["idx_ln_b"].rearrange("l h -> h l")).then_inc(par_landed, 16)
                sp.dma_start(relb[:, :], a["rel_bias"]).then_inc(l_landed, 16)
                sp.dma_start(hot[:, :], a["bucket_onehot"]).then_inc(l_landed, 16)
            for st in STAGES:
                n = UB[st]
                if st.startswith("ffn"):
                    q = int(st[3])
                    g_src, u_src, d_src = (kp(w[q // 2, q % 2]) for w in (wg, wu, wd))
                    for f0, nf in PHASES:
                        first = n == 0
                        if first:
                            for j in range(4):
                                load(j, 0, [(slot(j), (g_src, u_src)[j % 2][:, :, (j // 2) * P:(j // 2 + 1) * P])])
                        with sp.Fori(1 if first else 0, nf // 2) as i:
                            for j in range(4):
                                src = (g_src, u_src)[j % 2]
                                load(n + j, i, [(slot(n + j), src[:, :, bass.ds(i * (2 * P) + (f0 + j // 2) * P, P)])])
                        n = columns(n + 2 * nf, d_src[:, f0:f0 + nf, :], 0, KT, nf)
                elif st == "mix0":
                    w = kp(w_in)
                    s0 = slot(n)
                    load(n, 0, [(s0[:, :, 0:64], w[:, :, HY_G:HY_G + 64]),
                                (s0[:, :, DT0:DT0 + SH], w[:, :, HY_DT:HY_DT + SH]),
                                (s0[:, :, DT0 + SH:P], w[:, :, HY_Z:HY_Z + P - DT0 - SH])])
                    n = columns(n + 1, w, HY_Q, 8 + 2 * GVT)
                    wo = kp(w_out)
                    n = columns(n, wo[:, 0:KT, :], 0, KT)
                    n = columns(n, w, HY_Z, SI // P + XT)
                    n = columns(n, wo[:, KT:2 * KT, :], 0, KT)
                else:
                    dkv, iw, ww = kp(a["dsa_w_dkv"][0]), kp(a["idx_w_k"][0]), kp(a["idx_w_w"][0])
                    for j in range(2):
                        load(n + j, 0, [(slot(n + j), kp(a["dsa_w_dq"][0])[:, :, j * P:(j + 1) * P])])
                    load(n + 2, 0, [(slot(n + 2), dkv)])
                    s0 = slot(n + 3)
                    load(n + 3, 0, [(s0[:, :, 0:IDIM], iw), (s0[:, :, IDIM:IDIM + IH], ww), (s0[:, :, IDIM + IH:P], dkv[:, :, IDIM + IH:P])])
                    for j in range(2):
                        load(n + 4 + j, 0, [(slot(n + 4 + j, 2, 512), kp(a["idx_w_q"][0])[:, :, j * 512:(j + 1) * 512])])
                    for j in range(4):
                        load(n + 6 + j, 0, [(slot(n + 6 + j, 2, 512), kp(a["dsa_w_uq"][0])[:, :, j * 512:(j + 1) * 512])])
                    n = columns(n + 10, kp(a["dsa_w_o"][0]), 0, KT)
            sp.wait_ge(x_upd, xn)
            sp.dma_start(gfin[:, :], a["final_norm_g"].rearrange("(o n) -> o n", o=1).to_broadcast([P, D])).then_inc(gfin_landed, 16)
            for t in range(TT):
                sp.wait_ge(fin_ready, 2 * t + 2)
                sp.dma_start(out[0, t * P:(t + 1) * P, :], otile[:, t % 2, :]).then_inc(stored[t % 2], 16)
            sp.wait_ge(stored[0], 32)
            sp.wait_ge(stored[1], 32)

        @block.gpsimd
        def _(pool):
            pool.memset(ones[:, :], 1.0).then_inc(consts_ready, 1)
            pool.memset(ident[:, :], 0.0).then_inc(consts_ready, 1)
            pool.iota(ij[:, 0, :], pattern=[[1, P]], base=0, channel_multiplier=0).then_inc(iota_ready, 1)
            pool.iota(ij[:, 1, :], pattern=[[0, P]], base=0, channel_multiplier=1).then_inc(iota_ready, 1)
            pool.wait_ge(consts_ready, 2)
            pool.affine_select(out=ident[:, :], in_=ident[:, :], compare_op=ALU.not_equal, fill=1.0,
                               base=0, pattern=[[-1, P]], channel_multiplier=1).then_inc(consts_ready, 1)
            pool.wait_ge(l_ev, 2)
            pool.dma_start(line_dram, line[:, :].rearrange("h (o c) -> h o c", o=1).to_broadcast([AH, P, LINE])).then_inc(l_scr, 16)
            if "mix0" in STAGES:
                pool.wait_ge(x_upd, XB["mix0"])
                pool.dma_start(small[0:GRANK, :], a["gla_w_gate2"][0]).then_inc(wg2_landed, 16)
                pool.memset(gattn[:, :, :, :], 0.0).then_inc(g_zero, 1)
                pool.wait_ge(s_acum, TT)
                pool.dma_start(acum_dram, dt_tmp[DT0:DT0 + SH, 2, :]).then_inc(s_scr, 16)
                pool.wait_ge(s_scr, 16)
                pool.wait_ge(x_upd, XB["mix0"] + KT)
                pool.memset(xp[:, :, 0:3], 0.0).then_inc(s_pad, 1)
                for c in range(TT):
                    if c >= 2:
                        pool.wait_ge(s_ea, 2 * (c - 1))
                        pool.wait_ge(s_wd, c - 1)
                    pool.dma_start(acb[:, c % 2, :, :],
                                   acum_dram[:, c * P:(c + 1) * P].rearrange("(o h) t -> o h t", o=1).to_broadcast([P, SH, P])
                                   ).then_inc(s_acb[c % 2], 16)

            if "mix1" in STAGES:
                pool.wait_ge(x_upd, XB["ffn1"] if "mix0" in STAGES else KT)
                pool.wait_ge(l_scr, 16)
                lines = bass.AP(tensor=line_dram.tensor, offset=P - 1, ap=[[LINE - 1, P], [P * LINE, AH], [1, TOK]])
                pool.dma_start(aT[:, :, :], lines).then_inc(t_landed, 16)
                pool.dma_start(wuv[:, :, :], a["dsa_w_uv"][0].rearrange("h c d -> c h d")).then_inc(uv_landed, 16)
                pool.memset(cneg[:, :], 0.0).then_inc(a_cneg, 1)
                pool.wait_ge(a_cneg, 1)
                pool.affine_select(out=cneg[:, :], in_=cneg[:, :], compare_op=ALU.is_ge, fill=MASKED,
                                   base=0, pattern=[[-1, P]], channel_multiplier=1).then_inc(a_cneg, 1)
                pool.wait_ge(d_kn, 2)
                pool.dma_start(kn[IDIM:2 * IDIM, :], kn[0:IDIM, :]).then_inc(d_dup, 16)
                for r in range(TT * AH):
                    w = P * (r // AH + 1)
                    pool.wait_ge(a_rec, r + 1)
                    pool.tensor_scalar(lp[:, r % 4, 0:w], lp[:, r % 4, 0:w], stat[:, 2, r % 4:r % 4 + 1], 1.0,
                                       ALU.mult, ALU.mult).then_inc(a_nrm, 1)

        @block.scalar
        def _(act):
            def produce_hi(n, i=0):
                if n >= NUNITS:
                    return
                s = n % SLOTS
                act.wait_ge(raw_landed[s], LAND[n] + 16 * i)
                if n >= SLOTS:
                    act.wait_ge(unit_used, n - SLOTS + 1 + 4 * i)
                act.activation(w_hi[:, s, :], w_raw[:, s, :], ACT.Copy).then_inc(hi_ready, 1)

            def square(z, op_before, m, src):
                if m >= 4:
                    act.wait_ge(ss_done, KT * z + m - 3)
                elif op_before:
                    act.wait_ge(opnd_ready, op_before)
                act.activation(sq[:, m % 4, :], src, ACT.Square).then_inc(sq_ready, 1)

            def square_x(st, xc, m):
                act.wait_ge(x_upd, xc + m + 1)
                square(NORMS[st], OPS.get(st, 8 * len(OPS)), m, x[:, m, :])

            def operand_hi(o, dst):
                for d in range(KT):
                    act.wait_ge(omul_done, o + d + 1)
                    act.activation(dst[:, d, :], sq[:, d % 4, :], ACT.Copy).then_inc(ohi_done, 1)

            def ffn(st, nxt):
                n, fb = UB[st], FT * int(st[3])
                fb = FT * [s for s in STAGES if s.startswith("ffn")].index(st)
                operand_hi(OPS[st], h_hi)
                for ph, (f0, nf) in enumerate(PHASES):
                    with act.Fori(0, nf // 2) as i:
                        for j in range(2):
                            produce_hi(n + 2 * j + SLOTS, i)
                            act.wait_ge(mul_done, fb + f0 + 2 * i + 1)
                            act.activation(sg[:, j, :], ps[:, 2 * j, :], ACT.Silu).then_inc(silu_done, 1)
                            produce_hi(n + 2 * j + 1 + SLOTS, i)
                    n += 2 * nf
                    if ph < 2:
                        with act.Fori(0, 2) as i:
                            for j in range(4):
                                produce_hi(n + j + SLOTS, i)
                    else:
                        for m in range(KT):
                            produce_hi(n + m + SLOTS)
                            square_x(nxt, XB[st] + 2 * KT, m)
                    n += KT

            def mix0(nxt):
                n = UB["mix0"]
                operand_hi(OPS["mix0"], h_hi)

                def tile(t, dst, func, scale=1.0):
                    produce_hi(n + t + SLOTS)
                    act.wait_ge(unit_used, n + t + 1)
                    act.activation(dst, ps[0:dst.shape[0], 4 + t % 4, :], func, scale=scale).then_inc(tile_out, 1)
                produce_hi(n + SLOTS)
                act.wait_ge(unit_used, n + 1)
                act.wait_ge(opnd_ready, OPS["mix0"] + KT)
                act.activation(sq[0:GRANK, 0, :], ps[0:GRANK, 4, :], ACT.Copy).then_inc(g_glr, 1)
                act.activation(small[DT0:DT0 + SH, :], ps[DT0:DT0 + SH, 4, :], ACT.Copy).then_inc(tile_out, 1)
                for h in range(GH):
                    tile(1 + h, gq[:, h, :], ACT.Copy, float(GDK) ** -0.5)
                for h in range(GH):
                    tile(5 + h, gk[:, h, :], ACT.Copy)
                act.wait_ge(g_gate_b, GH)
                g0, g1 = gm[:, 0, :, :], gm[:, 1, :, :]
                act.activation(g0, g1, ACT.Abs).then_inc(g_abs, 1)
                act.wait_ge(g_abs, 1)
                act.activation(g0, g0, ACT.Exp, scale=-1.0).then_inc(g_abs, 1)
                act.wait_ge(g_abs, 2)
                act.activation(g0, g0, ACT.Ln, bias=1.0).then_inc(g_abs, 1)
                for s in range(8):
                    for j in range(2):
                        t = 9 + 2 * s + j
                        v = 2 * s + j
                        tile(t, gvT[:, v, :] if v < GVT else gr[:, v - GVT, :], ACT.Copy if v < GVT else ACT.Silu)
                    if s < LEVELS:
                        act.wait_ge(g_diff, 2 * (s + 1))
                        act.activation(gm[:, s % 2, :, :], gm[:, s % 2, :, :], ACT.Exp, scale=1.0 / GTAU).then_inc(g_exp, 1)
                act.wait_ge(g_lvl, TT * LEVELS)
                act.activation(gm[:, 0, :, :], gb[:, :, :], ACT.Exp, scale=1.0 / GTAU).then_inc(g_dec, 1)
                act.activation(el[:, :, :], gb[:, :, :].rearrange("p h (c t) -> p h c t", t=P)[:, :, :, P - 1], ACT.Exp,
                               scale=1.0 / GTAU).then_inc(g_dec, 1)
                act.wait_ge(g_decm, 2)
                act.activation(gm[:, 1, :, :], gm[:, 1, :, :], ACT.Exp, scale=1.0 / GTAU).then_inc(g_dec, 1)
                R = slice(DT0, DT0 + SH)
                act.wait_ge(s_dta, 1)
                act.activation(dt_tmp[R, 0, :], small[R, :], ACT.Abs).then_inc(s_dt, 1)
                act.wait_ge(s_dt, 1)
                act.activation(dt_tmp[R, 0, :], dt_tmp[R, 0, :], ACT.Exp, scale=-1.0).then_inc(s_dt, 1)
                act.wait_ge(s_dt, 2)
                act.activation(dt_tmp[R, 0, :], dt_tmp[R, 0, :], ACT.Ln, bias=1.0).then_inc(s_dt, 1)
                act.activation(pcols[R, 10:11], pcols[R, 9:10], ACT.Exp).then_inc(s_dt, 1)
                for c in range(TT):
                    act.wait_ge(g_o, c + 1)
                    if c == 0:
                        act.wait_ge(g_vt, GVT)
                    for b in range(2):
                        act.activation(gvT[:, 4 * b:4 * b + 4, c * P:(c + 1) * P],
                                       ps[:, 4 + 2 * (c % 2) + b, :].rearrange("p (m t) -> p m t", m=4), ACT.Copy).then_inc(g_oev, 1)
                for m in range(GVT):
                    if m == 0:
                        act.wait_ge(g_oev, 2 * TT)
                    square(NORMS["gla"], OPS["gla"], m, gvT[:, m, :])
                operand_hi(OPS["gla"], o_hi)
                n0 = UB["mix0"] + 25
                with act.Fori(0, 2) as i:
                    for j in range(4):
                        produce_hi(n0 + j + SLOTS, i)
                n0 += KT
                tb = 25
                act.wait_ge(s_scr, 16)
                for m in range(SI // P):
                    produce_hi(n0 + m + SLOTS)
                    act.wait_ge(unit_used, n0 + m + 1)
                    act.activation(sz[:, m, :], ps[:, 4 + (tb + m) % 4, :], ACT.Silu).then_inc(tile_out, 1)
                n0 += SI // P
                tb += SI // P

                def conv_silu(m):
                    act.wait_ge(s_conved, m + 1)
                    act.activation(xbc[:, m, :], sq[:, m % 2, :], ACT.Silu).then_inc(s_silu, 1)
                act.wait_ge(s_pad, 1)
                for m in range(XT):
                    produce_hi(n0 + m + SLOTS)
                    act.wait_ge(unit_used, n0 + m + 1)
                    if m >= 2:
                        act.wait_ge(s_conved, m - 1)
                    act.activation(xp[:, m % 2, 3:3 + TOK], ps[:, 4 + (tb + m) % 4, :], ACT.Copy).then_inc(tile_out, 1)
                    if m:
                        conv_silu(m - 1)
                conv_silu(XT - 1)
                for c in range(TT):
                    act.wait_ge(s_acb[c % 2], 16 * (c // 2 + 1))
                    ab = acb[:, c % 2, :, :]
                    if c:
                        act.wait_ge(s_y, c)
                    act.activation(ce[:, :, :], ab, ACT.Exp).then_inc(s_ea, 1)
                    if c:
                        act.wait_ge(s_S1, c - 1) if c > 1 else None
                        act.wait_ge(s_xdtw, c)
                    act.activation(wtok[:, 1, :], ab[:, :, P - 1], ACT.Exp).then_inc(s_ea, 1)
                    act.wait_ge(s_D, c + 1)
                    act.activation(pm[:, :, :], pm[:, :, :], ACT.Exp).then_inc(s_pexp, 1)
                    act.wait_ge(s_wd, c + 1)
                    act.activation(wtok[:, 0, :], wtok[:, 0, :], ACT.Exp).then_inc(s_w, 1)
                    act.wait_ge(s_trB, c + 1)
                    act.activation(sB[:, :, :], ps[:, 1, 0:SG * P].rearrange("p (g n) -> p g n", g=SG), ACT.Copy).then_inc(s_Bev, 1)
                for m in range(KT):
                    act.wait_ge(s_gate, m + 1)
                    square(NORMS["ssd"], OPS["ssd"], m, xbc[:, m, :])
                operand_hi(OPS["ssd"], h_hi)
                n0 = UB["mix0"] + NU["mix0"] - KT
                for m in range(KT):
                    produce_hi(n0 + m + SLOTS)
                    square_x(nxt, XB["mix0"] + KT, m)

            def mix1(nxt):
                n = UB["mix1"]
                operand_hi(OPS["mix1"], h_hi)
                for t in range(4):
                    produce_hi(n + t + SLOTS)
                    act.wait_ge(unit_used, n + t + 1)
                    b = 4 + (T1 + t) % 4
                    if t == 0:
                        act.wait_ge(opnd_ready, OPS["mix1"] + KT)
                    if t < 3:
                        act.activation((qlr[:, t, :] if t < 2 else kvr[:, :]), ps[:, b, :], ACT.Copy).then_inc(d_raw, 1)
                        act.activation(sq[:, t, :], ps[:, b, :], ACT.Square).then_inc(tile_out, 1)
                    else:
                        act.activation(kx[0:IDIM, :], ps[0:IDIM, b, :], ACT.Copy).then_inc(d_kx, 1)
                        act.activation(kx[IDIM:IDIM + IH, :], ps[IDIM:IDIM + IH, b, :], ACT.Copy,
                                       scale=float(IH) ** -0.5 * float(IDIM) ** -0.5).then_inc(tile_out, 1)
                act.wait_ge(d_cen, 1)
                act.activation(sq[0:IDIM, 3, :], ps[0:IDIM, 0, :], ACT.Square).then_inc(d_sq, 1)
                act.activation(kc[:, :], ps[0:IDIM, 0, :], ACT.Copy).then_inc(d_kc, 1)
                for d in range(2):
                    act.wait_ge(d_mul, d + 1)
                    act.activation(ql_hi[:, d, :], sq[:, d, :], ACT.Copy).then_inc(d_hi, 1)
                act.wait_ge(d_tr, 1)
                act.activation(wtk[:, :, :], ps[:, 2, 0:TT * IH].rearrange("p (c h) -> p c h", c=TT), ACT.Copy).then_inc(d_trev, 1)
                act.wait_ge(d_tr, 2)
                act.activation(kvtok[:, :, :], ps[:, 0, :].rearrange("p (c d) -> p c d", c=TT), ACT.Copy).then_inc(d_trev, 1)
                for t in range(KT + AH):
                    if t % 4 == 3:
                        act.wait_ge(unit_used, n + 4 + t // 4 + 1)
                    else:
                        act.wait_ge(d_tile, 3 * (t // 4) + t % 4 + 1)
                    dst = qix[:, t, :] if t < KT else aq[:, t - KT, :]
                    act.activation(dst, ps[:, 4 + (T1 + t) % 4, :], ACT.Copy,
                                   scale=1.0 if t < KT else float(AL) ** -0.5).then_inc(tile_out, 1)
                    if t % 4 == 3:
                        produce_hi(n + 4 + t // 4 + SLOTS)
                for r in range((TT - 1) * IH):
                    w = P * (r // IH + 2)
                    act.wait_ge(d_ix, r + 1)
                    if r >= 4:
                        act.wait_ge(d_acc, r - 3)
                    act.activation(sq[:, r % 4, 0:w], ps[:, r % 4, 0:w], ACT.Relu).then_inc(d_relu, 1)
                NR = TT * AH

                def p_out(r):
                    w = P * (r // AH + 1)
                    act.wait_ge(a_tr, r + 1)
                    if r >= 2:
                        act.wait_ge(a_pv, r - 1)
                    act.activation(pt[:, r % 2, 0:w], ps[:, 2 + r % 2, 0:w], ACT.Copy).then_inc(a_pt, 1)

                def latent_out(g):
                    act.wait_ge(a_pv, 4 * g + 4)
                    if g >= 2:
                        act.wait_ge(a_uv, g - 1)
                    act.activation(olat[:, g % 2, :], ps[:, 4 + g % 2, :], ACT.Copy).then_inc(a_ol, 1)

                def values_out(g):
                    act.wait_ge(a_uv, g + 1)
                    b, half = g // 4, (g % 4) // 2
                    act.activation(ao[:, 4 * half:4 * half + 4, b * P:(b + 1) * P],
                                   ps[:, 6 + half, :].rearrange("p (m t) -> p m t", m=4), ACT.Copy).then_inc(a_o, 1)
                for r in range(NR + 6):
                    if r < NR:
                        w = P * (r // AH + 1)
                        act.wait_ge(a_max, r + 1)
                        if r >= 4:
                            act.wait_ge(a_rec, r - 3)
                        act.activation(lp[:, r % 4, 0:w], lp[:, r % 4, 0:w], ACT.Exp, scale=-1.0, bias=stat[:, 0, r % 4:r % 4 + 1],
                                       accum_out=stat[:, 1, r % 4:r % 4 + 1]).then_inc(a_exp, 1)
                    if 2 <= r < NR + 2:
                        p_out(r - 2)
                    if r >= 4 and (r - 4) % 4 == 3 and (r - 4) // 4 < NR // 4:
                        latent_out((r - 4) // 4)
                    if r >= 5 and (r - 5) % 8 == 7 and (r - 5) // 4 < NR // 4:
                        values_out((r - 5) // 4)
                for d in range(KT):
                    if d == 0:
                        act.wait_ge(a_o, 2 * TT)
                    act.activation(o_hi[:, d, :], ao[:, d, :], ACT.Copy).then_inc(ohi_done, 1)
                n0 = n + NU["mix1"] - KT
                for m in range(KT):
                    produce_hi(n0 + m + SLOTS)
                    square_x(nxt, XB["mix1"], m)

            act.wait_ge(l_mm, 1)
            act.activation(line[:, 0:TOK], ps[0:AH, 2, :], ACT.Copy).then_inc(l_ev, 1)
            act.activation(line[:, TOK:LINE], ps[0:AH, 3, 0:P], ACT.Copy).then_inc(l_ev, 1)
            for n in range(SLOTS):
                produce_hi(n)
            for m in range(KT):
                square_x(STAGES[0], 0, m)
            for k, st in enumerate(STAGES):
                nxt = (STAGES + ["final"])[k + 1]
                if st.startswith("ffn"):
                    ffn(st, nxt)
                elif st == "mix0":
                    mix0(nxt)
                else:
                    mix1(nxt)

        @block.vector
        def _(dve):
            def produce_lo(n, i=0):
                if n >= NUNITS:
                    return
                s = n % SLOTS
                dve.wait_ge(hi_ready, n + 1 + 4 * i)
                dve.tensor_tensor(w_lo[:, s, :], w_raw[:, s, :], w_hi[:, s, :].bitcast(F32),
                                  ALU.subtract).then_inc(lo_ready, 1)

            steps = [0]

            def step(ins):
                steps[0] += 1
                ins.then_inc(rsq_steps, 1)
                dve.wait_ge(rsq_steps, steps[0])

            def newton(val, y, t):
                step(dve.tensor_scalar(t.bitcast(I32), val.bitcast(I32), 1, None, ALU.logical_shift_right))
                step(dve.tensor_scalar(y.bitcast(I32), t.bitcast(I32), -1.0, float(0x5f3759df), ALU.mult, ALU.add))
                for r in range(3):
                    step(dve.scalar_tensor_tensor(out=t, in0=y, scalar=-0.5, in1=y, op0=ALU.mult, op1=ALU.mult))
                    step(dve.tensor_tensor(t, t, val, ALU.mult))
                    last = dve.scalar_tensor_tensor(out=y, in0=t, scalar=1.5, in1=y, op0=ALU.add, op1=ALU.mult)
                    if r < 2:
                        step(last)
                return last

            def rsqrt(z, c, scale):
                dve.wait_ge(ss_done, KT * (z + 1))
                if z:
                    dve.wait_ge(bc_done, z)
                val, y, t = rs[:, 0, 0:c], rs[:, 1, 0:c], rs[:, 2, 0:c]
                step(dve.tensor_scalar(val, ps[:, 2, 0:c], scale, EPS, ALU.mult, ALU.add))
                newton(val, y, t).then_inc(rstd_ready, 1)

            def operand(z, o, src, g0, bank, hi, lo, gate=None):
                dve.wait_ge(bc_done, z + 1)

                def low(d):
                    dve.wait_ge(ohi_done, o + d + 1)
                    dve.tensor_tensor(lo[:, d, :], sq[:, d % 4, :], hi[:, d, :].bitcast(F32),
                                      ALU.subtract).then_inc(opnd_ready, 1)
                for d in range(KT):
                    if d >= 4:
                        dve.wait_ge(opnd_ready, o + d - 3)
                    ins = dve.scalar_tensor_tensor(out=sq[:, d % 4, :], in0=src[:, d, :], scalar=gains[:, g0 + d:g0 + d + 1],
                                                   in1=ps[:, bank(d), :], op0=ALU.mult, op1=ALU.mult)
                    if gate is not None:
                        ins.then_inc(g_gated, 1)
                        dve.wait_ge(g_gated, d + 1)
                        ins = dve.tensor_tensor(sq[:, d % 4, :], sq[:, d % 4, :], gate[:, d, :], ALU.mult)
                    ins.then_inc(omul_done, 1)
                    if d:
                        low(d - 1)
                low(KT - 1)

            def add_x(xc, n, i, j, scale):
                dve.wait_ge(unit_used, n + 1 + j + 4 * i)
                dve.wait_ge(x_upd, xc)
                xt = x[:, bass.ds(4 * i + j, 1), :] if not isinstance(i, int) else x[:, 4 * i + j:4 * i + j + 1, :]
                dve.scalar_tensor_tensor(out=xt, in0=ps[:, 4 + j:5 + j, :], scalar=scale, in1=xt,
                                         op0=ALU.mult, op1=ALU.add).then_inc(x_upd, 1)

            def ffn(st):
                n = UB[st]
                fb = FT * [s for s in STAGES if s.startswith("ffn")].index(st)
                z = NORMS[st]
                rsqrt(z, TT, 1.0 / D)
                operand(z, OPS[st], x, KT * int(st[3]), lambda d: 3, h_hi, h_lo)
                xc = XB[st]
                for ph, (f0, nf) in enumerate(PHASES):
                    f = fb + f0
                    with dve.Fori(0, nf // 2) as i:
                        for j in range(2):
                            produce_lo(n + 2 * j + SLOTS, i)
                            dve.wait_ge(silu_done, f + 2 * i + j + 2)
                            dve.wait_ge(unit_used, n + 4 * i + 2 * j + 2)
                            dve.wait_ge(alo_done, f + 2 * i + 1)
                            dve.tensor_tensor(prod[:, j, :], sg[:, j, :], ps[:, 2 * j + 1, :], ALU.mult).then_inc(mul_done, 1)
                            dve.wait_ge(mul_done, f + 2 * i + j + 2)
                            dve.tensor_copy(act_hi[:, bass.ds(2 * i + j, 1), :], prod[:, j:j + 1, :]).then_inc(ahi_done, 1)
                            dve.wait_ge(ahi_done, f + 2 * i + j + 1)
                            dve.tensor_tensor(act_lo[:, bass.ds(2 * i + j, 1), :], prod[:, j:j + 1, :],
                                              act_hi[:, bass.ds(2 * i + j, 1), :].bitcast(F32), ALU.subtract).then_inc(alo_done, 1)
                            produce_lo(n + 2 * j + 1 + SLOTS, i)
                    n += 2 * nf
                    if ph < 2:
                        with dve.Fori(0, 2) as i:
                            for j in range(4):
                                add_x(xc, n, i, j, 0.5)
                                produce_lo(n + j + SLOTS, i)
                    else:
                        for m in range(KT):
                            add_x(xc, n, m // 4, m % 4, 0.5)
                            produce_lo(n + m + SLOTS)
                    n += KT
                    xc += KT

            def mix0():
                n = UB["mix0"]
                z = NORMS["mix0"]
                rsqrt(z, TT, 1.0 / D)
                operand(z, OPS["mix0"], x, 32, lambda d: 3, h_hi, h_lo)
                for t in range(9):
                    produce_lo(n + t + SLOTS)
                    if t == 1:
                        for h in range(GH):
                            dve.wait_ge(g_gate_mm, h + 1)
                            dve.tensor_scalar(gm[:, 1, h, :], ps[:, h, :], gains[:, GB_B + h:GB_B + h + 1], None,
                                              ALU.add).then_inc(g_gate_b, 1)
                g1 = gm[:, 1, :, :]
                dve.wait_ge(g_abs, 3)
                dve.scalar_tensor_tensor(out=g1, in0=g1, scalar=0.0, in1=gm[:, 0, :, :], op0=ALU.min,
                                         op1=ALU.subtract).then_inc(g_scan, 1)
                dve.wait_ge(g_scan, 1)
                for h in range(GH):
                    for c in range(TT):
                        dve.tensor_tensor_scan(gb[:, h, c * P:(c + 1) * P], ones[:, :], gm[:, 1, h, c * P:(c + 1) * P], 0.0,
                                               ALU.mult, ALU.add).then_inc(g_scan, 1)
                dve.wait_ge(g_scan, 1 + GH * TT)

                def level(m, s):
                    return m.rearrange("p h t -> p (h t)").rearrange("p (n two s) -> p n two s", two=2, s=s)

                def diff(l):
                    s = 1 << (LEVELS - 1 - l)
                    b4, m4 = level(gb[:, :, :], s), level(gm[:, l % 2, :, :], s)
                    ref = b4[:, :, 0, s - 1:s].to_broadcast([P, GH * TOK // (2 * s), s])
                    if l >= 2:
                        dve.wait_ge(g_lvl, TT * (l - 1))
                    dve.tensor_tensor(m4[:, :, 0, :], ref, b4[:, :, 0, :], ALU.subtract).then_inc(g_diff, 1)
                    dve.tensor_tensor(m4[:, :, 1, :], b4[:, :, 1, :], ref, ALU.subtract).then_inc(g_diff, 1)

                def mult(l):
                    s = 1 << (LEVELS - 1 - l)
                    m4 = level(gm[:, l % 2, :, :], s)
                    dve.wait_ge(g_exp, l + 1)
                    dve.tensor_tensor(m4[:, :, 0, :], m4[:, :, 0, :], level(gk[:, :, :], s)[:, :, 0, :], ALU.mult).then_inc(g_mul, 1)
                    dve.tensor_tensor(m4[:, :, 1, :], m4[:, :, 1, :], level(gq[:, :, :], s)[:, :, 1, :], ALU.mult).then_inc(g_mul, 1)

                def masked(l):
                    for c in range(TT):
                        dve.wait_ge(g_lvl, TT * l + c + 1)
                        if l:
                            dve.wait_ge(g_mask, TT * (l - 1) + c + 1)
                        dve.copy_predicated(gattn[:, c, :, :], masks[:, l:l + 1, :].to_broadcast([P, GH, P]),
                                            ps[:, c, :].rearrange("p (h t) -> p h t", h=GH)).then_inc(g_mask, 1)

                def v_out(v):
                    dve.wait_ge(g_vt, v + 1)
                    dve.tensor_copy(gv[:, :, v * P:(v + 1) * P], ps[:, v % 2, :].rearrange("p (c d) -> p c d", c=TT)).then_inc(g_vev, 1)
                dve.wait_ge(g_zero, 1)
                for s in range(8):
                    if s < LEVELS:
                        diff(s)
                    produce_lo(n + 9 + 2 * s + SLOTS)
                    if s >= 4:
                        v_out(2 * (s - 4))
                        v_out(2 * (s - 4) + 1)
                    produce_lo(n + 10 + 2 * s + SLOTS)
                    if s < LEVELS:
                        mult(s)
                    if s:
                        masked(s - 1)
                dve.wait_ge(g_mul, 2 * LEVELS)
                b3 = gb[:, :, :].rearrange("p h (c t) -> p (h c) t", t=P)
                m3 = gm[:, 1, :, :].rearrange("p h (c t) -> p (h c) t", t=P)
                dve.wait_ge(g_lvl, TT * LEVELS)
                dve.tensor_tensor(m3, b3[:, :, P - 1:P].to_broadcast([P, GH * TT, P]), b3, ALU.subtract).then_inc(g_decm, 1)
                masked(LEVELS)
                dve.wait_ge(g_dec, 1)
                dve.tensor_tensor(gq[:, :, :], gq[:, :, :], gm[:, 0, :, :], ALU.mult).then_inc(g_decm, 1)
                dve.wait_ge(g_dec, 3)
                dve.tensor_tensor(gk[:, :, :], gk[:, :, :], gm[:, 1, :, :], ALU.mult).then_inc(g_decm, 1)
                dve.wait_ge(g_decm, 3)
                for c in range(TT):
                    dve.wait_ge(g_kt, c + 1)
                    dve.tensor_copy(gkd[:, c, :, :], ps[:, c, :].rearrange("p (h k) -> p h k", h=GH)).then_inc(g_kev, 1)
                R = slice(DT0, DT0 + SH)
                dve.wait_ge(tile_out, 5)
                dve.tensor_scalar(small[R, :], small[R, :], pcols[R, 8:9], None, ALU.add).then_inc(s_dta, 1)
                for c in range(TT - 1):
                    for h in range(GH):
                        dve.wait_ge(g_st, GH * c + 2 * (h // 2) + 2)
                        src = ps[:, 2 * (c % 2) + h // 2, (h % 2) * GDV:(h % 2 + 1) * GDV]
                        if c == 0:
                            dve.tensor_copy(gS[:, h, :], src).then_inc(g_S, 1)
                        else:
                            dve.wait_ge(g_o, c + 1)
                            dve.wait_ge(g_S, GH * (c - 1) + h + 1)
                            dve.scalar_tensor_tensor(out=gS[:, h, :], in0=gS[:, h, :], scalar=el[:, h, c:c + 1], in1=src,
                                                     op0=ALU.mult, op1=ALU.add).then_inc(g_S, 1)
                dve.wait_ge(s_dt, 4)
                dve.scalar_tensor_tensor(out=small[R, :], in0=small[R, :], scalar=0.0, in1=dt_tmp[R, 0, :],
                                         op0=ALU.max, op1=ALU.add).then_inc(s_dta, 1)
                dve.wait_ge(s_dta, 2)
                dve.tensor_scalar(dt_tmp[R, 1, :], small[R, :], pcols[R, 10:11], -1.0, ALU.mult, ALU.mult).then_inc(s_dta, 1)
                dve.wait_ge(s_dta, 3)
                for c in range(TT):
                    dve.tensor_tensor_scan(dt_tmp[R, 2, c * P:(c + 1) * P], ones[R, :], dt_tmp[R, 1, c * P:(c + 1) * P], 0.0,
                                           ALU.mult, ALU.add).then_inc(s_acum, 1)
                dve.wait_ge(s_tok, 1)
                dve.tensor_copy(toks[:, :, :, :], ps[:, 0, 0:2 * TT * SH].rearrange("p (a c h) -> p a c h", a=2, c=TT)).then_inc(s_tokev, 1)
                z = NORMS["gla"]
                rsqrt(z, GH * TT, 1.0 / GDV)
                operand(z, OPS["gla"], gvT, GB_N, lambda d: d // 2, o_hi, o_lo, gr)
                n0 = n + 25
                with dve.Fori(0, 2) as i:
                    for j in range(4):
                        add_x(XB["mix0"], n0, i, j, 1.0)
                        produce_lo(n0 + j + SLOTS, i)
                n0 += KT
                with dve.Fori(0, 2) as i:
                    for j in range(4):
                        produce_lo(n0 + j + SLOTS, i)
                n0 += SI // P
                taps = [0]
                for m in range(XT):
                    produce_lo(n0 + m + SLOTS)
                    dve.wait_ge(tile_out, 4 + 25 + SI // P + m + 1)
                    if m >= 2:
                        dve.wait_ge(s_silu, m - 1)
                    cv = sq[:, m % 2, :]
                    dve.tensor_scalar(cv, xp[:, m % 2, 0:TOK], gains[:, GB_CW + m:GB_CW + m + 1],
                                      gains[:, GB_CB + m:GB_CB + m + 1], ALU.mult, ALU.add).then_inc(s_conv, 1)
                    for k in range(1, TAPS):
                        taps[0] += 1
                        dve.wait_ge(s_conv, taps[0])
                        dve.scalar_tensor_tensor(out=cv, in0=xp[:, m % 2, k:k + TOK],
                                                 scalar=gains[:, GB_CW + XT * k + m:GB_CW + XT * k + m + 1],
                                                 in1=cv, op0=ALU.mult, op1=ALU.add).then_inc(s_conv if k < TAPS - 1 else s_conved, 1)
                acum_tok, dt_tok = toks[:, 1, :, :], toks[:, 0, :, :]
                for c in range(TT):
                    dve.wait_ge(s_acb[c % 2], 16 * (c // 2 + 1))
                    ab = acb[:, c % 2, :, :]
                    if c:
                        dve.wait_ge(s_y, c)
                    for h in range(SH):
                        ins = dve.tensor_scalar(pm[:, h, :], ab[:, h, :], acum_tok[:, c, h:h + 1], 0.0, ALU.subtract, ALU.min)
                    ins.then_inc(s_D, 1)
                    if c:
                        dve.wait_ge(s_xdtw, c)
                    dve.tensor_tensor(wtok[:, 0, :], ab[:, :, P - 1], acum_tok[:, c, :], ALU.subtract).then_inc(s_wd, 1)
                    dve.wait_ge(s_cb, c + 1)
                    dve.tensor_tensor(cb[:, :, :], ps[:, 0, 0:SG * P].rearrange("p (g t) -> p g t", g=SG),
                                      tri[:, :].rearrange("p (o t) -> p o t", o=1).to_broadcast([P, SG, P]), ALU.mult).then_inc(s_cbm, 1)
                    dve.wait_ge(s_tr, c + 1)
                    if c:
                        dve.wait_ge(s_st, c)
                    dve.tensor_tensor(xdt[:, :].rearrange("p (h d) -> p h d", h=SH),
                                      ps[:, 2:4, :].rearrange("p b (h d) -> p (b h) d", d=SHD),
                                      dt_tok[:, c, :].rearrange("p (h o) -> p h o", o=1).to_broadcast([P, SH, SHD]),
                                      ALU.mult).then_inc(s_xdt, 1)
                    dve.wait_ge(s_ea, 2 * c + 2)
                    hg = SH // SG
                    for g in range(SG):
                        dve.tensor_tensor(ce[:, g * hg:(g + 1) * hg, :], ce[:, g * hg:(g + 1) * hg, :],
                                          xbc[:, 10 + g:11 + g, c * P:(c + 1) * P].to_broadcast([P, hg, P]), ALU.mult).then_inc(s_C, 1)
                    dve.wait_ge(s_pexp, c + 1)
                    dve.wait_ge(s_cbm, c + 1)
                    for g in range(SG):
                        dve.tensor_tensor(pm[:, g * hg:(g + 1) * hg, :], pm[:, g * hg:(g + 1) * hg, :],
                                          cb[:, g:g + 1, :].to_broadcast([P, hg, P]), ALU.mult).then_inc(s_P, 1)
                    dve.wait_ge(s_w, c + 1)
                    dve.wait_ge(s_xdt, c + 1)
                    dve.tensor_tensor(xdtw[:, :].rearrange("p (h d) -> p h d", h=SH),
                                      xdt[:, :].rearrange("p (h d) -> p h d", h=SH),
                                      wtok[:, 0, :].rearrange("p (h o) -> p h o", o=1).to_broadcast([P, SH, SHD]),
                                      ALU.mult).then_inc(s_xdtw, 1)
                    dve.wait_ge(s_y, c + 1)
                    if c < TT - 1:
                        if c:
                            dve.tensor_tensor(sS[:, :].rearrange("p (h d) -> p h d", h=SH), sS[:, :].rearrange("p (h d) -> p h d", h=SH),
                                              wtok[:, 1, :].rearrange("p (h o) -> p h o", o=1).to_broadcast([P, SH, SHD]),
                                              ALU.mult).then_inc(s_S1, 1)
                        dve.wait_ge(s_st, c + 1)
                        if c:
                            dve.wait_ge(s_S1, c)
                            dve.tensor_tensor(sS[:, :], sS[:, :], ps[:, 2:4, :].rearrange("p b t -> p (b t)"), ALU.add).then_inc(s_S2, 1)
                        else:
                            dve.tensor_copy(sS[:, :], ps[:, 2:4, :].rearrange("p b t -> p (b t)")).then_inc(s_S2, 1)
                    for m in range(SI // P):
                        xt = xbc[:, m, c * P:(c + 1) * P]
                        ins = dve.scalar_tensor_tensor(out=xt, in0=xt, scalar=pcols[:, m:m + 1],
                                                       in1=ps[:, 4 + 2 * (c % 2) + m // 4, (m % 4) * P:(m % 4 + 1) * P],
                                                       op0=ALU.mult, op1=ALU.add)
                    ins.then_inc(s_yev, 1)
                dve.wait_ge(s_yev, TT)
                for m in range(SI // P):
                    dve.tensor_tensor(xbc[:, m, :], xbc[:, m, :], sz[:, m, :], ALU.mult).then_inc(s_gate, 1)
                z = NORMS["ssd"]
                rsqrt(z, SG * TT, 1.0 / (SI // SG))
                operand(z, OPS["ssd"], xbc, GB_SN, lambda d: d // 4, h_hi, h_lo)
                n0 = n + NU["mix0"] - KT
                for m in range(KT):
                    add_x(XB["mix0"] + KT, n0, m // 4, m % 4, 1.0)
                    produce_lo(n0 + m + SLOTS)

            def mix1():
                n = UB["mix1"]
                z = NORMS["mix1"]
                dve.wait_ge(a_cneg, 2)
                dve.tensor_copy(identr[:, :], ident[:, :]).then_inc(a_const, 1)
                dve.tensor_scalar(cmat[:, :], ident[0:IDIM, 0:IDIM], 1.0 / IDIM, None, ALU.subtract).then_inc(a_const, 1)
                rsqrt(z, TT, 1.0 / D)
                operand(z, OPS["mix1"], x, 40, lambda d: 3, h_hi, h_lo)
                for t in range(4):
                    produce_lo(n + t + SLOTS)
                dve.wait_ge(d_ss, 1)
                val, y, t = rs[:, 0, 0:12], rs[:, 1, 0:12], rs[:, 2, 0:12]
                for c, width in enumerate((AQR, AL, IDIM)):
                    step(dve.tensor_scalar(rs[:, 0, 4 * c:4 * c + 4], ps[:, 2, 4 * c:4 * c + 4], 1.0 / width, EPS, ALU.mult, ALU.add))
                newton(val, y, t).then_inc(d_rs, 1)
                dve.wait_ge(d_bc, 1)
                for d in range(2):
                    dve.scalar_tensor_tensor(out=sq[:, d, :], in0=qlr[:, d, :], scalar=gains[:, GB_Q + d:GB_Q + d + 1],
                                             in1=ps[:, 0, :], op0=ALU.mult, op1=ALU.mult).then_inc(d_mul, 1)
                dve.scalar_tensor_tensor(out=kvT[:, :], in0=kvr[:, :], scalar=gains[:, GB_KV:GB_KV + 1],
                                         in1=ps[:, 1, :], op0=ALU.mult, op1=ALU.mult).then_inc(d_kv, 1)
                for d in range(2):
                    dve.wait_ge(d_hi, d + 1)
                    dve.tensor_tensor(ql_lo[:, d, :], sq[:, d, :], ql_hi[:, d, :].bitcast(F32), ALU.subtract).then_inc(d_ql, 1)
                dve.wait_ge(d_kc, 1)
                dve.scalar_tensor_tensor(out=kn[0:IDIM, :], in0=kc[:, :], scalar=pcols[0:IDIM, 11:12],
                                         in1=ps[0:IDIM, 3, :], op0=ALU.mult, op1=ALU.mult).then_inc(d_kn, 1)
                dve.wait_ge(d_kn, 1)
                dve.tensor_scalar(kn[0:IDIM, :], kn[0:IDIM, :], pcols[0:IDIM, 12:13], None, ALU.add).then_inc(d_kn, 1)
                dve.wait_ge(d_kv, 1)
                dve.wait_ge(d_tr, 1)
                dve.tensor_copy(amask[:, 0, 0:P], cneg[:, :]).then_inc(k_mask, 1)
                for t in range(6):
                    produce_lo(n + 4 + t + SLOTS)
                dve.wait_ge(d_trev, 1)
                for r in range((TT - 1) * IH):
                    b, h = r // IH, r % IH
                    w = P * (b + 2)
                    dve.wait_ge(d_relu, r + 1)
                    wcol = wtk[:, b + 1, h:h + 1]
                    if h == 0:
                        dve.tensor_scalar(sc[:, b, 0:w], sq[:, r % 4, 0:w], wcol, None, ALU.mult).then_inc(d_acc, 1)
                    else:
                        dve.wait_ge(d_acc, r)
                        dve.scalar_tensor_tensor(out=sc[:, b, 0:w], in0=sq[:, r % 4, 0:w], scalar=wcol, in1=sc[:, b, 0:w],
                                                 op0=ALU.mult, op1=ALU.add).then_inc(d_acc, 1)
                NI = (TT - 1) * IH
                dve.wait_ge(d_acc, NI)
                for b in range(TT - 1):
                    dve.tensor_tensor(sc[:, b, P * (b + 1):P * (b + 2)], sc[:, b, P * (b + 1):P * (b + 2)], cneg[:, :], ALU.add).then_inc(d_acc, 1)
                dve.wait_ge(d_acc, NI + TT - 1)
                dve.wait_ge(t_landed, 16)
                NR = TT * AH
                tops = [0]
                for r in range(NR + 1):
                    b, h = r // AH, r % AH
                    w = P * (b + 1)
                    if r < NR:
                        dve.wait_ge(a_log, r + 1)
                        if r >= 4:
                            dve.wait_ge(a_tr, r - 3)
                        dve.tensor_tensor_reduce(lp[:, r % 4, 0:w], ps[:, r % 2, 0:w], aT[:, h, TOK - w:TOK], -1.0, 3e38,
                                                 ALU.add, ALU.min, stat[:, 0, r % 4:r % 4 + 1]).then_inc(a_max, 1)
                        if b < TT - 1:
                            s1 = sc[:, b, 0:w + P]
                            if tops[0]:
                                dve.wait_ge(k_top, tops[0])
                            dve.max(stat[:, 3, :], s1).then_inc(k_top, 1)
                            tops[0] += 1
                            dve.wait_ge(k_top, tops[0])
                            dve.match_replace(s1, stat[:, 3, :], s1, TAKEN).then_inc(k_top, 1)
                            tops[0] += 1
                            if h == AH - 1:
                                dve.wait_ge(k_top, tops[0])
                                dve.tensor_scalar(amask[:, b + 1, 0:w + P], s1, TAKEN, MASKED, ALU.not_equal, ALU.mult).then_inc(k_mask, 1)
                    if r:
                        q = r - 1
                        dve.wait_ge(a_exp, r)
                        if q >= 4:
                            dve.wait_ge(a_nrm, q - 3)
                        dve.reciprocal(stat[:, 2, q % 4:q % 4 + 1], stat[:, 1, q % 4:q % 4 + 1]).then_inc(a_rec, 1)
                for d in range(KT):
                    dve.wait_ge(ohi_done, OPS["dsa"] + d + 1)
                    dve.tensor_tensor(o_lo[:, d, :], ao[:, d, :], o_hi[:, d, :].bitcast(F32), ALU.subtract).then_inc(opnd_ready, 1)
                dve.sem_inc(omul_done, KT)
                n0 = n + NU["mix1"] - KT
                for m in range(KT):
                    add_x(XB["mix1"], n0, m // 4, m % 4, 1.0)
                    produce_lo(n0 + m + SLOTS)

            dve.sem_inc(mul_done, 1)
            dve.sem_inc(alo_done, 1)
            dve.sem_inc(silu_done, 1)
            dve.sem_inc(tile_out, 4)
            dve.wait_ge(iota_ready, 2)
            ms = [0]

            def mstep(ins):
                ms[0] += 1
                ins.then_inc(mask_steps, 1)
                dve.wait_ge(mask_steps, ms[0])
            mstep(dve.tensor_tensor(ij[:, 2, :], ij[:, 0, :], ij[:, 1, :], ALU.bitwise_xor))
            mstep(dve.tensor_tensor(tri[:, :], ij[:, 0, :], ij[:, 1, :], ALU.is_ge))
            for l in range(LEVELS):
                mstep(dve.tensor_scalar(ij[:, 3, :], ij[:, 2, :], LEVELS - 1 - l, None, ALU.logical_shift_right))
                mstep(dve.scalar_tensor_tensor(out=masks[:, l, :], in0=ij[:, 3, :], scalar=1.0, in1=tri[:, :],
                                               op0=ALU.is_equal, op1=ALU.mult))
            mstep(dve.tensor_scalar(masks[:, LEVELS, :], ij[:, 2, :], 0.0, None, ALU.is_equal))
            dve.wait_ge(par_done, 2)
            dve.wait_ge(par_landed, 16 * 15)
            dve.tensor_copy(gains[:, 0:83], ps[:, 0, 0:83]).then_inc(gains_ready, 1)
            dve.tensor_copy(gains[:, GB_CW:GB_CW + 48], ps[:, 1, 0:48]).then_inc(gains_ready, 1)
            for m in range(KT):
                dve.wait_ge(xt_done, m + 1)
                dve.tensor_copy(x[:, m, :], ps[:, 4 + m % 4, :]).then_inc(x_upd, 1)
            for n in range(SLOTS):
                produce_lo(n)
            dve.wait_ge(gains_ready, 2)
            for st in STAGES:
                if st.startswith("ffn"):
                    ffn(st)
                elif st == "mix0":
                    mix0()
                else:
                    mix1()
            rsqrt(NORMS["final"], TT, 1.0 / D)
            dve.wait_ge(rstd_ready, NORMS["final"] + 1)
            dve.wait_ge(gfin_landed, 16)
            for t in range(TT):
                if t >= 2:
                    dve.wait_ge(stored[t % 2], 16)
                for c in range(2):
                    dve.wait_ge(fin_t, 2 * t + c + 1)
                    dve.scalar_tensor_tensor(out=otile[:, t % 2, c * 512:(c + 1) * 512], in0=ps[:, 4 + (2 * t + c) % 4, :],
                                             scalar=rs[:, 1, t:t + 1], in1=gfin[:, c * 512:(c + 1) * 512],
                                             op0=ALU.mult, op1=ALU.mult).then_inc(fin_ready, 1)

        @block.tensor
        def _(pe):
            def unit(n, bank, rh, rl, nk, i=0, ready=None):
                s = n % SLOTS
                pe.wait_ge(lo_ready, n + 1 + 4 * i)
                for k in range(nk):
                    if ready:
                        ready(k)
                    wh, wl = w_hi[:, s, k * P:(k + 1) * P], w_lo[:, s, k * P:(k + 1) * P]
                    pe.matmul(ps[:, bank, :], wh, rh[:, k, :], start=k == 0, stop=False)
                    pe.matmul(ps[:, bank, :], wh, rl[:, k, :], start=False, stop=False)
                    mm = pe.matmul(ps[:, bank, :], wl, rh[:, k, :], start=False, stop=k == nk - 1)
                mm.then_inc(unit_used, 1)

            def sumsq(z, m, cols=None, first=None, last=None):
                pe.wait_ge(sq_ready, KT * z + m + 1)
                c0 = cols if cols is not None else 0
                for t in range(TT):
                    mm = pe.matmul(ps[:, 2, c0 + t:c0 + t + 1], sq[:, m % 4, t * P:(t + 1) * P], ones[:, 0:1],
                                   start=(m == 0 and t == 0), stop=(m == KT - 1 if last is None else last), skip_group_check=True)
                mm.then_inc(ss_done, 1)

            def spread(z, banks):
                pe.wait_ge(rstd_ready, z + 1)
                for b, bank in enumerate(banks):
                    for t in range(TT):
                        c = b * TT + t
                        mm = pe.matmul(ps[:, bank, t * P:(t + 1) * P], rs[:, 1, c:c + 1].to_broadcast([P, P]), ident[:, :],
                                       start=True, stop=True, skip_group_check=True)
                mm.then_inc(bc_done, 1)

            def ready_of(o):
                return lambda k: pe.wait_ge(opnd_ready, o + k + 1)

            def ffn(st, nxt):
                n = UB[st]
                fb = FT * [s for s in STAGES if s.startswith("ffn")].index(st)
                xc = XB[st]
                spread(NORMS[st], [3])
                for ph, (f0, nf) in enumerate(PHASES):
                    f = fb + f0
                    with pe.Fori(0, nf // 2) as i:
                        for j in range(2):
                            pe.wait_ge(silu_done, f + 2 * i + 1)
                            unit(n + 2 * j, 2 * j, h_hi, h_lo, KT, i, ready_of(OPS[st]) if (ph == 0 and j == 0) else None)
                            pe.wait_ge(mul_done, f + 2 * i + 1)
                            unit(n + 2 * j + 1, 2 * j + 1, h_hi, h_lo, KT, i)
                    n += 2 * nf
                    pe.wait_ge(alo_done, f + nf - 2 + 1)

                    def dwait(k):
                        if k >= nf - 2:
                            pe.wait_ge(alo_done, f + k + 2)
                    if ph < 2:
                        with pe.Fori(0, 2) as i:
                            for j in range(4):
                                pe.wait_ge(x_upd, xc - 4 + j + 1 + 4 * i)
                                unit(n + j, 4 + j, act_hi, act_lo, nf, i, dwait if j == 0 else None)
                    else:
                        z = NORMS[nxt]
                        for m in range(KT):
                            pe.wait_ge(x_upd, xc - 4 + m + 1)
                            unit(n + m, 4 + m % 4, act_hi, act_lo, nf, 0, dwait if m == 0 else None)
                            if m:
                                sumsq(z, m - 1)
                        sumsq(z, KT - 1)
                    n += KT
                    xc += KT

            def mix0(nxt):
                n = UB["mix0"]
                spread(NORMS["mix0"], [3])
                pe.wait_ge(wg2_landed, 16)
                unit(n, 4, h_hi, h_lo, KT, 0, ready_of(OPS["mix0"]))
                unit(n + 1, 5, h_hi, h_lo, KT)
                pe.wait_ge(g_glr, 1)
                for h in range(GH):
                    pe.matmul(ps[:, h, :], small[0:GRANK, h * P:(h + 1) * P], sq[0:GRANK, 0, :], start=True, stop=True).then_inc(g_gate_mm, 1)
                for t in range(2, 9):
                    pe.wait_ge(tile_out, t + 1)
                    unit(n + t, 4 + t % 4, h_hi, h_lo, KT)

                def level(l):
                    if l < LEVELS:
                        pe.wait_ge(g_mul, 2 * (l + 1))
                    for c in range(TT):
                        if l:
                            pe.wait_ge(g_mask, TT * (l - 1) + c + 1)
                        for h in range(GH):
                            kk = gm[:, l % 2, h, c * P:(c + 1) * P] if l < LEVELS else gk[:, h, c * P:(c + 1) * P]
                            qq = gm[:, l % 2, h, c * P:(c + 1) * P] if l < LEVELS else gq[:, h, c * P:(c + 1) * P]
                            mm = pe.matmul(ps[:, c, h * P:(h + 1) * P], kk, qq, start=True, stop=True, skip_group_check=True)
                        mm.then_inc(g_lvl, 1)
                for s in range(8):
                    for j in range(2):
                        t = 9 + 2 * s + j
                        pe.wait_ge(tile_out, t + 1)
                        unit(n + t, 4 + t % 4, h_hi, h_lo, KT)
                        if s >= 4:
                            v = 2 * (s - 4) + j
                            pe.wait_ge(g_mask, TT * (s - 2) + v % 2 + 1)
                            pe.wait_ge(tile_out, 4 + 9 + v + 1)
                            for c in range(TT):
                                mm = pe.transpose(ps[:, v % 2, c * P:(c + 1) * P], gvT[:, v, c * P:(c + 1) * P], ident[:, :])
                            mm.then_inc(g_vt, 1)
                    if s >= 4:
                        pe.wait_ge(g_vev, 2 * (s - 3))
                    if s:
                        level(s - 1) if s < 7 else None
                    if s == 7:
                        level(6)
                level(LEVELS)
                pe.wait_ge(tile_out, 4 + 25)
                pe.wait_ge(g_decm, 3)
                for c in range(TT):
                    pe.wait_ge(g_mask, TT * LEVELS + c + 1)
                    for h in range(GH):
                        mm = pe.transpose(ps[:, c, h * P:(h + 1) * P], gk[:, h, c * P:(c + 1) * P], ident[:, :])
                    mm.then_inc(g_kt, 1)
                for c in range(TT):
                    if c >= 2:
                        pe.wait_ge(g_oev, 2 * (c - 1))
                    if c:
                        pe.wait_ge(g_S, GH * c)
                    for m in range(GVT):
                        h, vt = m // 2, m % 2
                        dst = ps[:, 4 + 2 * (c % 2) + m // 4, (m % 4) * P:(m % 4 + 1) * P]
                        if c:
                            pe.matmul(dst, gS[:, h, vt * P:(vt + 1) * P], gq[:, h, c * P:(c + 1) * P], start=True, stop=False, skip_group_check=True)
                        mm = pe.matmul(dst, gv[:, c, m * P:(m + 1) * P], gattn[:, c, h, :], start=c == 0, stop=True, skip_group_check=True)
                    mm.then_inc(g_o, 1)
                    if c < TT - 1:
                        pe.wait_ge(g_kev, TT)
                        for h in range(GH):
                            pe.matmul(ps[:, 2 * (c % 2) + h // 2, (h % 2) * GDV:(h % 2 + 1) * GDV], gkd[:, c, h, :],
                                      gv[:, c, h * GDV:(h + 1) * GDV], start=True, stop=True, skip_group_check=True).then_inc(g_st, 1)
                R = slice(DT0, DT0 + SH)
                pe.wait_ge(s_acum, TT)
                pe.wait_ge(g_S, GH * (TT - 1))
                for b in range(2):
                    for c in range(TT):
                        src = (small[R, c * P:(c + 1) * P], dt_tmp[R, 2, c * P:(c + 1) * P])[b]
                        mm = pe.transpose(ps[:, 0, (b * TT + c) * SH:(b * TT + c + 1) * SH], src, ident[R, R])
                mm.then_inc(s_tok, 1)
                z = NORMS["gla"]
                for m in range(GVT):
                    sumsq(z, m, (m // 2) * TT)
                pe.wait_ge(s_tokev, 1)
                spread(z, [0, 1, 2, 3])
                n0 = n + 25
                for m in range(KT):
                    if m >= 4:
                        pe.wait_ge(x_upd, XB["mix0"] + m - 3)
                    unit(n0 + m, 4 + m % 4, o_hi, o_lo, KT, 0, ready_of(OPS["gla"]) if m == 0 else None)
                n0 += KT
                pe.wait_ge(x_upd, XB["mix0"] + KT)
                tb = 25
                with pe.Fori(0, (SI // P + XT) // 4) as i:
                    for j in range(4):
                        pe.wait_ge(tile_out, tb + j + 1 + 4 * i)
                        unit(n0 + j, 4 + (tb + j) % 4, h_hi, h_lo, KT, i)
                pe.wait_ge(s_silu, XT)
                for c in range(TT):
                    if c:
                        pe.wait_ge(s_cbm, c)
                        pe.wait_ge(s_Bev, c)
                        pe.wait_ge(s_S2, c)
                    cc = slice(c * P, (c + 1) * P)
                    for g in range(SG):
                        mm = pe.matmul(ps[:, 0, g * P:(g + 1) * P], xbc[:, 8 + g, cc], xbc[:, 10 + g, cc], start=True, stop=True, skip_group_check=True)
                    mm.then_inc(s_cb, 1)
                    for g in range(SG):
                        mm = pe.transpose(ps[:, 1, g * P:(g + 1) * P], xbc[:, 8 + g, cc], ident[:, :])
                    mm.then_inc(s_trB, 1)
                    for m in range(SI // P):
                        mm = pe.transpose(ps[:, 2 + m // 4, (m % 4) * P:(m % 4 + 1) * P], xbc[:, m, cc], ident[:, :])
                    mm.then_inc(s_tr, 1)
                    pe.wait_ge(s_Bev, c + 1)
                    pe.wait_ge(s_xdtw, c + 1)
                    if c < TT - 1:
                        for g in range(SG):
                            mm = pe.matmul(ps[:, 2 + g, :], sB[:, g, :], xdtw[:, g * 512:(g + 1) * 512], start=True, stop=True)
                        mm.then_inc(s_st, 1)
                    pe.wait_ge(s_P, 2 * (c + 1))
                    pe.wait_ge(s_C, 2 * (c + 1))
                    if c >= 2:
                        pe.wait_ge(s_yev, c - 1)
                    else:
                        pe.wait_ge(tile_out, 4 + 25 + SI // P + XT)
                    for h in range(SH):
                        m = h // 2
                        dst = ps[(h % 2) * SHD:(h % 2 + 1) * SHD, 4 + 2 * (c % 2) + m // 4, (m % 4) * P:(m % 4 + 1) * P]
                        if c:
                            pe.matmul(dst, sS[:, h * SHD:(h + 1) * SHD], ce[:, h, :], start=True, stop=False, skip_group_check=True)
                        mm = pe.matmul(dst, xdt[:, h * SHD:(h + 1) * SHD], pm[:, h, :], start=c == 0, stop=True, skip_group_check=True)
                    mm.then_inc(s_y, 1)
                z = NORMS["ssd"]
                for m in range(KT):
                    sumsq(z, m, (m // 4) * TT)
                spread(z, [0, 1])
                n0 = n + NU["mix0"] - KT
                z = NORMS[nxt]
                for m in range(KT):
                    if m >= 4:
                        pe.wait_ge(x_upd, XB["mix0"] + KT + m - 3)
                    unit(n0 + m, 4 + m % 4, h_hi, h_lo, KT, 0, ready_of(OPS["ssd"]) if m == 0 else None)
                    if m:
                        sumsq(z, m - 1)
                sumsq(z, KT - 1)

            def mix1(nxt):
                n = UB["mix1"]
                spread(NORMS["mix1"], [3])
                for t in range(4):
                    pe.wait_ge(tile_out, T1 + t + 1)
                    unit(n + t, 4 + (T1 + t) % 4, h_hi, h_lo, KT, 0, ready_of(OPS["mix1"]) if t == 0 else None)
                pe.wait_ge(a_const, 2)
                pe.wait_ge(d_kx, 1)
                pe.matmul(ps[0:IDIM, 0, :], cmat[:, :], kx[0:IDIM, :], start=True, stop=True).then_inc(d_cen, 1)
                pe.wait_ge(tile_out, T1 + 4 + 3)
                for c in range(2):
                    for j in ((0, 1), (2,))[c]:
                        for t in range(TT):
                            pe.matmul(ps[:, 2, 4 * c + t:4 * c + t + 1], sq[:, j, t * P:(t + 1) * P], ones[:, 0:1],
                                      start=j == 0 and t == 0, stop=j == 2, skip_group_check=True)
                pe.wait_ge(d_sq, 1)
                for t in range(TT):
                    mm = pe.matmul(ps[:, 2, 8 + t:9 + t], sq[0:IDIM, 3, t * P:(t + 1) * P], ones[0:IDIM, 0:1],
                                   start=False, stop=True, skip_group_check=True)
                mm.then_inc(d_ss, 1)
                pe.wait_ge(d_kc, 1)
                pe.wait_ge(d_rs, 1)
                for b, bank in enumerate((0, 1, 3)):
                    for t in range(TT):
                        c = b * TT + t
                        mm = pe.matmul(ps[:, bank, t * P:(t + 1) * P], rs[:, 1, c:c + 1].to_broadcast([P, P]), ident[:, :],
                                       start=True, stop=True, skip_group_check=True)
                mm.then_inc(d_bc, 1)
                R = slice(IDIM, IDIM + IH)
                pe.wait_ge(tile_out, T1 + 4 + 4)
                for c in range(TT):
                    mm = pe.transpose(ps[:, 2, c * IH:(c + 1) * IH], kx[R, c * P:(c + 1) * P], ident[R, R])
                mm.then_inc(d_tr, 1)
                pe.wait_ge(d_kv, 1)
                for c in range(TT):
                    mm = pe.transpose(ps[:, 0, c * P:(c + 1) * P], kvT[:, c * P:(c + 1) * P], ident[:, :])
                mm.then_inc(d_tr, 1)
                pe.wait_ge(d_ql, 2)
                for u in range(6):
                    s = (n + 4 + u) % SLOTS
                    pe.wait_ge(lo_ready, n + 4 + u + 1)
                    for j in range(4):
                        t = 4 * u + j
                        pe.wait_ge(tile_out, T1 + 4 + t + 1)
                        dst = ps[:, 4 + (T1 + t) % 4, :]
                        for k in range(2):
                            c0 = k * 512 + j * P
                            wh, wl = w_hi[:, s, c0:c0 + P], w_lo[:, s, c0:c0 + P]
                            pe.matmul(dst, wh, ql_hi[:, k, :], start=k == 0, stop=False)
                            pe.matmul(dst, wh, ql_lo[:, k, :], start=False, stop=False)
                            mm = pe.matmul(dst, wl, ql_hi[:, k, :], start=False, stop=k == 1)
                        mm.then_inc(unit_used if j == 3 else d_tile, 1)
                pe.wait_ge(d_dup, 16)
                for r in range((TT - 1) * IH):
                    b, h = r // IH + 1, r % IH
                    w = P * (b + 1)
                    R = slice((h % 2) * IDIM, (h % 2 + 1) * IDIM)
                    if r >= 4:
                        pe.wait_ge(d_relu, r - 3)
                    pe.matmul(ps[:, r % 4, 0:w], qix[R, h // 2, b * P:(b + 1) * P], kn[R, 0:w], start=True, stop=True).then_inc(d_ix, 1)
                pe.wait_ge(d_relu, (TT - 1) * IH)
                pe.wait_ge(tile_out, T1 + 4 + 4 + KT + AH)
                pe.wait_ge(uv_landed, 16)
                NR = TT * AH

                def p_turn(r):
                    b = r // AH
                    pe.wait_ge(a_nrm, r + 1)
                    if r >= 2:
                        pe.wait_ge(a_pt, r - 1)
                    for st in range(b + 1):
                        mm = pe.transpose(ps[:, 2 + r % 2, st * P:(st + 1) * P], lp[:, r % 4, st * P:(st + 1) * P], ident[:, :])
                    mm.then_inc(a_tr, 1)

                def latent(r):
                    b, g = r // AH, r // 4
                    pe.wait_ge(a_pt, r + 1)
                    if r % 4 == 0 and g >= 2:
                        pe.wait_ge(a_ol, g - 1)
                    for st in range(b + 1):
                        mm = pe.matmul(ps[:, 4 + g % 2, (r % 4) * P:(r % 4 + 1) * P], kvtok[:, st, :], pt[:, r % 2, st * P:(st + 1) * P],
                                       start=st == 0, stop=st == b, skip_group_check=True)
                    mm.then_inc(a_pv, 1)

                def values(g):
                    pe.wait_ge(a_ol, g + 1)
                    if g >= 4:
                        pe.wait_ge(a_o, g // 2 - 1)
                    for j in range(4):
                        h = (4 * g + j) % AH
                        m = h // 2
                        mm = pe.matmul(ps[(h % 2) * AV:(h % 2 + 1) * AV, 6 + m // 4, (m % 4) * P:(m % 4 + 1) * P], wuv[:, h, :],
                                       olat[:, g % 2, j * P:(j + 1) * P], start=True, stop=True, skip_group_check=True)
                    mm.then_inc(a_uv, 1)
                for r in range(NR + 5):
                    if r < NR:
                        b, h = r // AH, r % AH
                        w = P * (b + 1)
                        if h == 0:
                            pe.wait_ge(k_mask, b + 1)
                        if r >= 2:
                            pe.wait_ge(a_max, r - 1)
                        pe.matmul(ps[:, r % 2, 0:w], aq[:, h, b * P:(b + 1) * P], kvT[:, 0:w], start=True, stop=False)
                        pe.matmul(ps[:, r % 2, 0:w], identr[:, :], amask[:, b, 0:w], start=False, stop=True).then_inc(a_log, 1)
                    if 2 <= r < NR + 2:
                        p_turn(r - 2)
                    if 3 <= r < NR + 3:
                        latent(r - 3)
                    if r >= 5 and (r - 5) % 4 == 3 and (r - 5) // 4 < NR // 4:
                        values((r - 5) // 4)
                n0 = n + NU["mix1"] - KT
                z = NORMS[nxt]
                for m in range(KT):
                    if m >= 4:
                        pe.wait_ge(x_upd, XB["mix1"] + m - 3)
                    unit(n0 + m, 4 + m % 4, o_hi, o_lo, KT, 0, ready_of(OPS["dsa"]) if m == 0 else None)
                    if m:
                        sumsq(z, m - 1)
                sumsq(z, KT - 1)

            pe.wait_ge(consts_ready, 3)
            pe.wait_ge(l_landed, 32)
            pe.matmul(ps[0:AH, 2, :], relb[:, :], hot[:, 0:TOK], start=True, stop=True)
            pe.matmul(ps[0:AH, 3, 0:P], relb[:, :], hot[:, TOK:LINE], start=True, stop=True).then_inc(l_mm, 1)
            pe.wait_ge(par_landed, 16 * 15)
            pe.transpose(ps[:, 0, 0:83], prow[0:83, 0, :], ident[0:83, 0:83]).then_inc(par_done, 1)
            pe.transpose(ps[:, 1, 0:48], prow[0:48, 1, :], ident[0:48, 0:48]).then_inc(par_done, 1)
            pe.wait_ge(x_landed, 16)
            for m in range(KT):
                if m >= 4:
                    pe.wait_ge(x_upd, m - 3)
                for t in range(TT):
                    mm = pe.transpose(ps[:, 4 + m % 4, t * P:(t + 1) * P], x_in[:, t, m * P:(m + 1) * P], ident[:, :])
                mm.then_inc(xt_done, 1)
            pe.wait_ge(l_ev, 2)
            for m in range(KT):
                sumsq(0, m)
            for k, st in enumerate(STAGES):
                nxt = (STAGES + ["final"])[k + 1]
                if st.startswith("ffn"):
                    ffn(st, nxt)
                elif st == "mix0":
                    mix0(nxt)
                else:
                    mix1(nxt)
            for t in range(TT):
                for c in range(2):
                    if 2 * t + c >= 4:
                        pe.wait_ge(fin_ready, 2 * t + c - 3)
                    for m in range(4):
                        mm = pe.transpose(ps[:, 4 + (2 * t + c) % 4, m * P:(m + 1) * P],
                                          x[:, 4 * c + m, t * P:(t + 1) * P], ident[:, :])
                    mm.then_inc(fin_t, 1)


_INS = ["x", "ffn_norm_g", "ffn_w_gate", "ffn_w_up", "ffn_w_down", "mix_norm_g", "final_norm_g",
        "hy_w_in", "gla_w_gate2", "gla_b_gate", "gla_norm_g", "ssd_conv_w", "ssd_conv_b", "ssd_dt_bias", "ssd_a_log",
        "ssd_d", "ssd_norm_g", "hy_w_out",
        "dsa_w_dq", "dsa_q_norm_g", "dsa_w_uq", "dsa_w_dkv", "dsa_kv_norm_g", "dsa_w_uv", "dsa_w_o",
        "idx_w_q", "idx_w_k", "idx_ln_g", "idx_ln_b", "idx_w_w", "rel_bias"]


def _CONSTS():
    import math
    import numpy as np

    dist = np.maximum(TOK - 1 - np.arange(LINE), 0)
    exact = REL_BUCKETS // 2
    large = exact + (np.log(np.maximum(dist, 1).astype(np.float32) / np.float32(exact))
                     / np.float32(math.log(REL_MAX_DIST / exact)) * np.float32(REL_BUCKETS - exact)).astype(np.int32)
    bucket = np.where(dist < exact, dist, np.minimum(large, REL_BUCKETS - 1))
    return {"bucket_onehot": (bucket[None, :] == np.arange(REL_BUCKETS)[:, None]).astype(np.float32)}


def kernel(**inputs):
    import numpy as np
    import concourse.bacc as bacc
    from concourse.bass_utils import run_bass_kernel_spmd

    nc = bacc.Bacc("TRN2", target_bir_lowering=False, num_devices=1)
    arrays, aps = {}, {}
    for name in _INS:
        arrays[f"in_{name}"] = np.ascontiguousarray(inputs[name])
        aps[name] = nc.dram_tensor(f"in_{name}", arrays[f"in_{name}"].shape, F32, kind="ExternalInput").ap()
    for name, value in _CONSTS().items():
        arrays[f"in_{name}"] = value
        aps[name] = nc.dram_tensor(f"in_{name}", value.shape, F32, kind="ExternalInput").ap()
    out = nc.dram_tensor("out", (1, TOK, D), F32, kind="ExternalOutput").ap()
    build_program(nc, aps, out)
    got = run_bass_kernel_spmd(nc, [arrays], core_ids=[0])
    return got.results[0]["out"]
```

```python
from contextlib import ExitStack

import concourse.bass as bass
from concourse import mybir

F32 = mybir.dt.float32
F32R = mybir.dt.float32r
I32 = mybir.dt.int32
I8 = mybir.dt.int8
ALU = mybir.AluOpType
ACT = mybir.ActivationFunctionType
KB = 1024

P = 128
TOK = 512
D = 1024
KT = D // P
TT = TOK // P
D_FF = 2816
FT = D_FF // P
EPS = 1e-6
GH, GDK, GDV, GRANK, GTAU = 4, 128, 256, 16, 16.0
GVT = GH * GDV // P
SH, SHD, SN, SG, TAPS = 16, 64, 128, 2, 4
SI = SH * SHD
XT = (SI + 2 * SG * SN) // P
HY_Q, HY_K, HY_V = 0, GH * GDK, 2 * GH * GDK
HY_R = HY_V + GH * GDV
HY_G = HY_R + GH * GDV
HY_Z = HY_G + GRANK
HY_XBC = HY_Z + SI
HY_DT = HY_XBC + XT * P
DT0 = 64
LEVELS = 7
AH, AL, AV, AQR = 16, 128, 64, 256
IH, IDIM, TOPK = 16, 64, min(256, TOK // 4)
REL_BUCKETS, REL_MAX_DIST = 32, 128
LINE = TOK + P
LAG = 3
MASKED, TAKEN = -1e30, -3e38

SLOTS = 4
UC = KT * P
PHASES = ((0, 8), (8, 8), (16, 6))
STAGES = ["ffn0", "mix0", "ffn1", "ffn2", "mix1", "ffn3"]


def build_program(nc, a, out):
    ctx = ExitStack()
    with ctx:
        def sb(name, shape, dt=F32):
            return ctx.enter_context(nc.sbuf_tensor(name, shape, dt))

        def sem(name):
            return ctx.enter_context(nc.semaphore(name))

        x = sb("x", [P, KT, TOK])
        H0 = nc.sbuf_base
        h_hi = sb("h_hi", [P, KT, TOK], F32R)
        h_lo = sb("h_lo", [P, KT, TOK], F32R)
        w_raw = sb("w_raw", [P, SLOTS, UC])
        w_hi = sb("w_hi", [P, SLOTS, UC], F32R)
        w_lo = sb("w_lo", [P, SLOTS, UC], F32R)
        ident = sb("ident", [P, P])
        ones = sb("ones", [P, P])
        sq = sb("sq", [P, 4, TOK])
        rs = sb("rs", [P, 4, 16])
        rb = sb("rb", [P, TOK])
        gains = sb("gains", [P, 176])
        pcols = sb("pcols", [P, 16])
        ps = ctx.enter_context(nc.psum_tensor("ps", [P, 8, 512], F32))
        ARENA = 99 * KB + 768
        sb("arena", [P, ARENA // 4])
        A0 = nc.sbuf_base - ARENA

        def at(name, shape, kb, dt=F32):
            return nc.alloc_sbuf_tensor_at(name, shape, dt, offset=A0 + int(kb * KB))
        act_hi = at("act_hi", [P, 8, TOK], 0, F32R)
        act_lo = at("act_lo", [P, 8, TOK], 16, F32R)
        sg = at("sg", [P, 2, TOK], 32)
        prod = at("prod", [P, 2, TOK], 36)
        x_in = at("x_in", [P, TT, D], 40)
        prow = at("prow", [P, 2, P], 56)
        ij = at("ij", [P, 4, P], 57, I32)
        gfin = at("gfin", [P, D], 60)
        otile = at("otile", [P, 2, D], 64)
        gq = at("gq", [P, GH, TOK], 0)
        gk = at("gk", [P, GH, TOK], 8)
        gv = at("gv", [P, TT, GH * GDV], 16)
        o_hi = at("o_hi", [P, KT, TOK], 0, F32R)
        o_lo = at("o_lo", [P, KT, TOK], 16, F32R)
        gb = at("gb", [P, GH, TOK], 32)
        gm = at("gm", [P, 2, GH, TOK], 40)
        gattn = at("gattn", [P, TT, GH, P], 56)
        gr = at("gr", [P, GVT, TOK], 64)
        gvT = at("gvT", [P, GVT, TOK], 80)
        small = at("small", [P, TOK], 96)
        masks = at("masks", [P, LEVELS + 1, P], 98, I8)
        tri = at("tri", [P, P], 99)
        gS = gm[:, 0, 0:2, :].rearrange("p a b -> p (a b)").rearrange("p (h v) -> p h v", h=GH)
        dt_tmp = gb[:, 0:3, :]
        gkd = gm[:, 1, :, :].rearrange("p c (h k) -> p c h k", h=GH)
        el = at("el", [P, GH, TT], 99.625)
        xbc = at("xbc", [P, XT, TOK], 0)
        sz = at("sz", [P, SI // P, TOK], 24)
        acb = at("acb", [P, 2, SH, P], 40)
        pm = at("pm", [P, 2, SH, P], 56)
        xdt = at("xdt", [P, SI], 72)
        xdtw = at("xdtw", [P, SI], 76)
        sB = at("sB", [P, SG, P], 80)
        cb = at("cb", [P, SG, P], 81)
        sS = at("sS", [P, SI], 82)
        y_hi = at("y_hi", [P, KT, TOK], 40, F32R)
        y_lo = at("y_lo", [P, KT, TOK], 56, F32R)
        xp = at("xp", [P, 2, TOK + 8], 86)
        toks = at("toks", [P, 2, TT, SH], 98)
        wtok = at("wtok", [P, 2, 2, SH], 98.5)
        acum_dram = nc.dram_tensor("acum_scratch", (SH, TOK), F32).ap()

        aT = at("aT", [P, AH, TOK], 64)
        aq = at("aq", [P, AH, TOK], 0)
        kvT = at("kvT", [P, TOK], 32)
        kvtok = at("kvtok", [P, TT, AL], 34)
        amask = at("amask", [P, TT, TOK], 36, F32R)
        kvr = at("kvr", [P, TOK], 36)
        kx = at("kx", [P, TOK], 38)
        kc = at("kc", [IDIM, TOK], 40)
        lp = at("lp", [P, 4, TOK], 44)
        qlr = at("qlr", [P, 2, TOK], 44)
        ql_hi = at("ql_hi", [P, 2, TOK], 48, F32R)
        ql_lo = at("ql_lo", [P, 2, TOK], 52, F32R)
        pt = at("pt", [P, 2, TOK], 52)
        olat = at("olat", [P, 2, TOK], 56)
        wuv = at("wuv", [P, AH, AV], 60)
        kn = at("kn", [P, TOK], 96)
        cneg = at("cneg", [P, P], 98)
        identr = at("identr", [P, P], 98.5, F32R)
        cmat = at("cmat", [IDIM, IDIM], 99)
        wtk = at("wtk", [P, TT, IH], 99.25)
        stat = at("stat", [P, 4, 8], 99.5)
        qix = nc.alloc_sbuf_tensor_at("qix", [P, KT, TOK], F32, offset=H0)
        ao = nc.alloc_sbuf_tensor_at("ao", [P, KT, TOK], F32, offset=H0)
        sc = nc.alloc_sbuf_tensor_at("sc", [P, TT - 1, TOK], F32, offset=H0 + 16 * KB)
        relb = at("relb", [REL_BUCKETS, AH], 72)
        hot = at("hot", [REL_BUCKETS, LINE], 73)
        line = at("line", [AH, LINE], 76)
        line_dram = nc.dram_tensor("line_scratch", (AH, P, LINE), F32).ap()

        NU = {"ffn": 2 * FT + 3 * KT, "mix0": 1 + 8 + 2 * GVT + KT + SI // P + XT + KT, "mix1": 18}
        NX = {"ffn": 3 * KT, "mix0": 2 * KT, "mix1": KT}
        UB, XB, un, xn = {}, {}, 0, KT
        for st in STAGES:
            UB[st], XB[st] = un, xn
            un += NU.get(st, NU["ffn"])
            xn += NX.get(st, NX["ffn"])
        NUNITS = un
        OPS, NORMS, XNORM = {}, {}, {}
        for st in STAGES:
            OPS[st] = 8 * len(OPS)
            NORMS[st] = len(NORMS)
            if st == "mix0":
                for e in ("gla", "ssd"):
                    OPS[e] = 8 * len(OPS)
                    NORMS[e] = len(NORMS)
            if st == "mix1":
                OPS["dsa"] = 8 * len(OPS)
            XNORM[st] = len(XNORM)
        NORMS["final"], XNORM["final"] = len(NORMS), len(XNORM)
        SS, acc_ss = {}, 0
        for st, z in NORMS.items():
            SS[z] = acc_ss
            acc_ss += 1 if st in XNORM else KT
        GATED = {"gla": 0, "ssd": KT}
        GAIN = {st: KT * int(st[3]) if st.startswith("ffn") else 32 + KT * int(st[3]) for st in STAGES}
        parts = [1] * NUNITS
        if "mix0" in UB:
            parts[UB["mix0"]] = 3
        if "mix1" in UB:
            parts[UB["mix1"] + 3] = 3
        LAND, acc = [], [0] * SLOTS
        for n in range(NUNITS):
            acc[n % SLOTS] += 16 * parts[n]
            LAND.append(acc[n % SLOTS])

        raw_landed = [sem(f"raw_landed{s}") for s in range(SLOTS)]
        hi_ready, lo_ready, unit_used = sem("hi_ready"), sem("lo_ready"), sem("unit_used")
        consts_ready, iota_ready, mask_steps = sem("consts_ready"), sem("iota_ready"), sem("mask_steps")
        x_landed, par_landed, gfin_landed = sem("x_landed"), sem("par_landed"), sem("gfin_landed")
        xt_done, par_done, gains_ready = sem("xt_done"), sem("par_done"), sem("gains_ready")
        x_upd = sem("x_upd")
        rb_ready, gate_scaled, up_scaled = sem("rb_ready"), sem("gate_scaled"), sem("up_scaled")
        r_silu, z_silu, z_out = sem("r_silu"), sem("z_silu"), sem("z_out")
        wg2_landed = sem("wg2_landed")
        silu_done, mul_done, ahi_done, alo_done = sem("silu_done"), sem("mul_done"), sem("ahi_done"), sem("alo_done")
        sq_ready, sq_added, ss_done = sem("sq_ready"), sem("sq_added"), sem("ss_done")
        rsq_steps, rstd_ready, bc_done = sem("rsq_steps"), sem("rstd_ready"), sem("bc_done")
        omul_done, ohi_done, opnd_ready = sem("omul_done"), sem("ohi_done"), sem("opnd_ready")
        fin_t, fin_ready = sem("fin_t"), sem("fin_ready")
        stored = [sem("stored_even"), sem("stored_odd")]
        tile_out = sem("tile_out")
        g_glr, g_gate_mm, g_gate_b, g_abs, g_scan = sem("g_glr"), sem("g_gate_mm"), sem("g_gate_b"), sem("g_abs"), sem("g_scan")
        g_diff, g_exp, g_mul, g_lvl, g_mask = sem("g_diff"), sem("g_exp"), sem("g_mul"), sem("g_lvl"), sem("g_mask")
        g_zero, g_vt, g_vev = sem("g_zero"), sem("g_vt"), sem("g_vev")
        g_dec, g_decm, g_kt, g_kev, g_o, g_oev, g_st, g_S = (sem(n) for n in (
            "g_dec", "g_decm", "g_kt", "g_kev", "g_o", "g_oev", "g_st", "g_S"))
        g_gated = sem("g_gated")
        s_dt, s_dta, s_acum, s_scr, s_tok, s_tokev = (sem(n) for n in ("s_dt", "s_dta", "s_acum", "s_scr", "s_tok", "s_tokev"))
        s_acb = [sem("s_acb_even"), sem("s_acb_odd")]
        s_conv, s_conved, s_silu, s_pad = sem("s_conv"), sem("s_conved"), sem("s_silu"), sem("s_pad")
        s_ea, s_pexp, s_wd, s_w, s_D, s_P, s_C = (sem(n) for n in ("s_ea", "s_pexp", "s_wd", "s_w", "s_D", "s_P", "s_C"))
        s_cb, s_cbm, s_tr, s_trB, s_Bev, s_xdt, s_xdtw = (sem(n) for n in ("s_cb", "s_cbm", "s_tr", "s_trB", "s_Bev", "s_xdt", "s_xdtw"))
        s_y, s_yev, s_st, s_S1, s_S2, s_gate = (sem(n) for n in ("s_y", "s_yev", "s_st", "s_S1", "s_S2", "s_gate"))

        l_landed, l_mm, l_ev, l_scr, t_landed = (sem(n) for n in ("l_landed", "l_mm", "l_ev", "l_scr", "t_landed"))
        uv_landed, a_cneg, a_const = sem("uv_landed"), sem("a_cneg"), sem("a_const")
        d_raw, d_kx, d_cen, d_kc, d_sq, d_ss, d_rs, d_bc = (sem("d_" + n) for n in ("raw", "kx", "cen", "kc", "sq", "ss", "rs", "bc"))
        d_mul, d_hi, d_ql, d_kv, d_kn, d_dup, d_tr, d_trev = (sem("d_" + n) for n in ("mul", "hi", "ql", "kv", "kn", "dup", "tr", "trev"))
        d_tile, d_ix, d_relu, d_acc = sem("d_tile"), sem("d_ix"), sem("d_relu"), sem("d_acc")
        a_log, a_max, a_exp, a_rec, a_nrm, a_tr, a_pt, a_pv, a_ol, a_uv, a_o = (sem("a_" + n) for n in (
            "log", "max", "exp", "rec", "nrm", "tr", "pt", "pv", "ol", "uv", "o"))
        k_top, k_mask, k_causal = sem("k_top"), sem("k_mask"), sem("k_causal")
        T1 = 25 + XT if "mix0" in STAGES else 0

        wg, wu, wd = a["ffn_w_gate"], a["ffn_w_up"], a["ffn_w_down"]
        w_in, w_out = a["hy_w_in"][0], a["hy_w_out"][0]
        GB_B, GB_N, GB_CB, GB_SN, GB_Q, GB_KV, GB_CW = 48, 52, 60, 72, 80, 82, 128

        block = ctx.enter_context(nc.Block())

        @block.sync
        def _(sp):
            def load(n, i, srcs):
                if n >= SLOTS or not isinstance(i, int):
                    sp.wait_ge(lo_ready, n - SLOTS + 1 + 4 * i)
                for dst, src in srcs:
                    sp.dma_start(dst, src).then_inc(raw_landed[n % SLOTS], 16)

            def slot(n, kt=KT, c=P):
                return w_raw[:, n % SLOTS, 0:kt * c].rearrange("p (k n) -> p k n", k=kt)

            def kp(w):
                return w.rearrange("(k p) n -> p k n", p=P)

            def columns(n, w, c0, tiles, kt=KT):
                with sp.Fori(0, tiles // 4) as i:
                    for j in range(4):
                        load(n + j, i, [(slot(n + j, kt), w[:, :, bass.ds(i * (4 * P) + (c0 + j * P), P)])])
                return n + tiles

            with nc.allow_non_contiguous_dma(reason="a few hundred parameters, one number each"):
                sp.dma_start(x_in[:, :, :], a["x"][0].rearrange("(t p) d -> p t d", p=P)).then_inc(x_landed, 16)
                rows = [(0, 0, a["ffn_norm_g"].rearrange("l a (k p) -> (l a k) p", p=P), 32),
                        (0, 32, a["mix_norm_g"].rearrange("l (k p) -> (l k) p", p=P), 16),
                        (0, GB_B, a["gla_b_gate"].rearrange("l (k p) -> (l k) p", p=P), 4),
                        (0, GB_N, a["gla_norm_g"].rearrange("l (k p) -> (l k) p", p=P), 8),
                        (0, GB_CB, a["ssd_conv_b"].rearrange("l (k p) -> (l k) p", p=P), 12),
                        (0, GB_SN, a["ssd_norm_g"].rearrange("l (k p) -> (l k) p", p=P), 8),
                        (0, GB_Q, a["dsa_q_norm_g"].rearrange("l (k p) -> (l k) p", p=P), 2),
                        (0, GB_KV, a["dsa_kv_norm_g"], 1),
                        (1, 0, a["ssd_conv_w"].rearrange("l w (k p) -> (l w k) p", p=P), 48)]
                for c, r, src, cnt in rows:
                    sp.dma_start(prow[r:r + cnt, c, :], src).then_inc(par_landed, 16)
                dv = a["ssd_d"].rearrange("l (t two) -> (l two) t", two=2)
                for h in range(2):
                    sp.dma_start(pcols[h * 64:(h + 1) * 64, 0:8], dv[h:h + 1, :].to_broadcast([64, 8])).then_inc(par_landed, 16)
                sp.dma_start(pcols[DT0:DT0 + SH, 8:9], a["ssd_dt_bias"].rearrange("l h -> h l")).then_inc(par_landed, 16)
                sp.dma_start(pcols[DT0:DT0 + SH, 9:10], a["ssd_a_log"].rearrange("l h -> h l")).then_inc(par_landed, 16)
                sp.dma_start(pcols[0:IDIM, 11:12], a["idx_ln_g"].rearrange("l h -> h l")).then_inc(par_landed, 16)
                sp.dma_start(pcols[0:IDIM, 12:13], a["idx_ln_b"].rearrange("l h -> h l")).then_inc(par_landed, 16)
                sp.dma_start(relb[:, :], a["rel_bias"]).then_inc(l_landed, 16)
                sp.dma_start(hot[:, :], a["bucket_onehot"]).then_inc(l_landed, 16)
            for st in STAGES:
                n = UB[st]
                if st.startswith("ffn"):
                    q = int(st[3])
                    g_src, u_src, d_src = (kp(w[q // 2, q % 2]) for w in (wg, wu, wd))
                    for f0, nf in PHASES:
                        first = n == 0
                        if first:
                            for j in range(4):
                                load(j, 0, [(slot(j), (g_src, u_src)[j % 2][:, :, (j // 2) * P:(j // 2 + 1) * P])])
                        with sp.Fori(1 if first else 0, nf // 2) as i:
                            for j in range(4):
                                src = (g_src, u_src)[j % 2]
                                load(n + j, i, [(slot(n + j), src[:, :, bass.ds(i * (2 * P) + (f0 + j // 2) * P, P)])])
                        n = columns(n + 2 * nf, d_src[:, f0:f0 + nf, :], 0, KT, nf)
                elif st == "mix0":
                    w = kp(w_in)
                    s0 = slot(n)
                    load(n, 0, [(s0[:, :, 0:64], w[:, :, HY_G:HY_G + 64]),
                                (s0[:, :, DT0:DT0 + SH], w[:, :, HY_DT:HY_DT + SH]),
                                (s0[:, :, DT0 + SH:P], w[:, :, HY_Z:HY_Z + P - DT0 - SH])])
                    n = columns(n + 1, w, HY_Q, 8 + 2 * GVT)
                    wo = kp(w_out)
                    n = columns(n, wo[:, 0:KT, :], 0, KT)
                    n = columns(n, w, HY_XBC, XT)
                    n = columns(n, w, HY_Z, SI // P)
                    n = columns(n, wo[:, KT:2 * KT, :], 0, KT)
                else:
                    dkv, iw, ww = kp(a["dsa_w_dkv"][0]), kp(a["idx_w_k"][0]), kp(a["idx_w_w"][0])
                    for j in range(2):
                        load(n + j, 0, [(slot(n + j), kp(a["dsa_w_dq"][0])[:, :, j * P:(j + 1) * P])])
                    load(n + 2, 0, [(slot(n + 2), dkv)])
                    s0 = slot(n + 3)
                    load(n + 3, 0, [(s0[:, :, 0:IDIM], iw), (s0[:, :, IDIM:IDIM + IH], ww), (s0[:, :, IDIM + IH:P], dkv[:, :, IDIM + IH:P])])
                    for j in range(2):
                        load(n + 4 + j, 0, [(slot(n + 4 + j, 2, 512), kp(a["idx_w_q"][0])[:, :, j * 512:(j + 1) * 512])])
                    for j in range(4):
                        load(n + 6 + j, 0, [(slot(n + 6 + j, 2, 512), kp(a["dsa_w_uq"][0])[:, :, j * 512:(j + 1) * 512])])
                    n = columns(n + 10, kp(a["dsa_w_o"][0]), 0, KT)
            sp.wait_ge(x_upd, xn)
            sp.dma_start(gfin[:, :], a["final_norm_g"].rearrange("(o n) -> o n", o=1).to_broadcast([P, D])).then_inc(gfin_landed, 16)
            for t in range(TT):
                sp.wait_ge(fin_ready, 2 * t + 2)
                sp.dma_start(out[0, t * P:(t + 1) * P, :], otile[:, t % 2, :]).then_inc(stored[t % 2], 16)
            sp.wait_ge(stored[0], 32)
            sp.wait_ge(stored[1], 32)

        @block.gpsimd
        def _(pool):
            pool.memset(ones[:, :], 1.0).then_inc(consts_ready, 1)
            pool.memset(ident[:, :], 0.0).then_inc(consts_ready, 1)
            pool.iota(ij[:, 0, :], pattern=[[1, P]], base=0, channel_multiplier=0).then_inc(iota_ready, 1)
            pool.iota(ij[:, 1, :], pattern=[[0, P]], base=0, channel_multiplier=1).then_inc(iota_ready, 1)
            pool.wait_ge(consts_ready, 2)
            pool.affine_select(out=ident[:, :], in_=ident[:, :], compare_op=ALU.not_equal, fill=1.0,
                               base=0, pattern=[[-1, P]], channel_multiplier=1).then_inc(consts_ready, 1)
            pool.wait_ge(l_ev, 2)
            pool.wait_ge(x_upd, 2 * KT)
            pool.dma_start(line_dram, line[:, :].rearrange("h (o c) -> h o c", o=1).to_broadcast([AH, P, LINE])).then_inc(l_scr, 16)
            if "mix0" in STAGES:
                pool.wait_ge(x_upd, XB["mix0"])
                pool.dma_start(small[0:GRANK, :], a["gla_w_gate2"][0]).then_inc(wg2_landed, 16)
                pool.memset(gattn[:, :, :, :], 0.0).then_inc(g_zero, 1)
                pool.wait_ge(s_acum, TT)
                pool.dma_start(acum_dram, dt_tmp[DT0:DT0 + SH, 2, :]).then_inc(s_scr, 16)
                pool.wait_ge(s_scr, 16)
                pool.wait_ge(x_upd, XB["mix0"] + KT)
                pool.memset(xp[:, :, 0:3], 0.0).then_inc(s_pad, 1)
                for c in range(TT):
                    if c >= 2:
                        pool.wait_ge(s_y, c - 1)
                    pool.dma_start(acb[:, c % 2, :, :],
                                   acum_dram[:, c * P:(c + 1) * P].rearrange("(o h) t -> o h t", o=1).to_broadcast([P, SH, P])
                                   ).then_inc(s_acb[c % 2], 16)

            if "mix1" in STAGES:
                pool.wait_ge(x_upd, XB["ffn1"] if "mix0" in STAGES else KT)
                pool.wait_ge(l_scr, 16)
                lines = bass.AP(tensor=line_dram.tensor, offset=P - 1, ap=[[LINE - 1, P], [P * LINE, AH], [1, TOK]])
                pool.dma_start(aT[:, :, :], lines).then_inc(t_landed, 16)
                pool.dma_start(wuv[:, :, :], a["dsa_w_uv"][0].rearrange("h c d -> c h d")).then_inc(uv_landed, 16)
                pool.memset(cneg[:, :], 0.0).then_inc(a_cneg, 1)
                pool.wait_ge(a_cneg, 1)
                pool.affine_select(out=cneg[:, :], in_=cneg[:, :], compare_op=ALU.is_ge, fill=MASKED,
                                   base=0, pattern=[[-1, P]], channel_multiplier=1).then_inc(a_cneg, 1)
                pool.wait_ge(d_kn, 2)
                pool.dma_start(kn[IDIM:2 * IDIM, :], kn[0:IDIM, :]).then_inc(d_dup, 16)
                for r in range(TT * AH):
                    w = P * (r // AH + 1)
                    pool.wait_ge(a_rec, r + 1)
                    pool.tensor_scalar(lp[:, r % 4, 0:w], lp[:, r % 4, 0:w], stat[:, 2, r % 4:r % 4 + 1], 1.0,
                                       ALU.mult, ALU.mult).then_inc(a_nrm, 1)

        @block.scalar
        def _(act):
            def produce_hi(n, i=0):
                if n >= NUNITS:
                    return
                s = n % SLOTS
                act.wait_ge(raw_landed[s], LAND[n] + 16 * i)
                if n >= SLOTS:
                    act.wait_ge(unit_used, n - SLOTS + 1 + 4 * i)
                act.activation(w_hi[:, s, :], w_raw[:, s, :], ACT.Copy).then_inc(hi_ready, 1)

            def square(z, op_before, m, src):
                if m >= 4:
                    act.wait_ge(ss_done, SS[z] + m - 3)
                elif op_before:
                    act.wait_ge(opnd_ready, op_before)
                act.activation(sq[:, m % 4, :], src, ACT.Square).then_inc(sq_ready, 1)

            def next_x(st, xc, m):
                act.wait_ge(x_upd, xc + m + 1)
                if st in GAIN:
                    act.activation(h_hi[:, m, :], x[:, m, :], ACT.Copy,
                                   scale=gains[:, GAIN[st] + m:GAIN[st] + m + 1]).then_inc(ohi_done, 1)
                if m >= 3:
                    act.wait_ge(sq_added, (KT - 1) * XNORM[st] + m - 2)
                act.activation(sq[:, m % 2 if m else 3, :], x[:, m, :], ACT.Square).then_inc(sq_ready, 1)

            def rms_out(st):
                act.wait_ge(bc_done, NORMS[st] + 1)
                act.activation(rb[:, :], ps[:, 3, :], ACT.Copy).then_inc(rb_ready, 1)

            def operand_hi(e, dst):
                for d in range(KT):
                    act.wait_ge(omul_done, GATED[e] + d + 1)
                    act.activation(dst[:, d, :], sq[:, d % 4, :], ACT.Copy).then_inc(ohi_done, 1)

            def ffn(st, nxt):
                n, fb = UB[st], FT * int(st[3])
                fb = FT * [s for s in STAGES if s.startswith("ffn")].index(st)
                for ph, (f0, nf) in enumerate(PHASES):
                    def pair(i):
                        for j in range(2):
                            produce_hi(n + 2 * j + SLOTS, i)
                            if ph == 0 and j == 0 and isinstance(i, int):
                                rms_out(st)
                            act.wait_ge(gate_scaled, fb + f0 + 2 * i + j + 2)
                            act.activation(sg[:, j, :], sg[:, j, :], ACT.Silu).then_inc(silu_done, 1)
                            produce_hi(n + 2 * j + 1 + SLOTS, i)
                    if ph == 0:
                        pair(0)
                    with act.Fori(ph == 0, nf // 2) as i:
                        pair(i)
                    n += 2 * nf
                    if ph < 2:
                        with act.Fori(0, 2) as i:
                            for j in range(4):
                                produce_hi(n + j + SLOTS, i)
                    else:
                        for m in range(KT):
                            produce_hi(n + m + SLOTS)
                            next_x(nxt, XB[st] + 2 * KT, m)
                    n += KT

            def mix0(nxt):
                n = UB["mix0"]
                produce_hi(n + SLOTS)
                rms_out("mix0")
                for t in range(1, 3):
                    produce_hi(n + t + SLOTS)
                act.wait_ge(g_gate_b, GH)
                g0, g1 = gm[:, 0, :, :], gm[:, 1, :, :]
                act.activation(g0, g1, ACT.Abs).then_inc(g_abs, 1)
                act.wait_ge(g_abs, 1)
                act.activation(g0, g0, ACT.Exp, scale=-1.0).then_inc(g_abs, 1)
                act.wait_ge(g_abs, 2)
                act.activation(g0, g0, ACT.Ln, bias=1.0).then_inc(g_abs, 1)
                for t in range(3, 9):
                    produce_hi(n + t + SLOTS)
                def r_gate(v):
                    produce_hi(n + 17 + v + SLOTS)
                    act.wait_ge(tile_out, 4 + 17 + v + 1)
                    act.activation(gr[:, v, :], gr[:, v, :], ACT.Silu).then_inc(r_silu, 1)
                for s in range(8):
                    produce_hi(n + 9 + s + SLOTS)
                    if s < LEVELS:
                        act.wait_ge(g_diff, 2 * (s + 1))
                        act.activation(gm[:, s % 2, :, :], gm[:, s % 2, :, :], ACT.Exp, scale=1.0 / GTAU).then_inc(g_exp, 1)
                act.wait_ge(g_lvl, TT * LEVELS)
                act.activation(gm[:, 0, :, :], gb[:, :, :], ACT.Exp, scale=1.0 / GTAU).then_inc(g_dec, 1)
                act.activation(el[:, :, :], gb[:, :, :].rearrange("p h (c t) -> p h c t", t=P)[:, :, :, P - 1], ACT.Exp,
                               scale=1.0 / GTAU).then_inc(g_dec, 1)
                act.wait_ge(g_decm, 1)
                act.activation(gm[:, 1, :, :], gm[:, 1, :, :], ACT.Exp, scale=1.0 / GTAU).then_inc(g_dec, 1)
                r_gate(0)
                r_gate(1)
                R = slice(DT0, DT0 + SH)
                act.wait_ge(s_dta, 1)
                act.activation(dt_tmp[R, 0, :], small[R, :], ACT.Abs).then_inc(s_dt, 1)
                act.wait_ge(s_dt, 1)
                act.activation(dt_tmp[R, 0, :], dt_tmp[R, 0, :], ACT.Exp, scale=-1.0).then_inc(s_dt, 1)
                act.wait_ge(s_dt, 2)
                act.activation(dt_tmp[R, 0, :], dt_tmp[R, 0, :], ACT.Ln, bias=1.0).then_inc(s_dt, 1)
                act.activation(pcols[R, 10:11], pcols[R, 9:10], ACT.Exp).then_inc(s_dt, 1)
                for c in range(TT):
                    act.wait_ge(g_o, c + 1)
                    if c == 0:
                        act.wait_ge(g_vt, GVT)
                    for b in range(2):
                        act.activation(gvT[:, 4 * b:4 * b + 4, c * P:(c + 1) * P],
                                       ps[:, 2 + b, :].rearrange("p (m t) -> p m t", m=4), ACT.Copy).then_inc(g_oev, 1)
                    if c < TT - 1:
                        r_gate(2 + c)
                for m in range(GVT):
                    if m == 0:
                        act.wait_ge(g_oev, 2 * TT)
                    if m == 4:
                        r_gate(5)
                        r_gate(6)
                    square(NORMS["gla"], OPS["gla"], m, gvT[:, m, :])
                r_gate(7)
                operand_hi("gla", o_hi)
                n0 = UB["mix0"] + 25
                with act.Fori(0, 2) as i:
                    for j in range(4):
                        produce_hi(n0 + j + SLOTS, i)
                n0 += KT

                def conv_silu(m):
                    act.wait_ge(s_conved, m + 1)
                    act.activation(xbc[:, m, :], sq[:, m % 2, :], ACT.Silu).then_inc(s_silu, 1)
                for m in range(XT):
                    produce_hi(n0 + m + SLOTS)
                    if m:
                        conv_silu(m - 1)
                n0 += XT

                def decays(c):
                    ab, wt = acb[:, c % 2, :, :], wtok[:, c % 2, :, :]
                    act.wait_ge(s_D, c + 1)
                    act.activation(pm[:, c % 2, :, :], pm[:, c % 2, :, :], ACT.Exp).then_inc(s_pexp, 1)
                    act.wait_ge(s_wd, c + 1)
                    act.activation(wt[:, 0, :], wt[:, 0, :], ACT.Exp).then_inc(s_w, 1)
                    act.activation(wt[:, 1, :], ab[:, :, P - 1], ACT.Exp).then_inc(s_ea, 1)
                    act.wait_ge(s_ea, 2 * c + 1)
                    act.activation(ab, ab, ACT.Exp).then_inc(s_ea, 1)

                def z_gate(m):
                    act.wait_ge(z_out, m + 1)
                    act.activation(sz[:, m, :], sz[:, m, :], ACT.Silu).then_inc(z_silu, 1)
                conv_silu(XT - 1)
                decays(0)
                produce_hi(n0 + SLOTS)
                z_gate(0)
                for c in range(TT):
                    produce_hi(n0 + 2 * c + 1 + SLOTS)
                    if c < TT - 1:
                        decays(c + 1)
                        produce_hi(n0 + 2 * c + 2 + SLOTS)
                    z_gate(2 * c + 1)
                    if c < TT - 1:
                        z_gate(2 * c + 2)
                for m in range(KT):
                    act.wait_ge(s_gate, m + 1)
                    square(NORMS["ssd"], OPS["ssd"], m, xbc[:, m, :])
                operand_hi("ssd", y_hi)
                n0 = UB["mix0"] + NU["mix0"] - KT
                for m in range(KT):
                    produce_hi(n0 + m + SLOTS)
                    next_x(nxt, XB["mix0"] + KT, m)

            def mix1(nxt):
                n = UB["mix1"]
                produce_hi(n + SLOTS)
                rms_out("mix1")
                for t in range(1, 4):
                    produce_hi(n + t + SLOTS)
                    act.wait_ge(tile_out, 4 + T1 + t)
                    act.activation(sq[:, t - 1, :], qlr[:, t - 1, :] if t < 3 else kvr[:, :], ACT.Square).then_inc(d_raw, 1)
                act.wait_ge(d_cen, 1)
                act.activation(sq[0:IDIM, 3, :], ps[0:IDIM, 0, :], ACT.Square).then_inc(d_sq, 1)
                act.activation(kc[:, :], ps[0:IDIM, 0, :], ACT.Copy).then_inc(d_kc, 1)
                for d in range(2):
                    act.wait_ge(d_mul, d + 1)
                    act.activation(ql_hi[:, d, :], sq[:, d, :], ACT.Copy).then_inc(d_hi, 1)
                act.wait_ge(d_tr, 1)
                act.activation(wtk[:, :, :], ps[:, 2, 0:TT * IH].rearrange("p (c h) -> p c h", c=TT), ACT.Copy).then_inc(d_trev, 1)
                act.wait_ge(d_tr, 2)
                act.activation(kvtok[:, :, :], ps[:, 0, :].rearrange("p (c d) -> p c d", c=TT), ACT.Copy).then_inc(d_trev, 1)
                for t in range(KT + AH):
                    if t % 4 == 3:
                        act.wait_ge(unit_used, n + 4 + t // 4 + 1)
                    else:
                        act.wait_ge(d_tile, 3 * (t // 4) + t % 4 + 1)
                    dst = qix[:, t, :] if t < KT else aq[:, t - KT, :]
                    act.activation(dst, ps[:, 4 + (T1 + t) % 4, :], ACT.Copy,
                                   scale=1.0 if t < KT else float(AL) ** -0.5).then_inc(tile_out, 1)
                    if t % 4 == 3:
                        produce_hi(n + 4 + t // 4 + SLOTS)
                for r in range((TT - 1) * IH):
                    w = P * (r // IH + 2)
                    act.wait_ge(d_ix, r + 1)
                    if r >= 4:
                        act.wait_ge(d_acc, r - 3)
                    act.activation(sq[:, r % 4, 0:w], ps[:, r % 4, 0:w], ACT.Relu).then_inc(d_relu, 1)
                NR = TT * AH

                def p_out(r):
                    w = P * (r // AH + 1)
                    act.wait_ge(a_tr, r + 1)
                    if r >= 2:
                        act.wait_ge(a_pv, r - 1)
                    act.activation(pt[:, r % 2, 0:w], ps[:, 2 + r % 2, 0:w], ACT.Copy).then_inc(a_pt, 1)

                def latent_out(g):
                    act.wait_ge(a_pv, 4 * g + 4)
                    if g >= 2:
                        act.wait_ge(a_uv, g - 1)
                    act.activation(olat[:, g % 2, :], ps[:, 4 + g % 2, :], ACT.Copy).then_inc(a_ol, 1)

                def values_out(g):
                    act.wait_ge(a_uv, g + 1)
                    b, half = g // 4, (g % 4) // 2
                    act.activation(ao[:, 4 * half:4 * half + 4, b * P:(b + 1) * P],
                                   ps[:, 6 + half, :].rearrange("p (m t) -> p m t", m=4), ACT.Copy).then_inc(a_o, 1)
                for r in range(NR + LAG + 4):
                    if r < NR:
                        w = P * (r // AH + 1)
                        act.wait_ge(a_max, r + 1)
                        if r >= 4:
                            act.wait_ge(a_rec, r - 3)
                        act.activation(lp[:, r % 4, 0:w], lp[:, r % 4, 0:w], ACT.Exp, scale=-1.0, bias=stat[:, 0, r % 4:r % 4 + 1],
                                       accum_out=stat[:, 1, r % 4:r % 4 + 1]).then_inc(a_exp, 1)
                    if LAG <= r < NR + LAG:
                        p_out(r - LAG)
                    if r >= LAG + 2 and (r - LAG - 2) % 4 == 3 and (r - LAG - 2) // 4 < NR // 4:
                        latent_out((r - LAG - 2) // 4)
                    if r >= LAG + 3 and (r - LAG - 3) % 8 == 7 and (r - LAG - 3) // 4 < NR // 4:
                        values_out((r - LAG - 3) // 4)
                for d in range(KT):
                    if d == 0:
                        act.wait_ge(a_o, 2 * TT)
                    act.activation(o_hi[:, d, :], ao[:, d, :], ACT.Copy).then_inc(ohi_done, 1)
                n0 = n + NU["mix1"] - KT
                for m in range(KT):
                    produce_hi(n0 + m + SLOTS)
                    next_x(nxt, XB["mix1"], m)

            act.wait_ge(l_mm, 1)
            act.activation(line[:, 0:TOK], ps[0:AH, 2, :], ACT.Copy).then_inc(l_ev, 1)
            act.activation(line[:, TOK:LINE], ps[0:AH, 3, 0:P], ACT.Copy).then_inc(l_ev, 1)
            act.wait_ge(gains_ready, 2)
            produce_hi(0)
            for m in range(KT):
                next_x(STAGES[0], 0, m)
                if m in (2, 4, 6):
                    produce_hi(m // 2)
            for k, st in enumerate(STAGES):
                nxt = (STAGES + ["final"])[k + 1]
                if st.startswith("ffn"):
                    ffn(st, nxt)
                elif st == "mix0":
                    mix0(nxt)
                else:
                    mix1(nxt)

        @block.vector
        def _(dve):
            def produce_lo(n, i=0):
                if n >= NUNITS:
                    return
                s = n % SLOTS
                dve.wait_ge(hi_ready, n + 1 + 4 * i)
                dve.tensor_tensor(w_lo[:, s, :], w_raw[:, s, :], w_hi[:, s, :].bitcast(F32),
                                  ALU.subtract).then_inc(lo_ready, 1)

            steps = [0]

            def step(ins):
                steps[0] += 1
                ins.then_inc(rsq_steps, 1)
                dve.wait_ge(rsq_steps, steps[0])

            def newton(val, y, t):
                step(dve.tensor_scalar(t.bitcast(I32), val.bitcast(I32), 1, None, ALU.logical_shift_right))
                step(dve.tensor_scalar(y.bitcast(I32), t.bitcast(I32), -1.0, float(0x5f3759df), ALU.mult, ALU.add))
                for r in range(3):
                    step(dve.scalar_tensor_tensor(out=t, in0=y, scalar=-0.5, in1=y, op0=ALU.mult, op1=ALU.mult))
                    step(dve.tensor_tensor(t, t, val, ALU.mult))
                    last = dve.scalar_tensor_tensor(out=y, in0=t, scalar=1.5, in1=y, op0=ALU.add, op1=ALU.mult)
                    if r < 2:
                        step(last)
                return last

            def rsqrt(z, c, scale):
                dve.wait_ge(ss_done, SS[z] + (KT if z in (NORMS.get("gla"), NORMS.get("ssd")) else 1))
                if z:
                    dve.wait_ge(bc_done, z)
                val, y, t = rs[:, 0, 0:c], rs[:, 1, 0:c], rs[:, 2, 0:c]
                step(dve.tensor_scalar(val, ps[:, 2, 0:c], scale, EPS, ALU.mult, ALU.add))
                newton(val, y, t).then_inc(rstd_ready, 1)

            def next_low(st, m):
                if st in GAIN:
                    dve.wait_ge(ohi_done, OPS[st] + m + 1)
                    dve.scalar_tensor_tensor(out=h_lo[:, m, :], in0=x[:, m, :], scalar=gains[:, GAIN[st] + m:GAIN[st] + m + 1],
                                             in1=h_hi[:, m, :].bitcast(F32), op0=ALU.mult, op1=ALU.subtract).then_inc(opnd_ready, 1)

            def add_square(st, m):
                if m:
                    dve.wait_ge(sq_ready, KT * NORMS[st] + m + 1)
                    if m > 1:
                        dve.wait_ge(sq_added, (KT - 1) * XNORM[st] + m - 1)
                    dve.tensor_tensor(sq[:, 3, :], sq[:, 3, :], sq[:, m % 2, :], ALU.add).then_inc(sq_added, 1)

            def last_updates(xc, n, scale, nxt):
                for m in range(KT):
                    add_x(xc, n, m // 4, m % 4, scale)
                    if m:
                        next_low(nxt, m - 1)
                        add_square(nxt, m - 1)
                    if m < KT - 1:
                        produce_lo(n + m + SLOTS)
                next_low(nxt, KT - 1)
                add_square(nxt, KT - 1)
                produce_lo(n + KT - 1 + SLOTS)
                rsqrt(NORMS[nxt], TT, 1.0 / D)

            def operand(z, o, src, g0, bank, hi, lo):
                dve.wait_ge(bc_done, z + 1)

                def low(d):
                    dve.wait_ge(ohi_done, o + d + 1)
                    dve.tensor_tensor(lo[:, d, :], sq[:, d % 4, :], hi[:, d, :].bitcast(F32),
                                      ALU.subtract).then_inc(opnd_ready, 1)
                for d in range(KT):
                    if d >= 4:
                        dve.wait_ge(opnd_ready, o + d - 3)
                    if g0 is None:
                        ins = dve.tensor_tensor(sq[:, d % 4, :], src[:, d, :], ps[:, bank(d), :], ALU.mult)
                    else:
                        ins = dve.scalar_tensor_tensor(out=sq[:, d % 4, :], in0=src[:, d, :], scalar=gains[:, g0 + d:g0 + d + 1],
                                                       in1=ps[:, bank(d), :], op0=ALU.mult, op1=ALU.mult)
                    ins.then_inc(omul_done, 1)
                    if d:
                        low(d - 1)
                low(KT - 1)

            def add_x(xc, n, i, j, scale):
                dve.wait_ge(unit_used, n + 1 + j + 4 * i)
                dve.wait_ge(x_upd, xc)
                xt = x[:, bass.ds(4 * i + j, 1), :] if not isinstance(i, int) else x[:, 4 * i + j:4 * i + j + 1, :]
                dve.scalar_tensor_tensor(out=xt, in0=ps[:, 4 + j:5 + j, :], scalar=scale, in1=xt,
                                         op0=ALU.mult, op1=ALU.add).then_inc(x_upd, 1)

            def ffn(st, nxt):
                n = UB[st]
                fb = FT * [s for s in STAGES if s.startswith("ffn")].index(st)
                xc = XB[st]
                for ph, (f0, nf) in enumerate(PHASES):
                    f = fb + f0

                    def pair(i):
                        for j in range(2):
                            produce_lo(n + 2 * j + SLOTS, i)
                            if ph == 0 and j == 0 and isinstance(i, int):
                                dve.wait_ge(rb_ready, XNORM[st] + 1)
                            dve.wait_ge(unit_used, n + 4 * i + 2 * j + 1)
                            dve.wait_ge(mul_done, f + 2 * i + 1)
                            dve.tensor_tensor(sg[:, j, :], ps[:, 2 * j, :], rb[:, :], ALU.mult).then_inc(gate_scaled, 1)
                            dve.wait_ge(unit_used, n + 4 * i + 2 * j + 2)
                            dve.wait_ge(alo_done, f + 2 * i + 1)
                            dve.tensor_tensor(prod[:, j, :], ps[:, 2 * j + 1, :], rb[:, :], ALU.mult).then_inc(up_scaled, 1)
                            dve.wait_ge(up_scaled, f + 2 * i + j + 1)
                            dve.wait_ge(silu_done, f + 2 * i + j + 2)
                            dve.tensor_tensor(prod[:, j, :], sg[:, j, :], prod[:, j, :], ALU.mult).then_inc(mul_done, 1)
                            dve.wait_ge(mul_done, f + 2 * i + j + 2)
                            dve.tensor_copy(act_hi[:, bass.ds(2 * i + j, 1), :], prod[:, j:j + 1, :]).then_inc(ahi_done, 1)
                            dve.wait_ge(ahi_done, f + 2 * i + j + 1)
                            dve.tensor_tensor(act_lo[:, bass.ds(2 * i + j, 1), :], prod[:, j:j + 1, :],
                                              act_hi[:, bass.ds(2 * i + j, 1), :].bitcast(F32), ALU.subtract).then_inc(alo_done, 1)
                            produce_lo(n + 2 * j + 1 + SLOTS, i)
                    if ph == 0:
                        pair(0)
                    with dve.Fori(ph == 0, nf // 2) as i:
                        pair(i)
                    n += 2 * nf
                    if ph < 2:
                        with dve.Fori(0, 2) as i:
                            for j in range(4):
                                add_x(xc, n, i, j, 0.5)
                                produce_lo(n + j + SLOTS, i)
                    else:
                        last_updates(xc, n, 0.5, nxt)
                    n += KT
                    xc += KT

            def mix0(nxt):
                n = UB["mix0"]

                def tile(t, dst, scale=None):
                    u = n + t + (KT if t >= 25 else 0)
                    dve.wait_ge(unit_used, u + 1)
                    src = ps[0:dst.shape[0], 4 + t % 4, :]
                    if scale is None:
                        dve.tensor_tensor(dst, src, rb[0:dst.shape[0], :], ALU.mult).then_inc(tile_out, 1)
                    else:
                        dve.scalar_tensor_tensor(out=dst, in0=src, scalar=scale, in1=rb[:, :], op0=ALU.mult,
                                                 op1=ALU.mult).then_inc(tile_out, 1)
                R = slice(DT0, DT0 + SH)
                produce_lo(n + SLOTS)
                dve.wait_ge(rb_ready, XNORM["mix0"] + 1)
                dve.wait_ge(unit_used, n + 1)
                dve.tensor_tensor(sq[0:GRANK, 0, :], ps[0:GRANK, 4, :], rb[0:GRANK, :], ALU.mult).then_inc(g_glr, 1)
                dve.tensor_tensor(small[R, :], ps[R, 4, :], rb[R, :], ALU.mult).then_inc(tile_out, 1)

                def gate_sums():
                    g1 = gm[:, 1, :, :]
                    dve.wait_ge(g_abs, 3)
                    dve.scalar_tensor_tensor(out=g1, in0=g1, scalar=0.0, in1=gm[:, 0, :, :], op0=ALU.min,
                                             op1=ALU.subtract).then_inc(g_scan, 1)
                    dve.wait_ge(g_scan, 1)
                    for h in range(GH):
                        for c in range(TT):
                            dve.tensor_tensor_scan(gb[:, h, c * P:(c + 1) * P], ones[:, :], gm[:, 1, h, c * P:(c + 1) * P], 0.0,
                                                   ALU.mult, ALU.add).then_inc(g_scan, 1)
                for t in range(1, 9):
                    if t == 5:
                        gate_sums()
                    produce_lo(n + t + SLOTS)
                    tile(t, gq[:, t - 1, :] if t < 5 else gk[:, t - 5, :], float(GDK) ** -0.5 if t < 5 else None)
                    if t == 1:
                        for h in range(GH):
                            dve.wait_ge(g_gate_mm, h + 1)
                            dve.tensor_scalar(gm[:, 1, h, :], ps[:, h, :], gains[:, GB_B + h:GB_B + h + 1], None,
                                              ALU.add).then_inc(g_gate_b, 1)
                dve.wait_ge(g_scan, 1 + GH * TT)

                def level(m, s):
                    return m.rearrange("p h t -> p (h t)").rearrange("p (n two s) -> p n two s", two=2, s=s)

                def diff(l):
                    s = 1 << (LEVELS - 1 - l)
                    b4, m4 = level(gb[:, :, :], s), level(gm[:, l % 2, :, :], s)
                    ref = b4[:, :, 0, s - 1:s].to_broadcast([P, GH * TOK // (2 * s), s])
                    if l >= 2:
                        dve.wait_ge(g_lvl, TT * (l - 1))
                    dve.tensor_tensor(m4[:, :, 0, :], ref, b4[:, :, 0, :], ALU.subtract).then_inc(g_diff, 1)
                    dve.tensor_tensor(m4[:, :, 1, :], b4[:, :, 1, :], ref, ALU.subtract).then_inc(g_diff, 1)

                def mult(l):
                    s = 1 << (LEVELS - 1 - l)
                    m4 = level(gm[:, l % 2, :, :], s)
                    dve.wait_ge(g_exp, l + 1)
                    dve.tensor_tensor(m4[:, :, 0, :], m4[:, :, 0, :], level(gk[:, :, :], s)[:, :, 0, :], ALU.mult).then_inc(g_mul, 1)
                    dve.tensor_tensor(m4[:, :, 1, :], m4[:, :, 1, :], level(gq[:, :, :], s)[:, :, 1, :], ALU.mult).then_inc(g_mul, 1)

                def masked(l):
                    for c in range(TT):
                        dve.wait_ge(g_lvl, TT * l + c + 1)
                        if l:
                            dve.wait_ge(g_mask, TT * (l - 1) + c + 1)
                        dve.copy_predicated(gattn[:, c, :, :], masks[:, l:l + 1, :].to_broadcast([P, GH, P]),
                                            ps[:, c, :].rearrange("p (h t) -> p h t", h=GH)).then_inc(g_mask, 1)

                def v_out(v):
                    dve.wait_ge(g_vt, v + 1)
                    dve.tensor_copy(gv[:, :, v * P:(v + 1) * P], ps[:, 4 + (9 + 4 + v // 2 + 1 + v % 2) % 4, :].rearrange("p (c d) -> p c d", c=TT)).then_inc(g_vev, 1)
                dve.wait_ge(g_zero, 1)
                def r_tile(v):
                    produce_lo(n + 17 + v + SLOTS)
                    tile(17 + v, gr[:, v, :])
                for s in range(8):
                    if s < LEVELS:
                        diff(s)
                    produce_lo(n + 9 + s + SLOTS)
                    tile(9 + s, gvT[:, s, :])
                    if s >= 4:
                        v_out(2 * (s - 4))
                        v_out(2 * (s - 4) + 1)
                    if s < LEVELS:
                        mult(s)
                    if s:
                        masked(s - 1)
                dve.wait_ge(g_mul, 2 * LEVELS)
                b3 = gb[:, :, :].rearrange("p h (c t) -> p (h c) t", t=P)
                m3 = gm[:, 1, :, :].rearrange("p h (c t) -> p (h c) t", t=P)
                dve.wait_ge(g_lvl, TT * LEVELS)
                dve.tensor_tensor(m3, b3[:, :, P - 1:P].to_broadcast([P, GH * TT, P]), b3, ALU.subtract).then_inc(g_decm, 1)
                r_tile(0)
                masked(LEVELS)
                dve.wait_ge(g_dec, 1)
                dve.tensor_tensor(gq[:, :, :], gq[:, :, :], gm[:, 0, :, :], ALU.mult).then_inc(g_decm, 1)
                r_tile(1)
                dve.wait_ge(g_dec, 3)
                dve.tensor_tensor(gk[:, :, :], gk[:, :, :], gm[:, 1, :, :], ALU.mult).then_inc(g_decm, 1)
                dve.wait_ge(g_decm, 3)
                for c in range(TT):
                    dve.wait_ge(g_kt, c + 1)
                    dve.tensor_copy(gkd[:, c, :, :], ps[:, c, :].rearrange("p (h k) -> p h k", h=GH)).then_inc(g_kev, 1)
                dve.wait_ge(tile_out, 5)
                dve.tensor_scalar(small[R, :], small[R, :], pcols[R, 8:9], None, ALU.add).then_inc(s_dta, 1)
                def dt_sums():
                    dve.wait_ge(s_dt, 4)
                    dve.scalar_tensor_tensor(out=small[R, :], in0=small[R, :], scalar=0.0, in1=dt_tmp[R, 0, :],
                                             op0=ALU.max, op1=ALU.add).then_inc(s_dta, 1)
                    dve.wait_ge(s_dta, 2)
                    dve.tensor_scalar(dt_tmp[R, 1, :], small[R, :], pcols[R, 10:11], -1.0, ALU.mult, ALU.mult).then_inc(s_dta, 1)
                    dve.wait_ge(s_dta, 3)
                    for c in range(TT):
                        dve.tensor_tensor_scan(dt_tmp[R, 2, c * P:(c + 1) * P], ones[R, :], dt_tmp[R, 1, c * P:(c + 1) * P], 0.0,
                                               ALU.mult, ALU.add).then_inc(s_acum, 1)
                for c in range(TT - 1):
                    for h in range(GH):
                        dve.wait_ge(g_st, GH * c + 2 * (h // 2) + 2)
                        src = ps[:, h // 2, (h % 2) * GDV:(h % 2 + 1) * GDV]
                        if c == 0:
                            dve.tensor_copy(gS[:, h, :], src).then_inc(g_S, 1)
                        else:
                            dve.wait_ge(g_o, c + 1)
                            dve.wait_ge(g_S, GH * (c - 1) + h + 1)
                            dve.scalar_tensor_tensor(out=gS[:, h, :], in0=gS[:, h, :], scalar=el[:, h, c:c + 1], in1=src,
                                                     op0=ALU.mult, op1=ALU.add).then_inc(g_S, 1)
                    if c == 0:
                        dt_sums()
                    r_tile(2 + c)
                dve.wait_ge(s_tok, 1)
                dve.tensor_copy(toks[:, :, :, :], ps[:, 0, 0:2 * TT * SH].rearrange("p (a c h) -> p a c h", a=2, c=TT)).then_inc(s_tokev, 1)
                r_tile(5)
                r_tile(6)
                z = NORMS["gla"]

                def gated(m):
                    dve.wait_ge(sq_ready, KT * z + m + 1)
                    dve.wait_ge(r_silu, m + 1)
                    dve.scalar_tensor_tensor(out=gvT[:, m, :], in0=gvT[:, m, :], scalar=gains[:, GB_N + m:GB_N + m + 1],
                                             in1=gr[:, m, :], op0=ALU.mult, op1=ALU.mult).then_inc(g_gated, 1)
                for m in range(4):
                    gated(m)
                rsqrt(z, GH * TT, 1.0 / GDV)
                for m in range(4, GVT - 1):
                    gated(m)
                r_tile(7)
                gated(GVT - 1)
                dve.wait_ge(g_gated, GVT)
                operand(z, OPS["gla"], gvT, None, lambda d: d // 2, o_hi, o_lo)
                n0 = n + 25
                with dve.Fori(0, 2) as i:
                    for j in range(4):
                        add_x(XB["mix0"], n0, i, j, 1.0)
                        produce_lo(n0 + j + SLOTS, i)
                n0 += KT
                taps = [0]
                dve.wait_ge(s_pad, 1)
                for m in range(XT):
                    produce_lo(n0 + m + SLOTS)
                    if m >= 2:
                        dve.wait_ge(s_silu, m - 1)
                    tile(25 + m, xp[:, m % 2, 3:3 + TOK])
                    dve.wait_ge(tile_out, 4 + 25 + m + 1)
                    cv = sq[:, m % 2, :]
                    dve.tensor_scalar(cv, xp[:, m % 2, 0:TOK], gains[:, GB_CW + m:GB_CW + m + 1],
                                      gains[:, GB_CB + m:GB_CB + m + 1], ALU.mult, ALU.add).then_inc(s_conv, 1)
                    for k in range(1, TAPS):
                        taps[0] += 1
                        dve.wait_ge(s_conv, taps[0])
                        dve.scalar_tensor_tensor(out=cv, in0=xp[:, m % 2, k:k + TOK],
                                                 scalar=gains[:, GB_CW + XT * k + m:GB_CW + XT * k + m + 1],
                                                 in1=cv, op0=ALU.mult, op1=ALU.add).then_inc(s_conv if k < TAPS - 1 else s_conved, 1)
                n0 += XT
                acum_tok, dt_tok = toks[:, 1, :, :], toks[:, 0, :, :]
                hg = SH // SG

                def by_head(t):
                    return t.rearrange("p (h d) -> p h d", h=SH)

                def over_width(w):
                    return w.rearrange("p (h o) -> p h o", o=1).to_broadcast([P, SH, SHD])

                def gaps(c):
                    dve.wait_ge(s_acb[c % 2], 16 * (c // 2 + 1))
                    ab = acb[:, c % 2, :, :]
                    for h in range(SH):
                        ins = dve.tensor_scalar(pm[:, c % 2, h, :], ab[:, h, :], acum_tok[:, c, h:h + 1], 0.0, ALU.subtract, ALU.min)
                    ins.then_inc(s_D, 1)
                    dve.tensor_tensor(wtok[:, c % 2, 0, :], ab[:, :, P - 1], acum_tok[:, c, :], ALU.subtract).then_inc(s_wd, 1)

                def from_start(c):
                    dve.wait_ge(s_ea, 2 * c + 2)
                    for g in range(SG):
                        ce = acb[:, c % 2, g * hg:(g + 1) * hg, :]
                        dve.tensor_tensor(ce, ce, xbc[:, 10 + g:11 + g, c * P:(c + 1) * P].to_broadcast([P, hg, P]), ALU.mult).then_inc(s_C, 1)

                def z_tile(m):
                    produce_lo(n0 + m + SLOTS)
                    dve.wait_ge(unit_used, n0 + m + 1)
                    dve.tensor_tensor(sz[:, m, :], ps[:, 1, :], rb[:, :], ALU.mult).then_inc(z_out, 1)
                gaps(0)
                z_tile(0)
                dve.wait_ge(s_silu, XT)
                from_start(0)
                for c in range(TT):
                    wt, pmc = wtok[:, c % 2, :, :], pm[:, c % 2, :, :]
                    dve.wait_ge(s_trB, c + 1)
                    dve.tensor_tensor(cb[:, :, :], ps[:, 0, 0:SG * P].rearrange("p (g t) -> p g t", g=SG),
                                      tri[:, :].rearrange("p (o t) -> p o t", o=1).to_broadcast([P, SG, P]), ALU.mult).then_inc(s_cbm, 1)
                    if c < TT - 1:
                        dve.tensor_copy(sB[:, :, :], ps[:, 0, SG * P:2 * SG * P].rearrange("p (g n) -> p g n", g=SG)).then_inc(s_Bev, 1)
                    dve.wait_ge(s_tr, c + 1)
                    dve.tensor_tensor(by_head(xdt[:, :]), ps[:, 2:4, :].rearrange("p b (h d) -> p (b h) d", d=SHD),
                                      over_width(dt_tok[:, c, :]), ALU.mult).then_inc(s_xdt, 1)
                    dve.wait_ge(s_w, c + 1)
                    dve.wait_ge(s_xdt, c + 1)
                    if c < TT - 1:
                        dve.tensor_tensor(by_head(xdtw[:, :]), by_head(xdt[:, :]), over_width(wt[:, 0, :]), ALU.mult).then_inc(s_xdtw, 1)
                    dve.wait_ge(s_pexp, c + 1)
                    dve.wait_ge(s_cbm, c + 1)
                    for g in range(SG):
                        dve.tensor_tensor(pmc[:, g * hg:(g + 1) * hg, :], pmc[:, g * hg:(g + 1) * hg, :],
                                          cb[:, g:g + 1, :].to_broadcast([P, hg, P]), ALU.mult).then_inc(s_P, 1)
                    z_tile(2 * c + 1)
                    if c < TT - 1:
                        gaps(c + 1)
                    dve.wait_ge(s_y, c + 1)
                    if c < TT - 1:
                        if c:
                            dve.tensor_tensor(by_head(sS[:, :]), by_head(sS[:, :]), over_width(wt[:, 1, :]), ALU.mult).then_inc(s_S1, 1)
                        dve.wait_ge(s_st, c + 1)
                        new = ps[:, 2:4, :].rearrange("p b t -> p (b t)")
                        if c:
                            dve.wait_ge(s_S1, c)
                            dve.tensor_tensor(sS[:, :], sS[:, :], new, ALU.add).then_inc(s_S2, 1)
                        else:
                            dve.tensor_copy(sS[:, :], new).then_inc(s_S2, 1)
                        z_tile(2 * c + 2)
                        from_start(c + 1)
                    for m in range(SI // P):
                        xt = xbc[:, m, c * P:(c + 1) * P]
                        ins = dve.scalar_tensor_tensor(out=xt, in0=xt, scalar=pcols[:, m:m + 1],
                                                       in1=ps[:, 4 + 2 * (c % 2) + m // 4, (m % 4) * P:(m % 4 + 1) * P],
                                                       op0=ALU.mult, op1=ALU.add)
                    ins.then_inc(s_yev, 1)
                dve.wait_ge(s_yev, TT)
                dve.wait_ge(z_silu, SI // P)
                for m in range(SI // P):
                    dve.tensor_tensor(xbc[:, m, :], xbc[:, m, :], sz[:, m, :], ALU.mult).then_inc(s_gate, 1)
                z = NORMS["ssd"]
                rsqrt(z, SG * TT, 1.0 / (SI // SG))
                operand(z, OPS["ssd"], xbc, GB_SN, lambda d: d // 4, y_hi, y_lo)
                last_updates(XB["mix0"] + KT, n + NU["mix0"] - KT, 1.0, nxt)

            def mix1(nxt):
                n = UB["mix1"]
                dve.wait_ge(a_cneg, 2)
                dve.tensor_copy(identr[:, :], ident[:, :]).then_inc(a_const, 1)
                dve.tensor_scalar(cmat[:, :], ident[0:IDIM, 0:IDIM], 1.0 / IDIM, None, ALU.subtract).then_inc(a_const, 1)
                for t in range(4):
                    produce_lo(n + t + SLOTS)
                    if t == 0:
                        dve.wait_ge(rb_ready, XNORM["mix1"] + 1)
                    dve.wait_ge(unit_used, n + t + 1)
                    b = 4 + (T1 + t) % 4
                    if t < 3:
                        dve.tensor_tensor(qlr[:, t, :] if t < 2 else kvr[:, :], ps[:, b, :], rb[:, :], ALU.mult).then_inc(tile_out, 1)
                    else:
                        dve.tensor_tensor(kx[0:IDIM, :], ps[0:IDIM, b, :], rb[0:IDIM, :], ALU.mult).then_inc(d_kx, 1)
                        W = slice(IDIM, IDIM + IH)
                        dve.scalar_tensor_tensor(out=kx[W, :], in0=ps[W, b, :], scalar=float(IH) ** -0.5 * float(IDIM) ** -0.5,
                                                 in1=rb[W, :], op0=ALU.mult, op1=ALU.mult).then_inc(tile_out, 1)
                dve.wait_ge(d_ss, 1)
                val, y, t = rs[:, 0, 0:12], rs[:, 1, 0:12], rs[:, 2, 0:12]
                for c, width in enumerate((AQR, AL, IDIM)):
                    step(dve.tensor_scalar(rs[:, 0, 4 * c:4 * c + 4], ps[:, 2, 4 * c:4 * c + 4], 1.0 / width, EPS, ALU.mult, ALU.add))
                newton(val, y, t).then_inc(d_rs, 1)
                dve.wait_ge(d_bc, 1)
                for d in range(2):
                    dve.scalar_tensor_tensor(out=sq[:, d, :], in0=qlr[:, d, :], scalar=gains[:, GB_Q + d:GB_Q + d + 1],
                                             in1=ps[:, 0, :], op0=ALU.mult, op1=ALU.mult).then_inc(d_mul, 1)
                dve.scalar_tensor_tensor(out=kvT[:, :], in0=kvr[:, :], scalar=gains[:, GB_KV:GB_KV + 1],
                                         in1=ps[:, 1, :], op0=ALU.mult, op1=ALU.mult).then_inc(d_kv, 1)
                for d in range(2):
                    dve.wait_ge(d_hi, d + 1)
                    dve.tensor_tensor(ql_lo[:, d, :], sq[:, d, :], ql_hi[:, d, :].bitcast(F32), ALU.subtract).then_inc(d_ql, 1)
                dve.wait_ge(d_kc, 1)
                dve.scalar_tensor_tensor(out=kn[0:IDIM, :], in0=kc[:, :], scalar=pcols[0:IDIM, 11:12],
                                         in1=ps[0:IDIM, 3, :], op0=ALU.mult, op1=ALU.mult).then_inc(d_kn, 1)
                dve.wait_ge(d_kn, 1)
                dve.tensor_scalar(kn[0:IDIM, :], kn[0:IDIM, :], pcols[0:IDIM, 12:13], None, ALU.add).then_inc(d_kn, 1)
                dve.wait_ge(d_kv, 1)
                dve.wait_ge(d_tr, 1)
                dve.tensor_copy(amask[:, 0, 0:P], cneg[:, :]).then_inc(k_mask, 1)
                for t in range(6):
                    produce_lo(n + 4 + t + SLOTS)
                ROUNDS = TOPK // 8

                def add_causal(b):
                    last = sc[:, b, P * (b + 1):P * (b + 2)]
                    dve.wait_ge(d_acc, IH * (b + 1))
                    dve.tensor_tensor(last, last, cneg[:, :], ALU.add).then_inc(k_causal, 1)

                def select(b, i):
                    s1, top = sc[:, b, 0:P * (b + 2)], stat[:, 3, :]
                    n_top = 2 * (ROUNDS * b + i)
                    if i == 0:
                        dve.wait_ge(k_causal, b + 1)
                    if n_top:
                        dve.wait_ge(k_top, n_top)
                    dve.max(top, s1).then_inc(k_top, 1)
                    dve.wait_ge(k_top, n_top + 1)
                    dve.match_replace(s1, top, s1, TAKEN).then_inc(k_top, 1)
                    if i == ROUNDS - 1:
                        dve.wait_ge(k_top, n_top + 2)
                        dve.tensor_scalar(amask[:, b + 1, 0:P * (b + 2)], s1, TAKEN, MASKED, ALU.not_equal, ALU.mult).then_inc(k_mask, 1)
                dve.wait_ge(d_trev, 1)
                for r in range((TT - 1) * IH):
                    b, h = r // IH, r % IH
                    w = P * (b + 2)
                    dve.wait_ge(d_relu, r + 1)
                    wcol = wtk[:, b + 1, h:h + 1]
                    if h == 0:
                        dve.tensor_scalar(sc[:, b, 0:w], sq[:, r % 4, 0:w], wcol, None, ALU.mult).then_inc(d_acc, 1)
                    else:
                        dve.wait_ge(d_acc, r)
                        dve.scalar_tensor_tensor(out=sc[:, b, 0:w], in0=sq[:, r % 4, 0:w], scalar=wcol, in1=sc[:, b, 0:w],
                                                 op0=ALU.mult, op1=ALU.add).then_inc(d_acc, 1)
                    if b:
                        if h == 0:
                            add_causal(b - 1)
                        select(b - 1, h)
                add_causal(TT - 2)
                dve.wait_ge(t_landed, 16)
                NR = TT * AH
                for r in range(NR + 1):
                    b, h = r // AH, r % AH
                    w = P * (b + 1)
                    if r < NR:
                        dve.wait_ge(a_log, r + 1)
                        if r >= 4:
                            dve.wait_ge(a_tr, r - 3)
                        dve.tensor_tensor_reduce(lp[:, r % 4, 0:w], ps[:, r % 2, 0:w], aT[:, h, TOK - w:TOK], -1.0, 3e38,
                                                 ALU.add, ALU.min, stat[:, 0, r % 4:r % 4 + 1]).then_inc(a_max, 1)
                        if r % 2 == 0 and r < 2 * ROUNDS:
                            select(TT - 2, r // 2)
                    if r:
                        q = r - 1
                        dve.wait_ge(a_exp, r)
                        if q >= 4:
                            dve.wait_ge(a_nrm, q - 3)
                        dve.reciprocal(stat[:, 2, q % 4:q % 4 + 1], stat[:, 1, q % 4:q % 4 + 1]).then_inc(a_rec, 1)
                for d in range(KT):
                    dve.wait_ge(ohi_done, OPS["dsa"] + d + 1)
                    dve.tensor_tensor(o_lo[:, d, :], ao[:, d, :], o_hi[:, d, :].bitcast(F32), ALU.subtract).then_inc(opnd_ready, 1)
                last_updates(XB["mix1"], n + NU["mix1"] - KT, 1.0, nxt)

            dve.sem_inc(mul_done, 1)
            dve.sem_inc(alo_done, 1)
            dve.sem_inc(silu_done, 1)
            dve.sem_inc(gate_scaled, 1)
            dve.sem_inc(tile_out, 4)
            dve.wait_ge(iota_ready, 2)
            ms = [0]

            def mstep(ins):
                ms[0] += 1
                ins.then_inc(mask_steps, 1)
                dve.wait_ge(mask_steps, ms[0])
            mstep(dve.tensor_tensor(ij[:, 2, :], ij[:, 0, :], ij[:, 1, :], ALU.bitwise_xor))
            mstep(dve.tensor_tensor(tri[:, :], ij[:, 0, :], ij[:, 1, :], ALU.is_ge))
            for l in range(LEVELS):
                mstep(dve.tensor_scalar(ij[:, 3, :], ij[:, 2, :], LEVELS - 1 - l, None, ALU.logical_shift_right))
                mstep(dve.scalar_tensor_tensor(out=masks[:, l, :], in0=ij[:, 3, :], scalar=1.0, in1=tri[:, :],
                                               op0=ALU.is_equal, op1=ALU.mult))
            mstep(dve.tensor_scalar(masks[:, LEVELS, :], ij[:, 2, :], 0.0, None, ALU.is_equal))
            dve.wait_ge(par_done, 2)
            dve.wait_ge(par_landed, 16 * 15)
            dve.tensor_copy(gains[:, 0:83], ps[:, 0, 0:83]).then_inc(gains_ready, 1)
            dve.tensor_copy(gains[:, GB_CW:GB_CW + 48], ps[:, 1, 0:48]).then_inc(gains_ready, 1)
            dve.wait_ge(gains_ready, 2)
            for m in range(KT):
                dve.wait_ge(xt_done, m + 1)
                dve.tensor_copy(x[:, m, :], ps[:, 4 + m % 4, :]).then_inc(x_upd, 1)
            produce_lo(0)
            for m in range(KT):
                next_low(STAGES[0], m)
                add_square(STAGES[0], m)
                if m in (3, 5):
                    produce_lo(m // 2)
            produce_lo(SLOTS - 1)
            rsqrt(0, TT, 1.0 / D)
            for k, st in enumerate(STAGES):
                nxt = (STAGES + ["final"])[k + 1]
                if st.startswith("ffn"):
                    ffn(st, nxt)
                elif st == "mix0":
                    mix0(nxt)
                else:
                    mix1(nxt)
            dve.wait_ge(rstd_ready, NORMS["final"] + 1)
            dve.wait_ge(gfin_landed, 16)
            for t in range(TT):
                if t >= 2:
                    dve.wait_ge(stored[t % 2], 16)
                for c in range(2):
                    dve.wait_ge(fin_t, 2 * t + c + 1)
                    dve.scalar_tensor_tensor(out=otile[:, t % 2, c * 512:(c + 1) * 512], in0=ps[:, 4 + (2 * t + c) % 4, :],
                                             scalar=rs[:, 1, t:t + 1], in1=gfin[:, c * 512:(c + 1) * 512],
                                             op0=ALU.mult, op1=ALU.mult).then_inc(fin_ready, 1)

        @block.tensor
        def _(pe):
            def unit(n, bank, rh, rl, nk, i=0, ready=None):
                s = n % SLOTS
                pe.wait_ge(lo_ready, n + 1 + 4 * i)
                for k in range(nk):
                    if ready:
                        ready(k)
                    wh, wl = w_hi[:, s, k * P:(k + 1) * P], w_lo[:, s, k * P:(k + 1) * P]
                    pe.matmul(ps[:, bank, :], wh, rh[:, k, :], start=k == 0, stop=False)
                    pe.matmul(ps[:, bank, :], wh, rl[:, k, :], start=False, stop=False)
                    mm = pe.matmul(ps[:, bank, :], wl, rh[:, k, :], start=False, stop=k == nk - 1)
                mm.then_inc(unit_used, 1)

            def sumsq(z, m, cols=None, first=None, last=None):
                pe.wait_ge(sq_ready, KT * z + m + 1)
                c0 = cols if cols is not None else 0
                for t in range(TT):
                    mm = pe.matmul(ps[:, 2, c0 + t:c0 + t + 1], sq[:, m % 4, t * P:(t + 1) * P], ones[:, 0:1],
                                   start=(m == 0 and t == 0), stop=(m == KT - 1 if last is None else last), skip_group_check=True)
                mm.then_inc(ss_done, 1)

            def sumsq_x(st):
                pe.wait_ge(sq_added, (KT - 1) * (XNORM[st] + 1))
                for t in range(TT):
                    mm = pe.matmul(ps[:, 2, t:t + 1], sq[:, 3, t * P:(t + 1) * P], ones[:, 0:1], start=True, stop=True, skip_group_check=True)
                mm.then_inc(ss_done, 1)

            def spread(z, banks):
                pe.wait_ge(rstd_ready, z + 1)
                for b, bank in enumerate(banks):
                    for t in range(TT):
                        c = b * TT + t
                        mm = pe.matmul(ps[:, bank, t * P:(t + 1) * P], rs[:, 1, c:c + 1].to_broadcast([P, P]), ident[:, :],
                                       start=True, stop=True, skip_group_check=True)
                mm.then_inc(bc_done, 1)

            def ready_of(o):
                return lambda k: pe.wait_ge(opnd_ready, o + k + 1)

            def ffn(st, nxt):
                n = UB[st]
                fb = FT * [s for s in STAGES if s.startswith("ffn")].index(st)
                xc = XB[st]
                for ph, (f0, nf) in enumerate(PHASES):
                    f = fb + f0

                    def pair(i):
                        first = ph == 0 and isinstance(i, int)
                        for j in range(2):
                            pe.wait_ge(gate_scaled, f + 2 * i + 1)
                            unit(n + 2 * j, 2 * j, h_hi, h_lo, KT, i, ready_of(OPS[st]) if first and j == 0 else None)
                            if first and j == 0:
                                sumsq_x(st)
                                spread(NORMS[st], [3])
                            if first and j == 1:
                                pe.wait_ge(rb_ready, XNORM[st] + 1)
                            pe.wait_ge(mul_done, f + 2 * i + 1)
                            unit(n + 2 * j + 1, 2 * j + 1, h_hi, h_lo, KT, i)
                    if ph == 0:
                        pair(0)
                    with pe.Fori(ph == 0, nf // 2) as i:
                        pair(i)
                    n += 2 * nf
                    pe.wait_ge(alo_done, f + nf - 2 + 1)

                    def dwait(k):
                        if k >= nf - 2:
                            pe.wait_ge(alo_done, f + k + 2)
                    if ph < 2:
                        with pe.Fori(0, 2) as i:
                            for j in range(4):
                                pe.wait_ge(x_upd, xc - 4 + j + 1 + 4 * i)
                                unit(n + j, 4 + j, act_hi, act_lo, nf, i, dwait if j == 0 else None)
                    else:
                        for m in range(KT):
                            pe.wait_ge(x_upd, xc - 4 + m + 1)
                            unit(n + m, 4 + m % 4, act_hi, act_lo, nf, 0, dwait if m == 0 else None)
                    n += KT
                    xc += KT

            def mix0(nxt):
                n = UB["mix0"]
                unit(n, 4, h_hi, h_lo, KT, 0, ready_of(OPS["mix0"]))
                sumsq_x("mix0")
                spread(NORMS["mix0"], [3])
                unit(n + 1, 5, h_hi, h_lo, KT)
                pe.wait_ge(wg2_landed, 16)
                pe.wait_ge(g_glr, 1)
                for h in range(GH):
                    pe.matmul(ps[:, h, :], small[0:GRANK, h * P:(h + 1) * P], sq[0:GRANK, 0, :], start=True, stop=True).then_inc(g_gate_mm, 1)
                for t in range(2, 9):
                    pe.wait_ge(tile_out, t + 1)
                    unit(n + t, 4 + t % 4, h_hi, h_lo, KT)

                def level(l):
                    if l < LEVELS:
                        pe.wait_ge(g_mul, 2 * (l + 1))
                    for c in range(TT):
                        if l:
                            pe.wait_ge(g_mask, TT * (l - 1) + c + 1)
                        for h in range(GH):
                            kk = gm[:, l % 2, h, c * P:(c + 1) * P] if l < LEVELS else gk[:, h, c * P:(c + 1) * P]
                            qq = gm[:, l % 2, h, c * P:(c + 1) * P] if l < LEVELS else gq[:, h, c * P:(c + 1) * P]
                            mm = pe.matmul(ps[:, c, h * P:(h + 1) * P], kk, qq, start=True, stop=True, skip_group_check=True)
                        mm.then_inc(g_lvl, 1)
                for s in range(8):
                    t = 9 + s
                    pe.wait_ge(tile_out, t + 1)
                    if s > 4:
                        pe.wait_ge(g_vev, 2 * (s - 4))
                    unit(n + t, 4 + t % 4, h_hi, h_lo, KT)
                    if s >= 4:
                        for v in (2 * (s - 4), 2 * (s - 4) + 1):
                            pe.wait_ge(tile_out, max(t + 2 + v % 2, 4 + 9 + v + 1))
                            for c in range(TT):
                                mm = pe.transpose(ps[:, 4 + (t + 1 + v % 2) % 4, c * P:(c + 1) * P], gvT[:, v, c * P:(c + 1) * P], ident[:, :])
                            mm.then_inc(g_vt, 1)
                    if s:
                        level(s - 1)
                level(LEVELS)

                def r_unit(v):
                    t = 17 + v
                    pe.wait_ge(tile_out, t + 1)
                    unit(n + t, 4 + t % 4, h_hi, h_lo, KT)
                pe.wait_ge(g_vev, GVT)
                r_unit(0)
                r_unit(1)
                pe.wait_ge(g_decm, 3)
                for c in range(TT):
                    pe.wait_ge(g_mask, TT * LEVELS + c + 1)
                    for h in range(GH):
                        mm = pe.transpose(ps[:, c, h * P:(h + 1) * P], gk[:, h, c * P:(c + 1) * P], ident[:, :])
                    mm.then_inc(g_kt, 1)
                for c in range(TT):
                    if c:
                        pe.wait_ge(g_oev, 2 * c)
                        pe.wait_ge(g_S, GH * c)
                    else:
                        pe.wait_ge(g_kev, TT)
                    for m in range(GVT):
                        h, vt = m // 2, m % 2
                        dst = ps[:, 2 + m // 4, (m % 4) * P:(m % 4 + 1) * P]
                        if c:
                            pe.matmul(dst, gS[:, h, vt * P:(vt + 1) * P], gq[:, h, c * P:(c + 1) * P], start=True, stop=False, skip_group_check=True)
                        mm = pe.matmul(dst, gv[:, c, m * P:(m + 1) * P], gattn[:, c, h, :], start=c == 0, stop=True, skip_group_check=True)
                    mm.then_inc(g_o, 1)
                    if c < TT - 1:
                        for h in range(GH):
                            pe.matmul(ps[:, h // 2, (h % 2) * GDV:(h % 2 + 1) * GDV], gkd[:, c, h, :],
                                      gv[:, c, h * GDV:(h + 1) * GDV], start=True, stop=True, skip_group_check=True).then_inc(g_st, 1)
                        r_unit(2 + c)
                R = slice(DT0, DT0 + SH)
                pe.wait_ge(s_acum, TT)
                pe.wait_ge(g_S, GH * (TT - 1))
                for b in range(2):
                    for c in range(TT):
                        src = (small[R, c * P:(c + 1) * P], dt_tmp[R, 2, c * P:(c + 1) * P])[b]
                        mm = pe.transpose(ps[:, 0, (b * TT + c) * SH:(b * TT + c + 1) * SH], src, ident[R, R])
                mm.then_inc(s_tok, 1)
                r_unit(5)
                r_unit(6)
                z = NORMS["gla"]
                for m in range(GVT):
                    sumsq(z, m, (m // 2) * TT)
                r_unit(7)
                pe.wait_ge(s_tokev, 1)
                spread(z, [0, 1, 2, 3])
                n0 = n + 25
                for m in range(KT):
                    if m >= 4:
                        pe.wait_ge(x_upd, XB["mix0"] + m - 3)
                    unit(n0 + m, 4 + m % 4, o_hi, o_lo, KT, 0, ready_of(OPS["gla"]) if m == 0 else None)
                n0 += KT
                tb = 25
                with pe.Fori(0, XT // 4) as i:
                    for j in range(4):
                        pe.wait_ge(x_upd, XB["mix0"] + KT - 3 + (tb + j) % 4)
                        pe.wait_ge(tile_out, tb + j + 1 + 4 * i)
                        unit(n0 + j, 4 + (tb + j) % 4, h_hi, h_lo, KT, i)
                n0 += XT

                def z_unit(m):
                    if m:
                        pe.wait_ge(z_out, m)
                    unit(n0 + m, 1, h_hi, h_lo, KT)
                z_unit(0)
                pe.wait_ge(s_silu, XT)
                for c in range(TT):
                    if c:
                        pe.wait_ge(s_cbm, c)
                        pe.wait_ge(s_Bev, c)
                        pe.wait_ge(s_S2, c)
                    cc = slice(c * P, (c + 1) * P)
                    for g in range(SG):
                        mm = pe.matmul(ps[:, 0, g * P:(g + 1) * P], xbc[:, 8 + g, cc], xbc[:, 10 + g, cc], start=True, stop=True, skip_group_check=True)
                    mm.then_inc(s_cb, 1)
                    for g in range(SG):
                        mm = pe.transpose(ps[:, 0, (SG + g) * P:(SG + g + 1) * P], xbc[:, 8 + g, cc], ident[:, :])
                    mm.then_inc(s_trB, 1)
                    for m in range(SI // P):
                        mm = pe.transpose(ps[:, 2 + m // 4, (m % 4) * P:(m % 4 + 1) * P], xbc[:, m, cc], ident[:, :])
                    mm.then_inc(s_tr, 1)
                    z_unit(2 * c + 1)
                    if c < TT - 1:
                        pe.wait_ge(s_Bev, c + 1)
                        pe.wait_ge(s_xdtw, c + 1)
                        for g in range(SG):
                            mm = pe.matmul(ps[:, 2 + g, :], sB[:, g, :], xdtw[:, g * 512:(g + 1) * 512], start=True, stop=True)
                        mm.then_inc(s_st, 1)
                    pe.wait_ge(s_P, 2 * (c + 1))
                    pe.wait_ge(s_C, 2 * (c + 1))
                    if c >= 2:
                        pe.wait_ge(s_yev, c - 1)
                    else:
                        pe.wait_ge(tile_out, 4 + 25 + XT)
                    for h in range(SH):
                        m = h // 2
                        dst = ps[(h % 2) * SHD:(h % 2 + 1) * SHD, 4 + 2 * (c % 2) + m // 4, (m % 4) * P:(m % 4 + 1) * P]
                        if c:
                            pe.matmul(dst, sS[:, h * SHD:(h + 1) * SHD], acb[:, c % 2, h, :], start=True, stop=False, skip_group_check=True)
                        mm = pe.matmul(dst, xdt[:, h * SHD:(h + 1) * SHD], pm[:, c % 2, h, :], start=c == 0, stop=True, skip_group_check=True)
                    mm.then_inc(s_y, 1)
                    if c < TT - 1:
                        z_unit(2 * c + 2)
                z = NORMS["ssd"]
                for m in range(KT):
                    sumsq(z, m, (m // 4) * TT)
                spread(z, [0, 1])
                n0 = n + NU["mix0"] - KT
                z = NORMS[nxt]
                for m in range(KT):
                    if m >= 4:
                        pe.wait_ge(x_upd, XB["mix0"] + KT + m - 3)
                    unit(n0 + m, 4 + m % 4, y_hi, y_lo, KT, 0, ready_of(OPS["ssd"]) if m == 0 else None)

            def mix1(nxt):
                n = UB["mix1"]
                for t in range(4):
                    pe.wait_ge(x_upd, XB["mix1"] - 3 + (T1 + t) % 4)
                    pe.wait_ge(tile_out, T1 + t + 1)
                    unit(n + t, 4 + (T1 + t) % 4, h_hi, h_lo, KT, 0, ready_of(OPS["mix1"]) if t == 0 else None)
                    if t == 0:
                        sumsq_x("mix1")
                        spread(NORMS["mix1"], [3])
                pe.wait_ge(a_const, 2)
                pe.wait_ge(d_kx, 1)
                pe.matmul(ps[0:IDIM, 0, :], cmat[:, :], kx[0:IDIM, :], start=True, stop=True).then_inc(d_cen, 1)
                pe.wait_ge(d_raw, 3)
                for c in range(2):
                    for j in ((0, 1), (2,))[c]:
                        for t in range(TT):
                            pe.matmul(ps[:, 2, 4 * c + t:4 * c + t + 1], sq[:, j, t * P:(t + 1) * P], ones[:, 0:1],
                                      start=j == 0 and t == 0, stop=j == 2, skip_group_check=True)
                pe.wait_ge(d_sq, 1)
                for t in range(TT):
                    mm = pe.matmul(ps[:, 2, 8 + t:9 + t], sq[0:IDIM, 3, t * P:(t + 1) * P], ones[0:IDIM, 0:1],
                                   start=False, stop=True, skip_group_check=True)
                mm.then_inc(d_ss, 1)
                pe.wait_ge(d_kc, 1)
                pe.wait_ge(d_rs, 1)
                for b, bank in enumerate((0, 1, 3)):
                    for t in range(TT):
                        c = b * TT + t
                        mm = pe.matmul(ps[:, bank, t * P:(t + 1) * P], rs[:, 1, c:c + 1].to_broadcast([P, P]), ident[:, :],
                                       start=True, stop=True, skip_group_check=True)
                mm.then_inc(d_bc, 1)
                R = slice(IDIM, IDIM + IH)
                pe.wait_ge(tile_out, T1 + 4 + 4)
                for c in range(TT):
                    mm = pe.transpose(ps[:, 2, c * IH:(c + 1) * IH], kx[R, c * P:(c + 1) * P], ident[R, R])
                mm.then_inc(d_tr, 1)
                pe.wait_ge(d_kv, 1)
                for c in range(TT):
                    mm = pe.transpose(ps[:, 0, c * P:(c + 1) * P], kvT[:, c * P:(c + 1) * P], ident[:, :])
                mm.then_inc(d_tr, 1)
                pe.wait_ge(d_ql, 2)
                for u in range(6):
                    s = (n + 4 + u) % SLOTS
                    pe.wait_ge(lo_ready, n + 4 + u + 1)
                    for j in range(4):
                        t = 4 * u + j
                        pe.wait_ge(tile_out, T1 + 4 + t + 1)
                        dst = ps[:, 4 + (T1 + t) % 4, :]
                        for k in range(2):
                            c0 = k * 512 + j * P
                            wh, wl = w_hi[:, s, c0:c0 + P], w_lo[:, s, c0:c0 + P]
                            pe.matmul(dst, wh, ql_hi[:, k, :], start=k == 0, stop=False)
                            pe.matmul(dst, wh, ql_lo[:, k, :], start=False, stop=False)
                            mm = pe.matmul(dst, wl, ql_hi[:, k, :], start=False, stop=k == 1)
                        mm.then_inc(unit_used if j == 3 else d_tile, 1)
                pe.wait_ge(d_dup, 16)
                for r in range((TT - 1) * IH):
                    b, h = r // IH + 1, r % IH
                    w = P * (b + 1)
                    R = slice((h % 2) * IDIM, (h % 2 + 1) * IDIM)
                    if r >= 4:
                        pe.wait_ge(d_relu, r - 3)
                    pe.matmul(ps[:, r % 4, 0:w], qix[R, h // 2, b * P:(b + 1) * P], kn[R, 0:w], start=True, stop=True).then_inc(d_ix, 1)
                pe.wait_ge(d_relu, (TT - 1) * IH)
                pe.wait_ge(tile_out, T1 + 4 + 4 + KT + AH)
                pe.wait_ge(uv_landed, 16)
                NR = TT * AH

                def p_turn(r):
                    b = r // AH
                    pe.wait_ge(a_nrm, r + 1)
                    if r >= 2:
                        pe.wait_ge(a_pt, r - 1)
                    for st in range(b + 1):
                        mm = pe.transpose(ps[:, 2 + r % 2, st * P:(st + 1) * P], lp[:, r % 4, st * P:(st + 1) * P], ident[:, :])
                    mm.then_inc(a_tr, 1)

                def latent(r):
                    b, g = r // AH, r // 4
                    pe.wait_ge(a_pt, r + 1)
                    if r % 4 == 0 and g >= 2:
                        pe.wait_ge(a_ol, g - 1)
                    for st in range(b + 1):
                        mm = pe.matmul(ps[:, 4 + g % 2, (r % 4) * P:(r % 4 + 1) * P], kvtok[:, st, :], pt[:, r % 2, st * P:(st + 1) * P],
                                       start=st == 0, stop=st == b, skip_group_check=True)
                    mm.then_inc(a_pv, 1)

                def values(g):
                    pe.wait_ge(a_ol, g + 1)
                    if g >= 4:
                        pe.wait_ge(a_o, g // 2 - 1)
                    for j in range(4):
                        h = (4 * g + j) % AH
                        m = h // 2
                        mm = pe.matmul(ps[(h % 2) * AV:(h % 2 + 1) * AV, 6 + m // 4, (m % 4) * P:(m % 4 + 1) * P], wuv[:, h, :],
                                       olat[:, g % 2, j * P:(j + 1) * P], start=True, stop=True, skip_group_check=True)
                    mm.then_inc(a_uv, 1)
                for r in range(NR + LAG + 3):
                    if r < NR:
                        b, h = r // AH, r % AH
                        w = P * (b + 1)
                        if h == 0:
                            pe.wait_ge(k_mask, b + 1)
                        if r >= 2:
                            pe.wait_ge(a_max, r - 1)
                        pe.matmul(ps[:, r % 2, 0:w], aq[:, h, b * P:(b + 1) * P], kvT[:, 0:w], start=True, stop=False)
                        pe.matmul(ps[:, r % 2, 0:w], identr[:, :], amask[:, b, 0:w], start=False, stop=True).then_inc(a_log, 1)
                    if LAG <= r < NR + LAG:
                        p_turn(r - LAG)
                    if LAG + 1 <= r < NR + LAG + 1:
                        latent(r - LAG - 1)
                    if r >= LAG + 3 and (r - LAG - 3) % 4 == 3 and (r - LAG - 3) // 4 < NR // 4:
                        values((r - LAG - 3) // 4)
                n0 = n + NU["mix1"] - KT
                z = NORMS[nxt]
                for m in range(KT):
                    if m >= 4:
                        pe.wait_ge(x_upd, XB["mix1"] + m - 3)
                    unit(n0 + m, 4 + m % 4, o_hi, o_lo, KT, 0, ready_of(OPS["dsa"]) if m == 0 else None)

            pe.wait_ge(consts_ready, 3)
            pe.wait_ge(l_landed, 32)
            pe.matmul(ps[0:AH, 2, :], relb[:, :], hot[:, 0:TOK], start=True, stop=True)
            pe.matmul(ps[0:AH, 3, 0:P], relb[:, :], hot[:, TOK:LINE], start=True, stop=True).then_inc(l_mm, 1)
            pe.wait_ge(par_landed, 16 * 15)
            pe.transpose(ps[:, 0, 0:83], prow[0:83, 0, :], ident[0:83, 0:83]).then_inc(par_done, 1)
            pe.transpose(ps[:, 1, 0:48], prow[0:48, 1, :], ident[0:48, 0:48]).then_inc(par_done, 1)
            pe.wait_ge(x_landed, 16)
            for m in range(KT):
                if m >= 4:
                    pe.wait_ge(x_upd, m - 3)
                for t in range(TT):
                    mm = pe.transpose(ps[:, 4 + m % 4, t * P:(t + 1) * P], x_in[:, t, m * P:(m + 1) * P], ident[:, :])
                mm.then_inc(xt_done, 1)
            pe.wait_ge(l_ev, 2)
            for k, st in enumerate(STAGES):
                nxt = (STAGES + ["final"])[k + 1]
                if st.startswith("ffn"):
                    ffn(st, nxt)
                elif st == "mix0":
                    mix0(nxt)
                else:
                    mix1(nxt)
            sumsq_x("final")
            for t in range(TT):
                for c in range(2):
                    if 2 * t + c >= 4:
                        pe.wait_ge(fin_ready, 2 * t + c - 3)
                    for m in range(4):
                        mm = pe.transpose(ps[:, 4 + (2 * t + c) % 4, m * P:(m + 1) * P],
                                          x[:, 4 * c + m, t * P:(t + 1) * P], ident[:, :])
                    mm.then_inc(fin_t, 1)


_INS = ["x", "ffn_norm_g", "ffn_w_gate", "ffn_w_up", "ffn_w_down", "mix_norm_g", "final_norm_g",
        "hy_w_in", "gla_w_gate2", "gla_b_gate", "gla_norm_g", "ssd_conv_w", "ssd_conv_b", "ssd_dt_bias", "ssd_a_log",
        "ssd_d", "ssd_norm_g", "hy_w_out",
        "dsa_w_dq", "dsa_q_norm_g", "dsa_w_uq", "dsa_w_dkv", "dsa_kv_norm_g", "dsa_w_uv", "dsa_w_o",
        "idx_w_q", "idx_w_k", "idx_ln_g", "idx_ln_b", "idx_w_w", "rel_bias"]


def _CONSTS():
    import math
    import numpy as np

    dist = np.maximum(TOK - 1 - np.arange(LINE), 0)
    exact = REL_BUCKETS // 2
    large = exact + (np.log(np.maximum(dist, 1).astype(np.float32) / np.float32(exact))
                     / np.float32(math.log(REL_MAX_DIST / exact)) * np.float32(REL_BUCKETS - exact)).astype(np.int32)
    bucket = np.where(dist < exact, dist, np.minimum(large, REL_BUCKETS - 1))
    return {"bucket_onehot": (bucket[None, :] == np.arange(REL_BUCKETS)[:, None]).astype(np.float32)}


def kernel(**inputs):
    import numpy as np
    import concourse.bacc as bacc
    from concourse.bass_utils import run_bass_kernel_spmd

    nc = bacc.Bacc("TRN2", target_bir_lowering=False, num_devices=1)
    arrays, aps = {}, {}
    for name in _INS:
        arrays[f"in_{name}"] = np.ascontiguousarray(inputs[name])
        aps[name] = nc.dram_tensor(f"in_{name}", arrays[f"in_{name}"].shape, F32, kind="ExternalInput").ap()
    for name, value in _CONSTS().items():
        arrays[f"in_{name}"] = value
        aps[name] = nc.dram_tensor(f"in_{name}", value.shape, F32, kind="ExternalInput").ap()
    out = nc.dram_tensor("out", (1, TOK, D), F32, kind="ExternalOutput").ap()
    build_program(nc, aps, out)
    got = run_bass_kernel_spmd(nc, [arrays], core_ids=[0])
    return got.results[0]["out"]
```

```python
from contextlib import ExitStack

import concourse.bass as bass
from concourse import mybir

F32 = mybir.dt.float32
F32R = mybir.dt.float32r
I32 = mybir.dt.int32
I8 = mybir.dt.int8
ALU = mybir.AluOpType
ACT = mybir.ActivationFunctionType
KB = 1024

P = 128
TOK = 512
D = 1024
KT = D // P
TT = TOK // P
D_FF = 2816
FT = D_FF // P
EPS = 1e-6
GH, GDK, GDV, GRANK, GTAU = 4, 128, 256, 16, 16.0
GVT = GH * GDV // P
SH, SHD, SN, SG, TAPS = 16, 64, 128, 2, 4
SI = SH * SHD
XT = (SI + 2 * SG * SN) // P
HY_Q, HY_K, HY_V = 0, GH * GDK, 2 * GH * GDK
HY_R = HY_V + GH * GDV
HY_G = HY_R + GH * GDV
HY_Z = HY_G + GRANK
HY_XBC = HY_Z + SI
HY_DT = HY_XBC + XT * P
DT0 = 64
LEVELS = 7
AH, AL, AV, AQR = 16, 128, 64, 256
IH, IDIM, TOPK = 16, 64, min(256, TOK // 4)
REL_BUCKETS, REL_MAX_DIST = 32, 128
LINE = TOK + P
LAG, RING = 4, 8
EARLY = TT * AH - 8
MASKED, TAKEN = -1e30, -3e38

SLOTS = 4
UC = KT * P
PHASES = ((0, 8), (8, 8), (16, 6))
STAGES = ["ffn0", "mix0", "ffn1", "ffn2", "mix1", "ffn3"]


def build_program(nc, a, out):
    ctx = ExitStack()
    with ctx:
        def sb(name, shape, dt=F32):
            return ctx.enter_context(nc.sbuf_tensor(name, shape, dt))

        def sem(name):
            return ctx.enter_context(nc.semaphore(name))

        x = sb("x", [P, KT, TOK])
        H0 = nc.sbuf_base
        h_hi = sb("h_hi", [P, KT, TOK], F32R)
        h_lo = sb("h_lo", [P, KT, TOK], F32R)
        w_raw = sb("w_raw", [P, SLOTS, UC])
        w_hi = sb("w_hi", [P, SLOTS, UC], F32R)
        w_lo = sb("w_lo", [P, SLOTS, UC], F32R)
        ident = sb("ident", [P, P])
        ones = sb("ones", [P, P])
        sq = sb("sq", [P, 4, TOK])
        rs = sb("rs", [P, 4, 16])
        rms_rows = sb("rms_rows", [P, TOK])
        gains = sb("gains", [P, 176])
        pcols = sb("pcols", [P, 16])
        ps = ctx.enter_context(nc.psum_tensor("ps", [P, 8, 512], F32))
        ARENA = 99 * KB + 768
        sb("arena", [P, ARENA // 4])
        A0 = nc.sbuf_base - ARENA

        def at(name, shape, kb, dt=F32):
            return nc.alloc_sbuf_tensor_at(name, shape, dt, offset=A0 + int(kb * KB))
        act_hi = at("act_hi", [P, 8, TOK], 0, F32R)
        act_lo = at("act_lo", [P, 8, TOK], 16, F32R)
        silu_gate = at("silu_gate", [P, 2, TOK], 32)
        prod = at("prod", [P, 2, TOK], 36)
        x_in = at("x_in", [P, TT, D], 40)
        prow = at("prow", [P, 2, P], 56)
        ij = at("ij", [P, 4, P], 57, I32)
        gfin = at("gfin", [P, D], 60)
        otile = at("otile", [P, 2, D], 64)
        gla_q = at("gla_q", [P, GH, TOK], 0)
        gla_k = at("gla_k", [P, GH, TOK], 8)
        gla_v = at("gla_v", [P, TT, GH * GDV], 16)
        o_hi = at("o_hi", [P, KT, TOK], 0, F32R)
        o_lo = at("o_lo", [P, KT, TOK], 16, F32R)
        gla_sums = at("gla_sums", [P, GH, TOK], 32)
        gla_level = at("gla_level", [P, 2, GH, TOK], 40)
        gla_attn = at("gla_attn", [P, TT, GH, P], 56)
        gla_gate = at("gla_gate", [P, GVT, TOK], 64)
        gla_vT = at("gla_vT", [P, GVT, TOK], 80)
        small = at("small", [P, TOK], 96)
        masks = at("masks", [P, LEVELS + 1, P], 98, I8)
        tri = at("tri", [P, P], 99)
        gla_state = gla_level[:, 0, 0:2, :].rearrange("p a b -> p (a b)").rearrange("p (h v) -> p h v", h=GH)
        dt_tmp = gla_sums[:, 0:3, :]
        gla_k_turned = gla_level[:, 1, :, :].rearrange("p c (h k) -> p c h k", h=GH)
        gla_chunk_decay = at("gla_chunk_decay", [P, GH, TT], 99.625)
        xbc = at("xbc", [P, XT, TOK], 0)
        z_gate_tiles = at("z_gate_tiles", [P, SI // P, TOK], 24)
        acum_rows = at("acum_rows", [P, 2, SH, P], 40)
        ssd_attn = at("ssd_attn", [P, 2, SH, P], 56)
        xdt = at("xdt", [P, SI], 72)
        xdtw = at("xdtw", [P, SI], 76)
        ssd_B = at("ssd_B", [P, SG, P], 80)
        ssd_CB = at("ssd_CB", [P, SG, P], 81)
        ssd_state = at("ssd_state", [P, SI], 82)
        y_hi = at("y_hi", [P, KT, TOK], 40, F32R)
        y_lo = at("y_lo", [P, KT, TOK], 56, F32R)
        osq = at("osq", [P, GH, 2, TOK], 0)
        ysq = at("ysq", [P, KT, TOK], 80)
        rgrp = at("rgrp", [P, SG, TOK], 72)
        xgrp = at("xgrp", [P, SG, TOK], 76)
        conv_in = at("conv_in", [P, 2, TOK + 8], 86)
        toks = at("toks", [P, 2, TT, SH], 98)
        wtok = at("wtok", [P, 2, 2, SH], 98.5)
        acum_dram = nc.dram_tensor("acum_scratch", (SH, TOK), F32).ap()

        bias_rows = at("bias_rows", [P, AH, TOK], 64)
        att_q = at("att_q", [P, AH, TOK], 0)
        kvT = at("kvT", [P, TOK], 32)
        kvtok = at("kvtok", [P, TT, AL], 34)
        att_mask = at("att_mask", [P, TT, TOK], 36, F32R)
        kv_raw = at("kv_raw", [P, TOK], 36)
        index_k_raw = at("index_k_raw", [P, TOK], 38)
        index_k_centred = at("index_k_centred", [IDIM, TOK], 40)
        probs = at("probs", [P, RING, TOK], 44)
        q_latent_raw = at("q_latent_raw", [P, 2, TOK], 44)
        q_latent_hi = at("q_latent_hi", [P, 2, TOK], 48, F32R)
        q_latent_lo = at("q_latent_lo", [P, 2, TOK], 52, F32R)
        probs_T = nc.alloc_sbuf_tensor_at("probs_T", [P, 2, TOK], F32, offset=H0 + 22 * KB)
        o_latent = nc.alloc_sbuf_tensor_at("o_latent", [P, 2, TOK], F32, offset=H0 + 26 * KB)
        w_uv_sb = at("w_uv_sb", [P, AH, AV], 60)
        index_k = at("index_k", [P, TOK], 96)
        causal_neg = at("causal_neg", [P, P], 98)
        identr = at("identr", [P, P], 98.5, F32R)
        cmat = at("cmat", [IDIM, IDIM], 99)
        index_w_tok = at("index_w_tok", [P, TT, IH], 99.25)
        stat = at("stat", [P, 4, 8], 99.5)
        index_q = nc.alloc_sbuf_tensor_at("index_q", [P, KT, TOK], F32, offset=H0)
        att_out = nc.alloc_sbuf_tensor_at("att_out", [P, KT, TOK], F32, offset=H0)
        index_scores = nc.alloc_sbuf_tensor_at("index_scores", [P, TT - 1, TOK], F32, offset=H0 + 16 * KB)
        rel_bias_sb = at("rel_bias_sb", [REL_BUCKETS, AH], 72)
        bucket_sb = at("bucket_sb", [REL_BUCKETS, LINE], 73)
        line = at("line", [AH, LINE], 76)
        line_dram = nc.dram_tensor("line_scratch", (AH, P, LINE), F32).ap()

        NU = {"ffn": 2 * FT + 3 * KT, "mix0": 1 + 8 + 2 * GVT + KT + SI // P + XT + KT, "mix1": 18}
        NX = {"ffn": 3 * KT, "mix0": 2 * KT, "mix1": KT}
        UB, XB, un, xn = {}, {}, 0, KT
        for st in STAGES:
            UB[st], XB[st] = un, xn
            un += NU.get(st, NU["ffn"])
            xn += NX.get(st, NX["ffn"])
        NUNITS = un
        OPS, NORMS, XNORM = {}, {}, {}
        for st in STAGES:
            OPS[st] = 8 * len(OPS)
            NORMS[st] = len(NORMS)
            if st == "mix0":
                for e in ("gla", "ssd"):
                    OPS[e] = 8 * len(OPS)
                    NORMS[e] = len(NORMS)
            if st == "mix1":
                OPS["dsa"] = 8 * len(OPS)
            XNORM[st] = len(XNORM)
        NORMS["final"], XNORM["final"] = len(NORMS), len(XNORM)
        SS, acc_ss = {}, 0
        for st, z in NORMS.items():
            SS[z] = acc_ss
            acc_ss += GH if st == "gla" else 1
        GATED = {"gla": 0, "ssd": KT}

        def SUM_BANK(st):
            return 6 if st.startswith("ffn") else 2

        GROUP_BANKS = (2, 6, 4)
        Z_BANKS = (1, 6, 7)

        def SPREAD_BANK(st):
            return 7 if st.startswith("ffn") else 3
        GAIN = {st: KT * int(st[3]) if st.startswith("ffn") else 32 + KT * int(st[3]) for st in STAGES}
        parts = [1] * NUNITS
        if "mix0" in UB:
            parts[UB["mix0"]] = 3
        if "mix1" in UB:
            parts[UB["mix1"] + 3] = 3
        LAND, acc = [], [0] * SLOTS
        for n in range(NUNITS):
            acc[n % SLOTS] += 16 * parts[n]
            LAND.append(acc[n % SLOTS])

        raw_landed = [sem(f"raw_landed{s}") for s in range(SLOTS)]
        hi_ready, lo_ready, unit_used = sem("hi_ready"), sem("lo_ready"), sem("unit_used")
        consts_ready, iota_ready, mask_steps = sem("consts_ready"), sem("iota_ready"), sem("mask_steps")
        x_landed, par_landed, cols_landed, gfin_landed = sem("x_landed"), sem("par_landed"), sem("cols_landed"), sem("gfin_landed")
        xt_done, par_done, gains_ready = sem("xt_done"), sem("par_done"), sem("gains_ready")
        x_upd = sem("x_upd")
        s_tap0, e_hi, e_lo = sem("s_tap0"), sem("e_hi"), sem("e_lo")
        y_gated = sem("y_gated")
        sq_paired, sq_tree = sem("sq_paired"), sem("sq_tree")
        rb_ready, gate_scaled, up_scaled = sem("rb_ready"), sem("gate_scaled"), sem("up_scaled")
        grp_ready, grp_steps = sem("grp_ready"), sem("grp_steps")
        r_silu, z_silu, z_out = sem("r_silu"), sem("z_silu"), sem("z_out")
        wg2_landed = sem("wg2_landed")
        silu_done, mul_done, ahi_done, alo_done = sem("silu_done"), sem("mul_done"), sem("ahi_done"), sem("alo_done")
        sq_ready, sq_added, ss_done = sem("sq_ready"), sem("sq_added"), sem("ss_done")
        rsq_steps, rstd_ready, bc_done = sem("rsq_steps"), sem("rstd_ready"), sem("bc_done")
        omul_done, ohi_done, opnd_ready = sem("omul_done"), sem("ohi_done"), sem("opnd_ready")
        fin_t, fin_ready = sem("fin_t"), sem("fin_ready")
        stored = [sem("stored_even"), sem("stored_odd")]
        tile_out = sem("tile_out")
        g_glr, g_gate_mm, g_gate_b, g_abs, g_scan = sem("g_glr"), sem("g_gate_mm"), sem("g_gate_b"), sem("g_abs"), sem("g_scan")
        g_diff, g_exp, g_mul, g_lvl, g_mask = sem("g_diff"), sem("g_exp"), sem("g_mul"), sem("g_lvl"), sem("g_mask")
        g_zero, g_vt, g_vev = sem("g_zero"), sem("g_vt"), sem("g_vev")
        g_dec, g_decm, g_kt, g_kev, g_o, g_oev, g_st, g_S = (sem(n) for n in (
            "g_dec", "g_decm", "g_kt", "g_kev", "g_o", "g_oev", "g_st", "g_S"))
        g_gated = sem("g_gated")
        s_dt, s_dta, s_acum, s_scr, s_tok, s_tokev = (sem(n) for n in ("s_dt", "s_dta", "s_acum", "s_scr", "s_tok", "s_tokev"))
        s_acb = [sem("s_acb_even"), sem("s_acb_odd")]
        s_conv, s_conved, s_silu, s_pad = sem("s_conv"), sem("s_conved"), sem("s_silu"), sem("s_pad")
        s_ea, s_pexp, s_wd, s_w, s_D, s_P, s_C = (sem(n) for n in ("s_ea", "s_pexp", "s_wd", "s_w", "s_D", "s_P", "s_C"))
        s_cbm, s_tr, s_trB, s_Bev, s_xdt, s_xdtw = (sem(n) for n in ("s_cbm", "s_tr", "s_trB", "s_Bev", "s_xdt", "s_xdtw"))
        s_y, s_yev, s_st, s_S1, s_S2, s_gate = (sem(n) for n in ("s_y", "s_yev", "s_st", "s_S1", "s_S2", "s_gate"))

        l_landed, l_mm, l_ev, l_scr, t_landed = (sem(n) for n in ("l_landed", "l_mm", "l_ev", "l_scr", "t_landed"))
        uv_landed, a_cneg, a_const = sem("uv_landed"), sem("a_cneg"), sem("a_const")
        d_raw, d_kx, d_cen, d_kc, d_sq, d_ss, d_rs, d_bc = (sem("d_" + n) for n in ("raw", "index_k_raw", "cen", "index_k_centred", "sq", "ss", "rs", "bc"))
        d_mul, d_hi, d_ql, d_kv, d_kn, d_dup, d_tr, d_trev = (sem("d_" + n) for n in ("mul", "hi", "ql", "kv", "index_k", "dup", "tr", "trev"))
        d_tile, d_ix, d_relu, d_acc = sem("d_tile"), sem("d_ix"), sem("d_relu"), sem("d_acc")
        a_log, a_max, a_exp, a_rec, a_nrm, a_tr, a_pt, a_pv, a_ol, a_uv, a_o = (sem("a_" + n) for n in (
            "log", "max", "exp", "rec", "nrm", "tr", "probs_T", "pv", "ol", "uv", "o"))
        k_top, k_mask, k_causal = sem("k_top"), sem("k_mask"), sem("k_causal")
        T1 = 25 + XT if "mix0" in STAGES else 0

        wg, wu, wd = a["ffn_w_gate"], a["ffn_w_up"], a["ffn_w_down"]
        w_in, w_out = a["hy_w_in"][0], a["hy_w_out"][0]
        GB_B, GB_N, GB_CB, GB_SN, GB_Q, GB_KV, GB_CW = 48, 52, 60, 72, 80, 82, 128

        block = ctx.enter_context(nc.Block())

        @block.sync
        def _(sp):
            def load(n, i, srcs):
                if n >= SLOTS or not isinstance(i, int):
                    sp.wait_ge(lo_ready, n - SLOTS + 1 + 4 * i)
                for dst, src in srcs:
                    sp.dma_start(dst, src).then_inc(raw_landed[n % SLOTS], 16)

            def slot(n, kt=KT, c=P):
                return w_raw[:, n % SLOTS, 0:kt * c].rearrange("p (k n) -> p k n", k=kt)

            def kp(w):
                return w.rearrange("(k p) n -> p k n", p=P)

            def columns(n, w, c0, tiles, kt=KT):
                with sp.Fori(0, tiles // 4) as i:
                    for j in range(4):
                        load(n + j, i, [(slot(n + j, kt), w[:, :, bass.ds(i * (4 * P) + (c0 + j * P), P)])])
                return n + tiles

            with nc.allow_non_contiguous_dma(reason="a few hundred parameters, one number each"):
                sp.dma_start(x_in[:, :, :], a["x"][0].rearrange("(t p) d -> p t d", p=P)).then_inc(x_landed, 16)
                rows = [(0, 0, a["ffn_norm_g"].rearrange("l a (k p) -> (l a k) p", p=P), 32),
                        (0, 32, a["mix_norm_g"].rearrange("l (k p) -> (l k) p", p=P), 16),
                        (0, GB_B, a["gla_b_gate"].rearrange("l (k p) -> (l k) p", p=P), 4),
                        (0, GB_N, a["gla_norm_g"].rearrange("l (k p) -> (l k) p", p=P), 8),
                        (0, GB_CB, a["ssd_conv_b"].rearrange("l (k p) -> (l k) p", p=P), 12),
                        (0, GB_SN, a["ssd_norm_g"].rearrange("l (k p) -> (l k) p", p=P), 8),
                        (0, GB_Q, a["dsa_q_norm_g"].rearrange("l (k p) -> (l k) p", p=P), 2),
                        (0, GB_KV, a["dsa_kv_norm_g"], 1),
                        (1, 0, a["ssd_conv_w"].rearrange("l w (k p) -> (l w k) p", p=P), 48)]
                for c, r, src, cnt in rows:
                    sp.dma_start(prow[r:r + cnt, c, :], src).then_inc(par_landed, 16)

            def column_params():
                dv = a["ssd_d"].rearrange("l (t two) -> (l two) t", two=2)
                for h in range(2):
                    sp.dma_start(pcols[h * 64:(h + 1) * 64, 0:8], dv[h:h + 1, :].to_broadcast([64, 8])).then_inc(cols_landed, 16)
                sp.dma_start(pcols[DT0:DT0 + SH, 8:9], a["ssd_dt_bias"].rearrange("l h -> h l")).then_inc(cols_landed, 16)
                sp.dma_start(pcols[DT0:DT0 + SH, 9:10], a["ssd_a_log"].rearrange("l h -> h l")).then_inc(cols_landed, 16)
                sp.dma_start(pcols[0:IDIM, 11:12], a["idx_ln_g"].rearrange("l h -> h l")).then_inc(cols_landed, 16)
                sp.dma_start(pcols[0:IDIM, 12:13], a["idx_ln_b"].rearrange("l h -> h l")).then_inc(cols_landed, 16)
                sp.dma_start(rel_bias_sb[:, :], a["rel_bias"]).then_inc(l_landed, 16)
                sp.dma_start(bucket_sb[:, :], a["bucket_onehot"]).then_inc(l_landed, 16)
            for st in STAGES:
                n = UB[st]
                if st.startswith("ffn"):
                    q = int(st[3])
                    g_src, u_src, d_src = (kp(w[q // 2, q % 2]) for w in (wg, wu, wd))
                    for f0, nf in PHASES:
                        first = n == 0
                        if first:
                            for j in range(4):
                                load(j, 0, [(slot(j), (g_src, u_src)[j % 2][:, :, (j // 2) * P:(j // 2 + 1) * P])])
                            with nc.allow_non_contiguous_dma(reason="a few parameters, one number each"):
                                column_params()
                        with sp.Fori(1 if first else 0, nf // 2) as i:
                            for j in range(4):
                                src = (g_src, u_src)[j % 2]
                                load(n + j, i, [(slot(n + j), src[:, :, bass.ds(i * (2 * P) + (f0 + j // 2) * P, P)])])
                        n = columns(n + 2 * nf, d_src[:, f0:f0 + nf, :], 0, KT, nf)
                elif st == "mix0":
                    w = kp(w_in)
                    s0 = slot(n)
                    load(n, 0, [(s0[:, :, 0:64], w[:, :, HY_G:HY_G + 64]),
                                (s0[:, :, DT0:DT0 + SH], w[:, :, HY_DT:HY_DT + SH]),
                                (s0[:, :, DT0 + SH:P], w[:, :, HY_Z:HY_Z + P - DT0 - SH])])
                    n = columns(n + 1, w, HY_Q, 8 + 2 * GVT)
                    wo = kp(w_out)
                    n = columns(n, wo[:, 0:KT, :], 0, KT)
                    n = columns(n, w, HY_XBC, XT)
                    n = columns(n, w, HY_Z, SI // P)
                    n = columns(n, wo[:, KT:2 * KT, :], 0, KT)
                else:
                    dkv, iw, ww = kp(a["dsa_w_dkv"][0]), kp(a["idx_w_k"][0]), kp(a["idx_w_w"][0])
                    for j in range(2):
                        load(n + j, 0, [(slot(n + j), kp(a["dsa_w_dq"][0])[:, :, j * P:(j + 1) * P])])
                    load(n + 2, 0, [(slot(n + 2), dkv)])
                    s0 = slot(n + 3)
                    load(n + 3, 0, [(s0[:, :, 0:IDIM], iw), (s0[:, :, IDIM:IDIM + IH], ww), (s0[:, :, IDIM + IH:P], dkv[:, :, IDIM + IH:P])])
                    for j in range(2):
                        load(n + 4 + j, 0, [(slot(n + 4 + j, 2, 512), kp(a["idx_w_q"][0])[:, :, j * 512:(j + 1) * 512])])
                    for j in range(4):
                        load(n + 6 + j, 0, [(slot(n + 6 + j, 2, 512), kp(a["dsa_w_uq"][0])[:, :, j * 512:(j + 1) * 512])])
                    n = columns(n + 10, kp(a["dsa_w_o"][0]), 0, KT)
            sp.wait_ge(x_upd, xn)
            sp.dma_start(gfin[:, :], a["final_norm_g"].rearrange("(o n) -> o n", o=1).to_broadcast([P, D])).then_inc(gfin_landed, 16)
            for t in range(TT):
                sp.wait_ge(fin_ready, 2 * t + 2)
                sp.dma_start(out[0, t * P:(t + 1) * P, :], otile[:, t % 2, :]).then_inc(stored[t % 2], 16)
            sp.wait_ge(stored[0], 32)
            sp.wait_ge(stored[1], 32)

        @block.gpsimd
        def _(pool):
            pool.memset(ones[:, :], 1.0).then_inc(consts_ready, 1)
            pool.memset(ident[:, :], 0.0).then_inc(consts_ready, 1)
            pool.iota(ij[:, 0, :], pattern=[[1, P]], base=0, channel_multiplier=0).then_inc(iota_ready, 1)
            pool.iota(ij[:, 1, :], pattern=[[0, P]], base=0, channel_multiplier=1).then_inc(iota_ready, 1)
            pool.wait_ge(consts_ready, 2)
            pool.affine_select(out=ident[:, :], in_=ident[:, :], compare_op=ALU.not_equal, fill=1.0,
                               base=0, pattern=[[-1, P]], channel_multiplier=1).then_inc(consts_ready, 1)
            pool.wait_ge(l_ev, 2)
            pool.wait_ge(x_upd, 2 * KT)
            pool.dma_start(line_dram, line[:, :].rearrange("h (o c) -> h o c", o=1).to_broadcast([AH, P, LINE])).then_inc(l_scr, 16)
            if "mix0" in STAGES:
                pool.wait_ge(x_upd, XB["mix0"])
                pool.dma_start(small[0:GRANK, :], a["gla_w_gate2"][0]).then_inc(wg2_landed, 16)
                pool.memset(gla_attn[:, :, :, :], 0.0).then_inc(g_zero, 1)
                pool.wait_ge(s_acum, TT)
                pool.dma_start(acum_dram, dt_tmp[DT0:DT0 + SH, 2, :]).then_inc(s_scr, 16)
                pool.wait_ge(s_scr, 16)
                pool.wait_ge(x_upd, XB["mix0"] + KT)
                pool.memset(conv_in[:, :, 0:3], 0.0).then_inc(s_pad, 1)
                for c in range(TT):
                    if c >= 2:
                        pool.wait_ge(s_y, c - 1)
                    pool.dma_start(acum_rows[:, c % 2, :, :],
                                   acum_dram[:, c * P:(c + 1) * P].rearrange("(o h) t -> o h t", o=1).to_broadcast([P, SH, P])
                                   ).then_inc(s_acb[c % 2], 16)

            if "mix1" in STAGES:
                pool.wait_ge(x_upd, XB["ffn1"] if "mix0" in STAGES else KT)
                pool.wait_ge(l_scr, 16)
                lines = bass.AP(tensor=line_dram.tensor, offset=P - 1, ap=[[LINE - 1, P], [P * LINE, AH], [1, TOK]])
                pool.dma_start(bias_rows[:, :, :], lines).then_inc(t_landed, 16)
                pool.dma_start(w_uv_sb[:, :, :], a["dsa_w_uv"][0].rearrange("h c d -> c h d")).then_inc(uv_landed, 16)
                pool.memset(causal_neg[:, :], 0.0).then_inc(a_cneg, 1)
                pool.wait_ge(a_cneg, 1)
                pool.affine_select(out=causal_neg[:, :], in_=causal_neg[:, :], compare_op=ALU.is_ge, fill=MASKED,
                                   base=0, pattern=[[-1, P]], channel_multiplier=1).then_inc(a_cneg, 1)
                pool.wait_ge(d_kn, 2)
                pool.dma_start(index_k[IDIM:2 * IDIM, :], index_k[0:IDIM, :]).then_inc(d_dup, 16)
                for r in range(TT * AH):
                    w = P * (r // AH + 1)
                    pool.wait_ge(a_rec, r + 1)
                    q = r % RING
                    pool.tensor_scalar(probs[:, q, 0:w], probs[:, q, 0:w], stat[:, 2, q:q + 1], 1.0,
                                       ALU.mult, ALU.mult).then_inc(a_nrm, 1)

        @block.scalar
        def _(act):
            def produce_hi(n, i=0):
                if n >= NUNITS:
                    return
                s = n % SLOTS
                act.wait_ge(raw_landed[s], LAND[n] + 16 * i)
                if n >= SLOTS:
                    act.wait_ge(unit_used, n - SLOTS + 1 + 4 * i)
                act.activation(w_hi[:, s, :], w_raw[:, s, :], ACT.Copy).then_inc(hi_ready, 1)

            def next_x(st, xc, m):
                act.wait_ge(x_upd, xc + m + 1)
                if st in GAIN:
                    act.activation(h_hi[:, m, :], x[:, m, :], ACT.Copy,
                                   scale=gains[:, GAIN[st] + m:GAIN[st] + m + 1]).then_inc(ohi_done, 1)
                if m >= 3:
                    act.wait_ge(sq_added, (KT - 1) * XNORM[st] + m - 2)
                act.activation(sq[:, m % 2 if m else 3, :], x[:, m, :], ACT.Square).then_inc(sq_ready, 1)

            def rms_out(st):
                act.wait_ge(bc_done, NORMS[st] + 1)
                act.activation(rms_rows[:, :], ps[:, SPREAD_BANK(st), :], ACT.Copy).then_inc(rb_ready, 1)

            def operand_hi(e, dst):
                for d in range(KT):
                    act.wait_ge(omul_done, GATED[e] + d + 1)
                    act.activation(dst[:, d, :], sq[:, d % 4, :], ACT.Copy).then_inc(ohi_done, 1)

            def ffn(st, nxt):
                n, fb = UB[st], FT * int(st[3])
                fb = FT * [s for s in STAGES if s.startswith("ffn")].index(st)
                for ph, (f0, nf) in enumerate(PHASES):
                    def pair(i):
                        for j in range(2):
                            produce_hi(n + 2 * j + SLOTS, i)
                            if ph == 0 and j == 0 and isinstance(i, int):
                                rms_out(st)
                            act.wait_ge(gate_scaled, fb + f0 + 2 * i + j + 2)
                            act.activation(silu_gate[:, j, :], silu_gate[:, j, :], ACT.Silu).then_inc(silu_done, 1)
                            produce_hi(n + 2 * j + 1 + SLOTS, i)
                    if ph == 0:
                        pair(0)
                    with act.Fori(ph == 0, nf // 2) as i:
                        pair(i)
                    n += 2 * nf
                    if ph < 2:
                        with act.Fori(0, 2) as i:
                            for j in range(4):
                                produce_hi(n + j + SLOTS, i)
                    else:
                        for m in range(KT):
                            produce_hi(n + m + SLOTS)
                            next_x(nxt, XB[st] + 2 * KT, m)
                    n += KT

            def mix0(nxt):
                n = UB["mix0"]
                act.wait_ge(cols_landed, 16 * 6)
                produce_hi(n + SLOTS)
                rms_out("mix0")
                for t in range(1, 4):
                    produce_hi(n + t + SLOTS)
                act.wait_ge(g_gate_b, GH)
                g0, g1 = gla_level[:, 0, :, :], gla_level[:, 1, :, :]
                act.activation(g0, g1, ACT.Abs).then_inc(g_abs, 1)
                act.wait_ge(g_abs, 1)
                act.activation(g0, g0, ACT.Exp, scale=-1.0).then_inc(g_abs, 1)
                act.wait_ge(g_abs, 2)
                act.activation(g0, g0, ACT.Ln, bias=1.0).then_inc(g_abs, 1)
                for t in range(4, 9):
                    produce_hi(n + t + SLOTS)
                def r_gate(v):
                    produce_hi(n + 17 + v + SLOTS)
                    act.wait_ge(tile_out, 4 + 17 + v + 1)
                    act.activation(gla_gate[:, v, :], gla_gate[:, v, :], ACT.Silu).then_inc(r_silu, 1)
                for s in range(8):
                    produce_hi(n + 9 + s + SLOTS)
                    if s < LEVELS:
                        act.wait_ge(g_diff, 2 * (s + 1))
                        act.activation(gla_level[:, s % 2, :, :], gla_level[:, s % 2, :, :], ACT.Exp, scale=1.0 / GTAU).then_inc(g_exp, 1)
                act.wait_ge(g_lvl, TT * LEVELS)
                act.activation(gla_level[:, 0, :, :], gla_sums[:, :, :], ACT.Exp, scale=1.0 / GTAU).then_inc(g_dec, 1)
                act.activation(gla_chunk_decay[:, :, :], gla_sums[:, :, :].rearrange("p h (c t) -> p h c t", t=P)[:, :, :, P - 1], ACT.Exp,
                               scale=1.0 / GTAU).then_inc(g_dec, 1)
                act.wait_ge(g_decm, 1)
                act.activation(gla_level[:, 1, :, :], gla_level[:, 1, :, :], ACT.Exp, scale=1.0 / GTAU).then_inc(g_dec, 1)
                for v in range(3):
                    r_gate(v)
                R = slice(DT0, DT0 + SH)
                act.wait_ge(s_dta, 1)
                act.activation(dt_tmp[R, 0, :], small[R, :], ACT.Abs).then_inc(s_dt, 1)
                act.wait_ge(s_dt, 1)
                act.activation(dt_tmp[R, 0, :], dt_tmp[R, 0, :], ACT.Exp, scale=-1.0).then_inc(s_dt, 1)
                act.wait_ge(s_dt, 2)
                act.activation(dt_tmp[R, 0, :], dt_tmp[R, 0, :], ACT.Ln, bias=1.0).then_inc(s_dt, 1)
                act.activation(pcols[R, 10:11], pcols[R, 9:10], ACT.Exp).then_inc(s_dt, 1)
                for c in range(TT):
                    act.wait_ge(g_o, c + 1)
                    if c == 0:
                        act.wait_ge(g_vt, GVT)
                    for b in range(2):
                        act.activation(gla_vT[:, 4 * b:4 * b + 4, c * P:(c + 1) * P],
                                       ps[:, 2 + b, :].rearrange("p (m t) -> p m t", m=4), ACT.Copy).then_inc(g_oev, 1)
                    if c < TT - 1:
                        r_gate(3 + c)
                for m in range(GVT):
                    if m == 0:
                        act.wait_ge(g_oev, 2 * TT)
                    act.activation(osq[:, m // 2, m % 2, :], gla_vT[:, m, :], ACT.Square).then_inc(sq_ready, 1)
                r_gate(6)
                r_gate(7)
                operand_hi("gla", o_hi)
                n0 = UB["mix0"] + 25
                with act.Fori(0, 2) as i:
                    for j in range(4):
                        produce_hi(n0 + j + SLOTS, i)
                n0 += KT

                def conv_silu(m):
                    act.wait_ge(s_conved, m + 1)
                    act.activation(xbc[:, m, :], sq[:, m % 2, :], ACT.Silu).then_inc(s_silu, 1)

                def decays(c):
                    acum_chunk, wt = acum_rows[:, c % 2, :, :], wtok[:, c % 2, :, :]
                    act.wait_ge(s_D, c + 1)
                    act.activation(ssd_attn[:, c % 2, :, :], ssd_attn[:, c % 2, :, :], ACT.Exp).then_inc(s_pexp, 1)
                    act.wait_ge(s_wd, c + 1)
                    act.activation(wt[:, 0, :], wt[:, 0, :], ACT.Exp).then_inc(s_w, 1)
                    act.activation(wt[:, 1, :], acum_chunk[:, :, P - 1], ACT.Exp).then_inc(s_ea, 1)
                    act.wait_ge(s_ea, 2 * c + 1)
                    act.activation(acum_chunk, acum_chunk, ACT.Exp).then_inc(s_ea, 1)

                def z_gate(m):
                    act.wait_ge(z_out, m + 1)
                    act.activation(z_gate_tiles[:, m, :], z_gate_tiles[:, m, :], ACT.Silu).then_inc(z_silu, 1)
                for m in range(XT):
                    produce_hi(n0 + m + SLOTS)
                    act.wait_ge(tile_out, 4 + 25 + m + 1)
                    if m >= 2:
                        act.wait_ge(s_silu, m - 1)
                    act.activation(sq[:, m % 2, :], conv_in[:, m % 2, 0:TOK], ACT.Identity, scale=gains[:, GB_CW + m:GB_CW + m + 1],
                                   bias=gains[:, GB_CB + m:GB_CB + m + 1]).then_inc(s_tap0, 1)
                    if m:
                        conv_silu(m - 1)
                    if m == 8:
                        decays(0)
                n0 += XT
                conv_silu(XT - 1)
                produce_hi(n0 + SLOTS)
                z_gate(0)
                for c in range(TT):
                    if c < TT - 1:
                        decays(c + 1)
                    produce_hi(n0 + 2 * c + 1 + SLOTS)
                    if c < TT - 1:
                        produce_hi(n0 + 2 * c + 2 + SLOTS)
                    if c:
                        z_gate(2 * c)
                    z_gate(2 * c + 1)
                for m in range(KT):
                    act.wait_ge(s_gate, m + 1)
                    act.activation(y_hi[:, m, :], xbc[:, m, :], ACT.Copy, scale=gains[:, GB_SN + m:GB_SN + m + 1]).then_inc(ohi_done, 1)
                    act.activation(ysq[:, m, :], xbc[:, m, :], ACT.Square).then_inc(sq_ready, 1)
                n0 = UB["mix0"] + NU["mix0"] - KT
                for m in range(KT):
                    produce_hi(n0 + m + SLOTS)
                    if m == 0:
                        act.wait_ge(bc_done, NORMS["ssd"] + 1)
                        act.activation(rgrp[:, :, :], ps[:, 0:SG, :], ACT.Copy).then_inc(grp_ready, 1)
                    if m:
                        next_x(nxt, XB["mix0"] + KT, m - 1)
                next_x(nxt, XB["mix0"] + KT, KT - 1)

            def mix1(nxt):
                n = UB["mix1"]
                produce_hi(n + SLOTS)
                rms_out("mix1")
                for t in range(1, 4):
                    act.wait_ge(tile_out, 4 + T1 + t)
                    act.activation(sq[:, t - 1, :], q_latent_raw[:, t - 1, :] if t < 3 else kv_raw[:, :], ACT.Square).then_inc(d_raw, 1)
                    produce_hi(n + t + SLOTS)
                for d in range(2):
                    act.wait_ge(d_mul, d + 1)
                    act.activation(q_latent_hi[:, d, :], sq[:, d, :], ACT.Copy).then_inc(d_hi, 1)
                act.wait_ge(d_cen, 1)
                act.activation(sq[0:IDIM, 3, :], ps[0:IDIM, 1, :], ACT.Square).then_inc(d_sq, 1)
                act.activation(index_k_centred[:, :], ps[0:IDIM, 1, :], ACT.Copy).then_inc(d_kc, 1)
                act.wait_ge(d_tr, 1)
                act.activation(index_w_tok[:, :, :], ps[:, 2, 0:TT * IH].rearrange("p (c h) -> p c h", c=TT), ACT.Copy).then_inc(d_trev, 1)
                for t in range(KT + AH):
                    if t % 4 == 3:
                        act.wait_ge(unit_used, n + 4 + t // 4 + 1)
                    else:
                        act.wait_ge(d_tile, 3 * (t // 4) + t % 4 + 1)
                    dst = index_q[:, t, :] if t < KT else att_q[:, t - KT, :]
                    act.activation(dst, ps[:, 4 + (T1 + t) % 4, :], ACT.Copy,
                                   scale=1.0 if t < KT else float(AL) ** -0.5).then_inc(tile_out, 1)
                    if t % 4 == 3:
                        produce_hi(n + 4 + t // 4 + SLOTS)
                    if t == 11:
                        act.wait_ge(d_tr, 2)
                        act.activation(kvtok[:, :, :], ps[:, 0, :].rearrange("p (c d) -> p c d", c=TT), ACT.Copy).then_inc(d_trev, 1)
                for r in range((TT - 1) * IH):
                    w = P * (r // IH + 2)
                    act.wait_ge(d_ix, r + 1)
                    if r >= 4:
                        act.wait_ge(d_acc, r - 3)
                    act.activation(sq[:, r % 4, 0:w], ps[:, r % 4, 0:w], ACT.Relu).then_inc(d_relu, 1)
                NR = TT * AH

                def p_out(r):
                    w = P * (r // AH + 1)
                    act.wait_ge(a_tr, r + 1)
                    if r >= 2:
                        act.wait_ge(a_pv, r - 1)
                    act.activation(probs_T[:, r % 2, 0:w], ps[:, 2 + r % 2, 0:w], ACT.Copy).then_inc(a_pt, 1)

                def latent_out(g):
                    act.wait_ge(a_pv, 4 * g + 4)
                    if g >= 2:
                        act.wait_ge(a_uv, g - 1)
                    act.activation(o_latent[:, g % 2, :], ps[:, 4 + g % 2, :], ACT.Copy).then_inc(a_ol, 1)

                def values_out(g):
                    act.wait_ge(a_uv, g + 1)
                    b, half = g // 4, (g % 4) // 2
                    act.activation(att_out[:, 4 * half:4 * half + 4, b * P:(b + 1) * P],
                                   ps[:, 6 + half, :].rearrange("p (m t) -> p m t", m=4), ACT.Copy).then_inc(a_o, 1)
                for r in range(NR + LAG + 4):
                    if r < NR:
                        w = P * (r // AH + 1)
                        act.wait_ge(a_max, r + 1)
                        if r >= RING:
                            act.wait_ge(a_rec, r - RING + 1)
                        q = r % RING
                        act.activation(probs[:, q, 0:w], probs[:, q, 0:w], ACT.Exp, scale=-1.0, bias=stat[:, 0, q:q + 1],
                                       accum_out=stat[:, 1, q:q + 1]).then_inc(a_exp, 1)
                    if LAG <= r < NR + LAG:
                        p_out(r - LAG)
                    if r >= LAG + 2 and (r - LAG - 2) % 4 == 3 and (r - LAG - 2) // 4 < NR // 4:
                        latent_out((r - LAG - 2) // 4)
                    if r >= LAG + 3 and (r - LAG - 3) % 8 == 7 and (r - LAG - 3) // 4 < NR // 4:
                        values_out((r - LAG - 3) // 4)
                    if EARLY <= r < EARLY + KT:
                        d = r - EARLY
                        act.wait_ge(a_o, 2 * (TT - 1))
                        act.activation(o_hi[:, d, 0:TOK - P], att_out[:, d, 0:TOK - P], ACT.Copy).then_inc(e_hi, 1)
                for d in range(KT):
                    if d % 4 == 0:
                        act.wait_ge(a_o, 2 * TT - 1 + d // 4)
                    act.activation(o_hi[:, d, TOK - P:TOK], att_out[:, d, TOK - P:TOK], ACT.Copy).then_inc(ohi_done, 1)
                n0 = n + NU["mix1"] - KT
                for m in range(KT):
                    produce_hi(n0 + m + SLOTS)
                    next_x(nxt, XB["mix1"], m)

            act.wait_ge(gains_ready, 2)
            produce_hi(0)
            for m in range(KT):
                next_x(STAGES[0], 0, m)
                if m in (2, 4, 6):
                    produce_hi(m // 2)
            act.wait_ge(l_mm, 1)
            act.activation(line[:, 0:TOK], ps[0:AH, 4, :], ACT.Copy).then_inc(l_ev, 1)
            act.activation(line[:, TOK:LINE], ps[0:AH, 5, 0:P], ACT.Copy).then_inc(l_ev, 1)
            for k, st in enumerate(STAGES):
                nxt = (STAGES + ["final"])[k + 1]
                if st.startswith("ffn"):
                    ffn(st, nxt)
                elif st == "mix0":
                    mix0(nxt)
                else:
                    mix1(nxt)

        @block.vector
        def _(dve):
            def produce_lo(n, i=0):
                if n >= NUNITS:
                    return
                s = n % SLOTS
                dve.wait_ge(hi_ready, n + 1 + 4 * i)
                dve.tensor_tensor(w_lo[:, s, :], w_raw[:, s, :], w_hi[:, s, :].bitcast(F32),
                                  ALU.subtract).then_inc(lo_ready, 1)

            steps = [0]

            def step(ins):
                steps[0] += 1
                ins.then_inc(rsq_steps, 1)
                dve.wait_ge(rsq_steps, steps[0])

            def newton(val, y, t):
                step(dve.tensor_scalar(t.bitcast(I32), val.bitcast(I32), 1, None, ALU.logical_shift_right))
                step(dve.tensor_scalar(y.bitcast(I32), t.bitcast(I32), -1.0, float(0x5f3759df), ALU.mult, ALU.add))
                for r in range(3):
                    step(dve.scalar_tensor_tensor(out=t, in0=y, scalar=-0.5, in1=y, op0=ALU.mult, op1=ALU.mult))
                    step(dve.tensor_tensor(t, t, val, ALU.mult))
                    last = dve.scalar_tensor_tensor(out=y, in0=t, scalar=1.5, in1=y, op0=ALU.add, op1=ALU.mult)
                    if r < 2:
                        step(last)
                return last

            def rsqrt(z, c, scale, bank=2):
                dve.wait_ge(ss_done, SS[z] + (GH if z == NORMS.get("gla") else 1))
                if z:
                    dve.wait_ge(bc_done, z)
                val, y, t = rs[:, 0, 0:c], rs[:, 1, 0:c], rs[:, 2, 0:c]
                step(dve.tensor_scalar(val, ps[:, bank, 0:c], scale, EPS, ALU.mult, ALU.add))
                newton(val, y, t).then_inc(rstd_ready, 1)

            def next_low(st, m):
                if st in GAIN:
                    dve.wait_ge(ohi_done, OPS[st] + m + 1)
                    dve.scalar_tensor_tensor(out=h_lo[:, m, :], in0=x[:, m, :], scalar=gains[:, GAIN[st] + m:GAIN[st] + m + 1],
                                             in1=h_hi[:, m, :].bitcast(F32), op0=ALU.mult, op1=ALU.subtract).then_inc(opnd_ready, 1)

            def add_square(st, m):
                if m:
                    dve.wait_ge(sq_ready, KT * NORMS[st] + m + 1)
                    if m > 1:
                        dve.wait_ge(sq_added, (KT - 1) * XNORM[st] + m - 1)
                    dve.tensor_tensor(sq[:, 3, :], sq[:, 3, :], sq[:, m % 2, :], ALU.add).then_inc(sq_added, 1)

            def add_groups(xc, n, m):
                if m == 0:
                    dve.wait_ge(grp_ready, 1)
                else:
                    dve.wait_ge(x_upd, xc + m)
                dve.wait_ge(unit_used, n + m + 1)
                for g in range(SG):
                    dve.tensor_tensor(xgrp[:, g, :], ps[:, GROUP_BANKS[m % 3] + g, :], rgrp[:, g, :], ALU.mult).then_inc(grp_steps, 1)
                dve.wait_ge(grp_steps, 3 * m + 2)
                dve.tensor_tensor(xgrp[:, 0, :], xgrp[:, 0, :], xgrp[:, 1, :], ALU.add).then_inc(grp_steps, 1)
                dve.wait_ge(grp_steps, 3 * m + 3)
                dve.tensor_tensor(x[:, m, :], x[:, m, :], xgrp[:, 0, :], ALU.add).then_inc(x_upd, 1)

            def last_updates(xc, n, scale, nxt, groups=None):
                for m in range(KT):
                    if groups:
                        groups(xc, n, m)
                    else:
                        add_x(xc, n, m // 4, m % 4, scale)
                    if m:
                        next_low(nxt, m - 1)
                        add_square(nxt, m - 1)
                    if m < KT - 1:
                        produce_lo(n + m + SLOTS)
                next_low(nxt, KT - 1)
                add_square(nxt, KT - 1)
                produce_lo(n + KT - 1 + SLOTS)
                rsqrt(NORMS[nxt], TT, 1.0 / D, SUM_BANK(nxt))

            def operand(z, o, src, bank, hi, lo, gated):
                dve.wait_ge(bc_done, z + 1)

                def low(d):
                    dve.wait_ge(ohi_done, o + d + 1)
                    dve.tensor_tensor(lo[:, d, :], sq[:, d % 4, :], hi[:, d, :].bitcast(F32),
                                      ALU.subtract).then_inc(opnd_ready, 1)
                for d in range(KT):
                    if d >= 4:
                        dve.wait_ge(opnd_ready, o + d - 3)
                    if d == KT - 2:
                        gated(KT - 1)
                    dve.wait_ge(g_gated, d + 1)
                    dve.tensor_tensor(sq[:, d % 4, :], src[:, d, :], ps[:, bank(d), :], ALU.mult).then_inc(omul_done, 1)
                    if d:
                        low(d - 1)
                low(KT - 1)

            def add_x(xc, n, i, j, scale):
                dve.wait_ge(unit_used, n + 1 + j + 4 * i)
                dve.wait_ge(x_upd, xc)
                xt = x[:, bass.ds(4 * i + j, 1), :] if not isinstance(i, int) else x[:, 4 * i + j:4 * i + j + 1, :]
                dve.scalar_tensor_tensor(out=xt, in0=ps[:, 4 + j:5 + j, :], scalar=scale, in1=xt,
                                         op0=ALU.mult, op1=ALU.add).then_inc(x_upd, 1)

            def ffn(st, nxt):
                n = UB[st]
                fb = FT * [s for s in STAGES if s.startswith("ffn")].index(st)
                xc = XB[st]
                for ph, (f0, nf) in enumerate(PHASES):
                    f = fb + f0

                    def pair(i):
                        for j in range(2):
                            produce_lo(n + 2 * j + SLOTS, i)
                            if ph == 0 and j == 0 and isinstance(i, int):
                                dve.wait_ge(rb_ready, XNORM[st] + 1)
                            dve.wait_ge(unit_used, n + 4 * i + 2 * j + 1)
                            dve.wait_ge(mul_done, f + 2 * i + 1)
                            dve.tensor_tensor(silu_gate[:, j, :], ps[:, 2 * j, :], rms_rows[:, :], ALU.mult).then_inc(gate_scaled, 1)
                            dve.wait_ge(unit_used, n + 4 * i + 2 * j + 2)
                            dve.wait_ge(alo_done, f + 2 * i + 1)
                            dve.tensor_tensor(prod[:, j, :], ps[:, 2 * j + 1, :], rms_rows[:, :], ALU.mult).then_inc(up_scaled, 1)
                            dve.wait_ge(up_scaled, f + 2 * i + j + 1)
                            dve.wait_ge(silu_done, f + 2 * i + j + 2)
                            dve.tensor_tensor(prod[:, j, :], silu_gate[:, j, :], prod[:, j, :], ALU.mult).then_inc(mul_done, 1)
                            dve.wait_ge(mul_done, f + 2 * i + j + 2)
                            dve.tensor_copy(act_hi[:, bass.ds(2 * i + j, 1), :], prod[:, j:j + 1, :]).then_inc(ahi_done, 1)
                            dve.wait_ge(ahi_done, f + 2 * i + j + 1)
                            dve.tensor_tensor(act_lo[:, bass.ds(2 * i + j, 1), :], prod[:, j:j + 1, :],
                                              act_hi[:, bass.ds(2 * i + j, 1), :].bitcast(F32), ALU.subtract).then_inc(alo_done, 1)
                            produce_lo(n + 2 * j + 1 + SLOTS, i)
                    if ph == 0:
                        pair(0)
                    with dve.Fori(ph == 0, nf // 2) as i:
                        pair(i)
                    n += 2 * nf
                    if ph < 2:
                        with dve.Fori(0, 2) as i:
                            for j in range(4):
                                add_x(xc, n, i, j, 0.5)
                                produce_lo(n + j + SLOTS, i)
                    else:
                        last_updates(xc, n, 0.5, nxt)
                    n += KT
                    xc += KT

            def mix0(nxt):
                n = UB["mix0"]
                dve.wait_ge(cols_landed, 16 * 6)

                def tile(t, dst, scale=None):
                    u = n + t + (KT if t >= 25 else 0)
                    dve.wait_ge(unit_used, u + 1)
                    src = ps[0:dst.shape[0], 4 + t % 4, :]
                    if scale is None:
                        dve.tensor_tensor(dst, src, rms_rows[0:dst.shape[0], :], ALU.mult).then_inc(tile_out, 1)
                    else:
                        dve.scalar_tensor_tensor(out=dst, in0=src, scalar=scale, in1=rms_rows[:, :], op0=ALU.mult,
                                                 op1=ALU.mult).then_inc(tile_out, 1)
                R = slice(DT0, DT0 + SH)
                produce_lo(n + SLOTS)
                dve.wait_ge(rb_ready, XNORM["mix0"] + 1)
                dve.wait_ge(unit_used, n + 1)
                dve.tensor_tensor(sq[0:GRANK, 0, :], ps[0:GRANK, 4, :], rms_rows[0:GRANK, :], ALU.mult).then_inc(g_glr, 1)
                dve.tensor_tensor(small[R, :], ps[R, 4, :], rms_rows[R, :], ALU.mult).then_inc(tile_out, 1)

                def gate_sums():
                    g1 = gla_level[:, 1, :, :]
                    dve.wait_ge(g_abs, 3)
                    dve.scalar_tensor_tensor(out=g1, in0=g1, scalar=0.0, in1=gla_level[:, 0, :, :], op0=ALU.min,
                                             op1=ALU.subtract).then_inc(g_scan, 1)
                    dve.wait_ge(g_scan, 1)
                    for h in range(GH):
                        for c in range(TT):
                            dve.tensor_tensor_scan(gla_sums[:, h, c * P:(c + 1) * P], ones[:, :], gla_level[:, 1, h, c * P:(c + 1) * P], 0.0,
                                                   ALU.mult, ALU.add).then_inc(g_scan, 1)
                for t in range(1, 9):
                    if t == 5:
                        gate_sums()
                    produce_lo(n + t + SLOTS)
                    tile(t, gla_q[:, t - 1, :] if t < 5 else gla_k[:, t - 5, :], float(GDK) ** -0.5 if t < 5 else None)
                    if t == 3:
                        for h in range(GH):
                            dve.wait_ge(g_gate_mm, h + 1)
                            dve.tensor_scalar(gla_level[:, 1, h, :], ps[:, h, :], gains[:, GB_B + h:GB_B + h + 1], None,
                                              ALU.add).then_inc(g_gate_b, 1)
                dve.wait_ge(g_scan, 1 + GH * TT)

                def level(m, s):
                    return m.rearrange("p h t -> p (h t)").rearrange("p (n two s) -> p n two s", two=2, s=s)

                def diff(l):
                    s = 1 << (LEVELS - 1 - l)
                    b4, m4 = level(gla_sums[:, :, :], s), level(gla_level[:, l % 2, :, :], s)
                    ref = b4[:, :, 0, s - 1:s].to_broadcast([P, GH * TOK // (2 * s), s])
                    if l >= 2:
                        dve.wait_ge(g_lvl, TT * (l - 1))
                    dve.tensor_tensor(m4[:, :, 0, :], ref, b4[:, :, 0, :], ALU.subtract).then_inc(g_diff, 1)
                    dve.tensor_tensor(m4[:, :, 1, :], b4[:, :, 1, :], ref, ALU.subtract).then_inc(g_diff, 1)

                def mult(l):
                    s = 1 << (LEVELS - 1 - l)
                    m4 = level(gla_level[:, l % 2, :, :], s)
                    dve.wait_ge(g_exp, l + 1)
                    dve.tensor_tensor(m4[:, :, 0, :], m4[:, :, 0, :], level(gla_k[:, :, :], s)[:, :, 0, :], ALU.mult).then_inc(g_mul, 1)
                    dve.tensor_tensor(m4[:, :, 1, :], m4[:, :, 1, :], level(gla_q[:, :, :], s)[:, :, 1, :], ALU.mult).then_inc(g_mul, 1)

                def masked(l):
                    for c in range(TT):
                        dve.wait_ge(g_lvl, TT * l + c + 1)
                        if l:
                            dve.wait_ge(g_mask, TT * (l - 1) + c + 1)
                        dve.copy_predicated(gla_attn[:, c, :, :], masks[:, l:l + 1, :].to_broadcast([P, GH, P]),
                                            ps[:, c, :].rearrange("p (h t) -> p h t", h=GH)).then_inc(g_mask, 1)

                def v_out(v):
                    dve.wait_ge(g_vt, v + 1)
                    dve.tensor_copy(gla_v[:, :, v * P:(v + 1) * P], ps[:, 4 + (9 + 4 + v // 2 + 1 + v % 2) % 4, :].rearrange("p (c d) -> p c d", c=TT)).then_inc(g_vev, 1)
                dve.wait_ge(g_zero, 1)
                def r_tile(v):
                    tile(17 + v, gla_gate[:, v, :])
                    produce_lo(n + 17 + v + SLOTS)
                for s in range(8):
                    if s < LEVELS:
                        diff(s)
                    produce_lo(n + 9 + s + SLOTS)
                    tile(9 + s, gla_vT[:, s, :])
                    if s >= 4:
                        v_out(2 * (s - 4))
                        v_out(2 * (s - 4) + 1)
                    if s < LEVELS:
                        mult(s)
                    if s:
                        masked(s - 1)
                dve.wait_ge(g_mul, 2 * LEVELS)
                b3 = gla_sums[:, :, :].rearrange("p h (c t) -> p (h c) t", t=P)
                m3 = gla_level[:, 1, :, :].rearrange("p h (c t) -> p (h c) t", t=P)
                dve.wait_ge(g_lvl, TT * LEVELS)
                dve.tensor_tensor(m3, b3[:, :, P - 1:P].to_broadcast([P, GH * TT, P]), b3, ALU.subtract).then_inc(g_decm, 1)
                r_tile(0)
                masked(LEVELS)
                dve.wait_ge(g_dec, 1)
                dve.tensor_tensor(gla_q[:, :, :], gla_q[:, :, :], gla_level[:, 0, :, :], ALU.mult).then_inc(g_decm, 1)
                r_tile(1)
                dve.wait_ge(g_dec, 3)
                dve.tensor_tensor(gla_k[:, :, :], gla_k[:, :, :], gla_level[:, 1, :, :], ALU.mult).then_inc(g_decm, 1)
                r_tile(2)
                dve.wait_ge(g_decm, 3)
                for c in range(TT):
                    dve.wait_ge(g_kt, c + 1)
                    dve.tensor_copy(gla_k_turned[:, c, :, :], ps[:, c, :].rearrange("p (h k) -> p h k", h=GH)).then_inc(g_kev, 1)
                dve.wait_ge(tile_out, 5)
                dve.tensor_scalar(small[R, :], small[R, :], pcols[R, 8:9], None, ALU.add).then_inc(s_dta, 1)
                def dt_sums():
                    dve.wait_ge(s_dt, 4)
                    dve.scalar_tensor_tensor(out=small[R, :], in0=small[R, :], scalar=0.0, in1=dt_tmp[R, 0, :],
                                             op0=ALU.max, op1=ALU.add).then_inc(s_dta, 1)
                    dve.wait_ge(s_dta, 2)
                    dve.tensor_scalar(dt_tmp[R, 1, :], small[R, :], pcols[R, 10:11], -1.0, ALU.mult, ALU.mult).then_inc(s_dta, 1)
                    dve.wait_ge(s_dta, 3)
                    for c in range(TT):
                        dve.tensor_tensor_scan(dt_tmp[R, 2, c * P:(c + 1) * P], ones[R, :], dt_tmp[R, 1, c * P:(c + 1) * P], 0.0,
                                               ALU.mult, ALU.add).then_inc(s_acum, 1)
                for c in range(TT - 1):
                    for h in range(GH):
                        dve.wait_ge(g_st, GH * c + 2 * (h // 2) + 2)
                        src = ps[:, h // 2, (h % 2) * GDV:(h % 2 + 1) * GDV]
                        if c == 0:
                            dve.tensor_copy(gla_state[:, h, :], src).then_inc(g_S, 1)
                        else:
                            dve.wait_ge(g_o, c + 1)
                            dve.wait_ge(g_S, GH * (c - 1) + h + 1)
                            dve.scalar_tensor_tensor(out=gla_state[:, h, :], in0=gla_state[:, h, :], scalar=gla_chunk_decay[:, h, c:c + 1], in1=src,
                                                     op0=ALU.mult, op1=ALU.add).then_inc(g_S, 1)
                    if c == 0:
                        dt_sums()
                    r_tile(3 + c)
                dve.wait_ge(s_tok, 1)
                dve.tensor_copy(toks[:, :, :, :], ps[:, 0, 0:2 * TT * SH].rearrange("p (a c h) -> p a c h", a=2, c=TT)).then_inc(s_tokev, 1)
                z = NORMS["gla"]
                for h in range(0, GH, 2):
                    dve.wait_ge(sq_ready, KT * z + 2 * h + 4)
                    dve.tensor_tensor(osq[:, h:h + 2, 0, :], osq[:, h:h + 2, 0, :], osq[:, h:h + 2, 1, :], ALU.add).then_inc(sq_paired, 1)
                r_tile(6)

                def gated(m):
                    dve.wait_ge(sq_ready, KT * z + m + 1)
                    dve.wait_ge(r_silu, m + 1)
                    dve.scalar_tensor_tensor(out=gla_vT[:, m, :], in0=gla_vT[:, m, :], scalar=gains[:, GB_N + m:GB_N + m + 1],
                                             in1=gla_gate[:, m, :], op0=ALU.mult, op1=ALU.mult).then_inc(g_gated, 1)
                for m in range(4):
                    gated(m)
                rsqrt(z, GH * TT, 1.0 / GDV)
                for m in range(4, GVT - 1):
                    gated(m)
                r_tile(7)
                operand(z, OPS["gla"], gla_vT, lambda d: d // 2, o_hi, o_lo, gated)
                n0 = n + 25
                with dve.Fori(0, 2) as i:
                    for j in range(4):
                        add_x(XB["mix0"], n0, i, j, 1.0)
                        produce_lo(n0 + j + SLOTS, i)
                n0 += KT
                acum_tok, dt_tok = toks[:, 1, :, :], toks[:, 0, :, :]
                hg = SH // SG

                def by_head(t):
                    return t.rearrange("p (h d) -> p h d", h=SH)

                def over_width(w):
                    return w.rearrange("p (h o) -> p h o", o=1).to_broadcast([P, SH, SHD])

                def gaps(c):
                    dve.wait_ge(s_acb[c % 2], 16 * (c // 2 + 1))
                    acum_chunk = acum_rows[:, c % 2, :, :]
                    for h in range(SH):
                        ins = dve.tensor_scalar(ssd_attn[:, c % 2, h, :], acum_chunk[:, h, :], acum_tok[:, c, h:h + 1], 0.0, ALU.subtract, ALU.min)
                    ins.then_inc(s_D, 1)
                    dve.tensor_tensor(wtok[:, c % 2, 0, :], acum_chunk[:, :, P - 1], acum_tok[:, c, :], ALU.subtract).then_inc(s_wd, 1)

                def from_start(c):
                    dve.wait_ge(s_ea, 2 * c + 2)
                    for g in range(SG):
                        ce = acum_rows[:, c % 2, g * hg:(g + 1) * hg, :]
                        dve.tensor_tensor(ce, ce, xbc[:, 10 + g:11 + g, c * P:(c + 1) * P].to_broadcast([P, hg, P]), ALU.mult).then_inc(s_C, 1)

                def z_tile(m):
                    dve.wait_ge(unit_used, n0 + m + 1)
                    dve.tensor_tensor(z_gate_tiles[:, m, :], ps[:, Z_BANKS[m % 3], :], rms_rows[:, :], ALU.mult).then_inc(z_out, 1)

                def taps(m):
                    cv = sq[:, m % 2, :]
                    dve.wait_ge(s_tap0, m + 1)
                    for k in range(1, TAPS):
                        if k > 1:
                            dve.wait_ge(s_conv, (TAPS - 2) * m + k - 1)
                        dve.scalar_tensor_tensor(out=cv, in0=conv_in[:, m % 2, k:k + TOK],
                                                 scalar=gains[:, GB_CW + XT * k + m:GB_CW + XT * k + m + 1],
                                                 in1=cv, op0=ALU.mult, op1=ALU.add).then_inc(s_conv if k < TAPS - 1 else s_conved, 1)
                dve.wait_ge(s_pad, 1)
                for m in range(XT):
                    if m >= 2:
                        dve.wait_ge(s_conved, m - 1)
                    tile(25 + m, conv_in[:, m % 2, 3:3 + TOK])
                    if m:
                        taps(m - 1)
                    produce_lo(n0 + m + SLOTS)
                    if m == 6:
                        gaps(0)
                taps(XT - 1)
                n0 += XT
                z_tile(0)
                produce_lo(n0 + SLOTS)
                dve.wait_ge(s_silu, XT)
                from_start(0)
                for c in range(TT):
                    wt, pmc = wtok[:, c % 2, :, :], ssd_attn[:, c % 2, :, :]
                    dve.wait_ge(s_trB, c + 1)
                    dve.tensor_tensor(ssd_CB[:, :, :], ps[:, 0, 0:SG * P].rearrange("p (g t) -> p g t", g=SG),
                                      tri[:, :].rearrange("p (o t) -> p o t", o=1).to_broadcast([P, SG, P]), ALU.mult).then_inc(s_cbm, 1)
                    if c < TT - 1:
                        dve.tensor_copy(ssd_B[:, :, :], ps[:, 0, SG * P:2 * SG * P].rearrange("p (g n) -> p g n", g=SG)).then_inc(s_Bev, 1)
                    dve.wait_ge(s_tr, c + 1)
                    dve.tensor_tensor(by_head(xdt[:, :]), ps[:, 2:4, :].rearrange("p b (h d) -> p (b h) d", d=SHD),
                                      over_width(dt_tok[:, c, :]), ALU.mult).then_inc(s_xdt, 1)
                    dve.wait_ge(s_w, c + 1)
                    dve.wait_ge(s_xdt, c + 1)
                    if c < TT - 1:
                        dve.tensor_tensor(by_head(xdtw[:, :]), by_head(xdt[:, :]), over_width(wt[:, 0, :]), ALU.mult).then_inc(s_xdtw, 1)
                    dve.wait_ge(s_pexp, c + 1)
                    dve.wait_ge(s_cbm, c + 1)
                    for g in range(SG):
                        dve.tensor_tensor(pmc[:, g * hg:(g + 1) * hg, :], pmc[:, g * hg:(g + 1) * hg, :],
                                          ssd_CB[:, g:g + 1, :].to_broadcast([P, hg, P]), ALU.mult).then_inc(s_P, 1)
                    if c < TT - 1:
                        gaps(c + 1)
                    if c:
                        z_tile(2 * c)
                        if c < TT - 1:
                            produce_lo(n0 + 2 * c + SLOTS)
                    z_tile(2 * c + 1)
                    if c == TT - 1:
                        dve.wait_ge(s_yev, c)
                        for m in range(SI // P):
                            dve.wait_ge(z_silu, m + 1)
                            ins = dve.tensor_tensor(xbc[:, m, 0:c * P], xbc[:, m, 0:c * P], z_gate_tiles[:, m, 0:c * P], ALU.mult)
                        ins.then_inc(y_gated, 1)
                    dve.wait_ge(s_y, c + 1)
                    if c < TT - 1:
                        if c:
                            dve.tensor_tensor(by_head(ssd_state[:, :]), by_head(ssd_state[:, :]), over_width(wt[:, 1, :]), ALU.mult).then_inc(s_S1, 1)
                        dve.wait_ge(s_st, c + 1)
                        new = ps[:, 2:4, :].rearrange("p b t -> p (b t)")
                        if c:
                            dve.wait_ge(s_S1, c)
                            dve.tensor_tensor(ssd_state[:, :], ssd_state[:, :], new, ALU.add).then_inc(s_S2, 1)
                        else:
                            dve.tensor_copy(ssd_state[:, :], new).then_inc(s_S2, 1)
                        from_start(c + 1)
                    if c == TT - 1:
                        break
                    for m in range(SI // P):
                        xt = xbc[:, m, c * P:(c + 1) * P]
                        ins = dve.scalar_tensor_tensor(out=xt, in0=xt, scalar=pcols[:, m:m + 1],
                                                       in1=ps[:, 4 + m // 4, (m % 4) * P:(m % 4 + 1) * P],
                                                       op0=ALU.mult, op1=ALU.add)
                    ins.then_inc(s_yev, 1)
                    produce_lo(n0 + 2 * c + 1 + SLOTS)
                def gated_low(m):
                    dve.wait_ge(ohi_done, OPS["ssd"] + m + 1)
                    dve.scalar_tensor_tensor(out=y_lo[:, m, :], in0=xbc[:, m, :], scalar=gains[:, GB_SN + m:GB_SN + m + 1],
                                             in1=y_hi[:, m, :].bitcast(F32), op0=ALU.mult, op1=ALU.subtract).then_inc(opnd_ready, 1)
                dve.wait_ge(y_gated, 1)
                last = slice((TT - 1) * P, TOK)
                for m in range(SI // P):
                    xt = xbc[:, m, last]
                    dve.scalar_tensor_tensor(out=xt, in0=xt, scalar=pcols[:, m:m + 1], in1=ps[:, 4 + m // 4, (m % 4) * P:(m % 4 + 1) * P],
                                             op0=ALU.mult, op1=ALU.add).then_inc(s_yev, 1)
                    dve.wait_ge(s_yev, TT + m)
                    dve.tensor_tensor(xt, xt, z_gate_tiles[:, m, last], ALU.mult).then_inc(s_gate, 1)
                    if m:
                        gated_low(m - 1)
                gated_low(KT - 1)
                produce_lo(n0 + 2 * TT - 2 + SLOTS)
                dve.wait_ge(sq_ready, KT * (NORMS["ssd"] + 1))
                for w in (2, 1):
                    if w == 1:
                        dve.wait_ge(sq_tree, SG)
                    for g in range(SG):
                        lo = ysq[:, 4 * g:4 * g + w, :]
                        dve.tensor_tensor(lo, lo, ysq[:, 4 * g + w:4 * g + 2 * w, :], ALU.add).then_inc(sq_tree, 1)
                produce_lo(n0 + 2 * TT - 1 + SLOTS)
                rsqrt(NORMS["ssd"], SG * TT, 1.0 / (SI // SG), 1)
                last_updates(XB["mix0"] + KT, n + NU["mix0"] - KT, 1.0, nxt, add_groups)

            def mix1(nxt):
                n = UB["mix1"]
                dve.wait_ge(a_cneg, 2)
                dve.tensor_copy(identr[:, :], ident[:, :]).then_inc(a_const, 1)
                dve.tensor_scalar(cmat[:, :], ident[0:IDIM, 0:IDIM], 1.0 / IDIM, None, ALU.subtract).then_inc(a_const, 1)

                def latent_rms(i, bank, cols):
                    dve.wait_ge(d_ss, i)
                    lo, hi = cols[0][0], cols[-1][0] + TT
                    for c, width in cols:
                        step(dve.tensor_scalar(rs[:, 0, c:c + TT], ps[:, bank, c:c + TT], 1.0 / width, EPS, ALU.mult, ALU.add))
                    newton(rs[:, 0, lo:hi], rs[:, 1, lo:hi], rs[:, 2, lo:hi]).then_inc(d_rs, 1)
                for t in range(4):
                    if t == 3:
                        latent_rms(1, 2, ((0, AQR),))
                    produce_lo(n + t + SLOTS)
                    if t == 0:
                        dve.wait_ge(rb_ready, XNORM["mix1"] + 1)
                    dve.wait_ge(unit_used, n + t + 1)
                    b = 4 + (T1 + t) % 4
                    if t < 3:
                        dve.tensor_tensor(q_latent_raw[:, t, :] if t < 2 else kv_raw[:, :], ps[:, b, :], rms_rows[:, :], ALU.mult).then_inc(tile_out, 1)
                    else:
                        dve.tensor_tensor(index_k_raw[0:IDIM, :], ps[0:IDIM, b, :], rms_rows[0:IDIM, :], ALU.mult).then_inc(d_kx, 1)
                        W = slice(IDIM, IDIM + IH)
                        dve.scalar_tensor_tensor(out=index_k_raw[W, :], in0=ps[W, b, :], scalar=float(IH) ** -0.5 * float(IDIM) ** -0.5,
                                                 in1=rms_rows[W, :], op0=ALU.mult, op1=ALU.mult).then_inc(tile_out, 1)
                dve.wait_ge(d_bc, 1)
                for d in range(2):
                    dve.scalar_tensor_tensor(out=sq[:, d, :], in0=q_latent_raw[:, d, :], scalar=gains[:, GB_Q + d:GB_Q + d + 1],
                                             in1=ps[:, 0, :], op0=ALU.mult, op1=ALU.mult).then_inc(d_mul, 1)
                for d in range(2):
                    dve.wait_ge(d_hi, d + 1)
                    dve.tensor_tensor(q_latent_lo[:, d, :], sq[:, d, :], q_latent_hi[:, d, :].bitcast(F32), ALU.subtract).then_inc(d_ql, 1)
                latent_rms(2, 3, ((4, AL), (8, IDIM)))
                produce_lo(n + 4 + SLOTS)
                dve.wait_ge(d_bc, 2)
                dve.scalar_tensor_tensor(out=kvT[:, :], in0=kv_raw[:, :], scalar=gains[:, GB_KV:GB_KV + 1],
                                         in1=ps[:, 1, :], op0=ALU.mult, op1=ALU.mult).then_inc(d_kv, 1)
                dve.wait_ge(d_kc, 1)
                dve.scalar_tensor_tensor(out=index_k[0:IDIM, :], in0=index_k_centred[:, :], scalar=pcols[0:IDIM, 11:12],
                                         in1=ps[0:IDIM, 3, :], op0=ALU.mult, op1=ALU.mult).then_inc(d_kn, 1)
                dve.wait_ge(d_kn, 1)
                dve.tensor_scalar(index_k[0:IDIM, :], index_k[0:IDIM, :], pcols[0:IDIM, 12:13], None, ALU.add).then_inc(d_kn, 1)
                dve.wait_ge(d_kv, 1)
                dve.wait_ge(d_tr, 1)
                dve.tensor_copy(att_mask[:, 0, 0:P], causal_neg[:, :]).then_inc(k_mask, 1)
                for t in range(1, 6):
                    produce_lo(n + 4 + t + SLOTS)
                ROUNDS = TOPK // 8

                def add_causal(b):
                    last = index_scores[:, b, P * (b + 1):P * (b + 2)]
                    dve.wait_ge(d_acc, IH * (b + 1))
                    dve.tensor_tensor(last, last, causal_neg[:, :], ALU.add).then_inc(k_causal, 1)

                def select(b, i):
                    s1, top = index_scores[:, b, 0:P * (b + 2)], stat[:, 3, :]
                    n_top = 2 * (ROUNDS * b + i)
                    if i == 0:
                        dve.wait_ge(k_causal, b + 1)
                    if n_top:
                        dve.wait_ge(k_top, n_top)
                    dve.max(top, s1).then_inc(k_top, 1)
                    dve.wait_ge(k_top, n_top + 1)
                    dve.match_replace(s1, top, s1, TAKEN).then_inc(k_top, 1)
                    if i == ROUNDS - 1:
                        dve.wait_ge(k_top, n_top + 2)
                        dve.tensor_scalar(att_mask[:, b + 1, 0:P * (b + 2)], s1, TAKEN, MASKED, ALU.not_equal, ALU.mult).then_inc(k_mask, 1)
                dve.wait_ge(d_trev, 1)
                for r in range((TT - 1) * IH):
                    b, h = r // IH, r % IH
                    w = P * (b + 2)
                    dve.wait_ge(d_relu, r + 1)
                    wcol = index_w_tok[:, b + 1, h:h + 1]
                    if h == 0:
                        dve.tensor_scalar(index_scores[:, b, 0:w], sq[:, r % 4, 0:w], wcol, None, ALU.mult).then_inc(d_acc, 1)
                    else:
                        dve.wait_ge(d_acc, r)
                        dve.scalar_tensor_tensor(out=index_scores[:, b, 0:w], in0=sq[:, r % 4, 0:w], scalar=wcol, in1=index_scores[:, b, 0:w],
                                                 op0=ALU.mult, op1=ALU.add).then_inc(d_acc, 1)
                    if b and h == 0:
                        add_causal(b - 1)
                    if b == 1:
                        select(0, h)
                    if b == 2 and h % 2:
                        select(1, h // 2)
                add_causal(TT - 2)
                dve.wait_ge(t_landed, 16)
                NR = TT * AH
                for r in range(NR + 1):
                    b, h = r // AH, r % AH
                    w = P * (b + 1)
                    if r < NR:
                        dve.wait_ge(a_log, r + 1)
                        if r >= RING:
                            dve.wait_ge(a_tr, r - RING + 1)
                        dve.tensor_tensor_reduce(probs[:, r % RING, 0:w], ps[:, r % 2, 0:w], bias_rows[:, h, TOK - w:TOK], -1.0, 3e38,
                                                 ALU.add, ALU.min, stat[:, 0, r % RING:r % RING + 1]).then_inc(a_max, 1)
                        if r < 3 * ROUNDS and r % 2 == 0:
                            i = ROUNDS // 2 + r // 2
                            select(1 + i // ROUNDS, i % ROUNDS)
                    if 1 <= r <= NR:
                        q = r - 1
                        dve.wait_ge(a_exp, r)
                        if q >= RING:
                            dve.wait_ge(a_nrm, q - RING + 1)
                        q = q % RING
                        dve.reciprocal(stat[:, 2, q:q + 1], stat[:, 1, q:q + 1]).then_inc(a_rec, 1)
                    if EARLY + 1 <= r:
                        d, c = r - EARLY - 1, slice(0, TOK - P)
                        dve.wait_ge(e_hi, d + 1)
                        dve.tensor_tensor(o_lo[:, d, c], att_out[:, d, c], o_hi[:, d, c].bitcast(F32), ALU.subtract).then_inc(e_lo, 1)
                dve.wait_ge(e_lo, KT)
                for d in range(KT):
                    c = slice(TOK - P, TOK)
                    dve.wait_ge(ohi_done, OPS["dsa"] + d + 1)
                    dve.tensor_tensor(o_lo[:, d, c], att_out[:, d, c], o_hi[:, d, c].bitcast(F32), ALU.subtract).then_inc(opnd_ready, 1)
                last_updates(XB["mix1"], n + NU["mix1"] - KT, 1.0, nxt)

            dve.sem_inc(mul_done, 1)
            dve.sem_inc(alo_done, 1)
            dve.sem_inc(silu_done, 1)
            dve.sem_inc(gate_scaled, 1)
            dve.sem_inc(tile_out, 4)
            dve.wait_ge(iota_ready, 2)
            ms = [0]

            def mstep(ins):
                ms[0] += 1
                ins.then_inc(mask_steps, 1)
                dve.wait_ge(mask_steps, ms[0])
            mstep(dve.tensor_tensor(ij[:, 2, :], ij[:, 0, :], ij[:, 1, :], ALU.bitwise_xor))
            mstep(dve.tensor_tensor(tri[:, :], ij[:, 0, :], ij[:, 1, :], ALU.is_ge))
            for l in range(LEVELS):
                mstep(dve.tensor_scalar(ij[:, 3, :], ij[:, 2, :], LEVELS - 1 - l, None, ALU.logical_shift_right))
                mstep(dve.scalar_tensor_tensor(out=masks[:, l, :], in0=ij[:, 3, :], scalar=1.0, in1=tri[:, :],
                                               op0=ALU.is_equal, op1=ALU.mult))
            mstep(dve.tensor_scalar(masks[:, LEVELS, :], ij[:, 2, :], 0.0, None, ALU.is_equal))
            dve.wait_ge(par_done, 2)
            dve.wait_ge(par_landed, 16 * 9)
            dve.tensor_copy(gains[:, 0:83], ps[:, 0, 0:83]).then_inc(gains_ready, 1)
            dve.tensor_copy(gains[:, GB_CW:GB_CW + 48], ps[:, 1, 0:48]).then_inc(gains_ready, 1)
            dve.wait_ge(gains_ready, 2)
            for m in range(KT):
                dve.wait_ge(xt_done, m + 1)
                dve.tensor_copy(x[:, m, :], ps[:, 4 + m % 4, :]).then_inc(x_upd, 1)
            produce_lo(0)
            for m in range(KT):
                next_low(STAGES[0], m)
                add_square(STAGES[0], m)
                if m in (3, 5):
                    produce_lo(m // 2)
            produce_lo(SLOTS - 1)
            rsqrt(0, TT, 1.0 / D, SUM_BANK(STAGES[0]))
            for k, st in enumerate(STAGES):
                nxt = (STAGES + ["final"])[k + 1]
                if st.startswith("ffn"):
                    ffn(st, nxt)
                elif st == "mix0":
                    mix0(nxt)
                else:
                    mix1(nxt)
            dve.wait_ge(rstd_ready, NORMS["final"] + 1)
            dve.wait_ge(gfin_landed, 16)
            for t in range(TT):
                if t >= 2:
                    dve.wait_ge(stored[t % 2], 16)
                for c in range(2):
                    dve.wait_ge(fin_t, 2 * t + c + 1)
                    dve.scalar_tensor_tensor(out=otile[:, t % 2, c * 512:(c + 1) * 512], in0=ps[:, 4 + (2 * t + c) % 4, :],
                                             scalar=rs[:, 1, t:t + 1], in1=gfin[:, c * 512:(c + 1) * 512],
                                             op0=ALU.mult, op1=ALU.mult).then_inc(fin_ready, 1)

        @block.tensor
        def _(pe):
            def unit(n, bank, rh, rl, nk, i=0, ready=None):
                s = n % SLOTS
                pe.wait_ge(lo_ready, n + 1 + 4 * i)
                for k in range(nk):
                    if ready:
                        ready(k)
                    wh, wl = w_hi[:, s, k * P:(k + 1) * P], w_lo[:, s, k * P:(k + 1) * P]
                    pe.matmul(ps[:, bank, :], wh, rh[:, k, :], start=k == 0, stop=False)
                    pe.matmul(ps[:, bank, :], wh, rl[:, k, :], start=False, stop=False)
                    mm = pe.matmul(ps[:, bank, :], wl, rh[:, k, :], start=False, stop=k == nk - 1)
                mm.then_inc(unit_used, 1)

            def first_units(n, banks, st):
                o = OPS[st]

                def blocks(u, ks):
                    s = (n + u) % SLOTS
                    if ks[0] == 0:
                        pe.wait_ge(lo_ready, n + u + 1)
                    for k in ks:
                        if u == 0:
                            pe.wait_ge(opnd_ready, o + k + 1)
                        wh, wl = w_hi[:, s, k * P:(k + 1) * P], w_lo[:, s, k * P:(k + 1) * P]
                        dst = ps[:, banks[u], :]
                        pe.matmul(dst, wh, h_hi[:, k, :], start=k == 0, stop=False)
                        pe.matmul(dst, wh, h_lo[:, k, :], start=False, stop=False)
                        mm = pe.matmul(dst, wl, h_hi[:, k, :], start=False, stop=k == KT - 1)
                        if k == KT - 1:
                            mm.then_inc(unit_used, 1)
                blocks(0, range(0, 6))
                blocks(1, range(0, 4))
                blocks(0, range(6, KT))
                sumsq_x(st)
                blocks(1, range(4, KT))
                spread(NORMS[st], [SPREAD_BANK(st)])

            def sums(src, c0, bank=2):
                for t in range(TT):
                    mm = pe.matmul(ps[:, bank, c0 + t:c0 + t + 1], src[:, t * P:(t + 1) * P], ones[:, 0:1], start=True, stop=True, skip_group_check=True)
                return mm

            def sumsq_x(st):
                bank = SUM_BANK(st)
                pe.wait_ge(sq_added, (KT - 1) * (XNORM[st] + 1))
                for t in range(TT):
                    mm = pe.matmul(ps[:, bank, t:t + 1], sq[:, 3, t * P:(t + 1) * P], ones[:, 0:1], start=True, stop=True, skip_group_check=True)
                mm.then_inc(ss_done, 1)

            def spread(z, banks):
                pe.wait_ge(rstd_ready, z + 1)
                for b, bank in enumerate(banks):
                    for t in range(TT):
                        c = b * TT + t
                        mm = pe.matmul(ps[:, bank, t * P:(t + 1) * P], rs[:, 1, c:c + 1].to_broadcast([P, P]), ident[:, :],
                                       start=True, stop=True, skip_group_check=True)
                mm.then_inc(bc_done, 1)

            def ready_of(o):
                return lambda k: pe.wait_ge(opnd_ready, o + k + 1)

            def ffn(st, nxt):
                n = UB[st]
                fb = FT * [s for s in STAGES if s.startswith("ffn")].index(st)
                xc = XB[st]
                for ph, (f0, nf) in enumerate(PHASES):
                    f = fb + f0

                    def pair(i):
                        first = ph == 0 and isinstance(i, int)
                        for j in range(2):
                            pe.wait_ge(gate_scaled, f + 2 * i + 1)
                            if first and j == 0:
                                pe.wait_ge(mul_done, f + 1)
                                first_units(n, (0, 1), st)
                                continue
                            unit(n + 2 * j, 2 * j, h_hi, h_lo, KT, i)
                            pe.wait_ge(mul_done, f + 2 * i + 1)
                            unit(n + 2 * j + 1, 2 * j + 1, h_hi, h_lo, KT, i)
                    if ph == 0:
                        pair(0)
                    with pe.Fori(ph == 0, nf // 2) as i:
                        pair(i)
                    n += 2 * nf
                    pe.wait_ge(alo_done, f + nf - 2 + 1)

                    def dwait(k):
                        if k >= nf - 2:
                            pe.wait_ge(alo_done, f + k + 2)
                    if ph < 2:
                        with pe.Fori(0, 2) as i:
                            for j in range(4):
                                pe.wait_ge(x_upd, xc - 4 + j + 1 + 4 * i)
                                unit(n + j, 4 + j, act_hi, act_lo, nf, i, dwait if j == 0 else None)
                    else:
                        for m in range(KT):
                            pe.wait_ge(x_upd, xc - 4 + m + 1)
                            unit(n + m, 4 + m % 4, act_hi, act_lo, nf, 0, dwait if m == 0 else None)
                    n += KT
                    xc += KT

            def mix0(nxt):
                n = UB["mix0"]
                first_units(n, (4, 5), "mix0")
                unit(n + 2, 6, h_hi, h_lo, KT)
                unit(n + 3, 7, h_hi, h_lo, KT)
                pe.wait_ge(wg2_landed, 16)
                pe.wait_ge(g_glr, 1)
                for h in range(GH):
                    pe.matmul(ps[:, h, :], small[0:GRANK, h * P:(h + 1) * P], sq[0:GRANK, 0, :], start=True, stop=True).then_inc(g_gate_mm, 1)
                for t in range(4, 9):
                    pe.wait_ge(tile_out, t + 1)
                    unit(n + t, 4 + t % 4, h_hi, h_lo, KT)

                def level(l):
                    if l < LEVELS:
                        pe.wait_ge(g_mul, 2 * (l + 1))
                    for c in range(TT):
                        if l:
                            pe.wait_ge(g_mask, TT * (l - 1) + c + 1)
                        for h in range(GH):
                            kk = gla_level[:, l % 2, h, c * P:(c + 1) * P] if l < LEVELS else gla_k[:, h, c * P:(c + 1) * P]
                            qq = gla_level[:, l % 2, h, c * P:(c + 1) * P] if l < LEVELS else gla_q[:, h, c * P:(c + 1) * P]
                            mm = pe.matmul(ps[:, c, h * P:(h + 1) * P], kk, qq, start=True, stop=True, skip_group_check=True)
                        mm.then_inc(g_lvl, 1)
                for s in range(8):
                    t = 9 + s
                    pe.wait_ge(tile_out, t + 1)
                    if s > 4:
                        pe.wait_ge(g_vev, 2 * (s - 4))
                    unit(n + t, 4 + t % 4, h_hi, h_lo, KT)
                    if s >= 4:
                        for v in (2 * (s - 4), 2 * (s - 4) + 1):
                            pe.wait_ge(tile_out, max(t + 2 + v % 2, 4 + 9 + v + 1))
                            for c in range(TT):
                                mm = pe.transpose(ps[:, 4 + (t + 1 + v % 2) % 4, c * P:(c + 1) * P], gla_vT[:, v, c * P:(c + 1) * P], ident[:, :])
                            mm.then_inc(g_vt, 1)
                    if s:
                        level(s - 1)
                level(LEVELS)

                def r_unit(v):
                    t = 17 + v
                    pe.wait_ge(tile_out, t + 1)
                    unit(n + t, 4 + t % 4, h_hi, h_lo, KT)
                pe.wait_ge(g_vev, GVT)
                for v in range(3):
                    r_unit(v)
                pe.wait_ge(g_decm, 3)
                for c in range(TT):
                    pe.wait_ge(g_mask, TT * LEVELS + c + 1)
                    for h in range(GH):
                        mm = pe.transpose(ps[:, c, h * P:(h + 1) * P], gla_k[:, h, c * P:(c + 1) * P], ident[:, :])
                    mm.then_inc(g_kt, 1)
                for c in range(TT):
                    if c:
                        pe.wait_ge(g_oev, 2 * c)
                        pe.wait_ge(g_S, GH * c)
                    else:
                        pe.wait_ge(g_kev, TT)
                    for m in range(GVT):
                        h, vt = m // 2, m % 2
                        dst = ps[:, 2 + m // 4, (m % 4) * P:(m % 4 + 1) * P]
                        if c:
                            pe.matmul(dst, gla_state[:, h, vt * P:(vt + 1) * P], gla_q[:, h, c * P:(c + 1) * P], start=True, stop=False, skip_group_check=True)
                        mm = pe.matmul(dst, gla_v[:, c, m * P:(m + 1) * P], gla_attn[:, c, h, :], start=c == 0, stop=True, skip_group_check=True)
                    mm.then_inc(g_o, 1)
                    if c < TT - 1:
                        for h in range(GH):
                            pe.matmul(ps[:, h // 2, (h % 2) * GDV:(h % 2 + 1) * GDV], gla_k_turned[:, c, h, :],
                                      gla_v[:, c, h * GDV:(h + 1) * GDV], start=True, stop=True, skip_group_check=True).then_inc(g_st, 1)
                        r_unit(3 + c)
                R = slice(DT0, DT0 + SH)
                pe.wait_ge(s_acum, TT)
                pe.wait_ge(g_S, GH * (TT - 1))
                for b in range(2):
                    for c in range(TT):
                        src = (small[R, c * P:(c + 1) * P], dt_tmp[R, 2, c * P:(c + 1) * P])[b]
                        mm = pe.transpose(ps[:, 0, (b * TT + c) * SH:(b * TT + c + 1) * SH], src, ident[R, R])
                mm.then_inc(s_tok, 1)
                r_unit(6)
                z = NORMS["gla"]
                for h in range(GH):
                    pe.wait_ge(sq_paired, h // 2 + 1)
                    sums(osq[:, h, 0, :], h * TT).then_inc(ss_done, 1)
                r_unit(7)
                pe.wait_ge(s_tokev, 1)
                spread(z, [0, 1, 2, 3])
                n0 = n + 25
                for m in range(KT):
                    if m >= 4:
                        pe.wait_ge(x_upd, XB["mix0"] + m - 3)
                    unit(n0 + m, 4 + m % 4, o_hi, o_lo, KT, 0, ready_of(OPS["gla"]) if m == 0 else None)
                n0 += KT
                tb = 25
                with pe.Fori(0, XT // 4) as i:
                    for j in range(4):
                        pe.wait_ge(x_upd, XB["mix0"] + KT - 3 + (tb + j) % 4)
                        pe.wait_ge(tile_out, tb + j + 1 + 4 * i)
                        unit(n0 + j, 4 + (tb + j) % 4, h_hi, h_lo, KT, i)
                n0 += XT

                def z_unit(m):
                    if m >= 3:
                        pe.wait_ge(z_out, m - 2)
                    unit(n0 + m, Z_BANKS[m % 3], h_hi, h_lo, KT)
                z_unit(0)
                pe.wait_ge(s_silu, XT)
                for c in range(TT):
                    if c:
                        pe.wait_ge(s_cbm, c)
                        pe.wait_ge(s_Bev, c)
                        pe.wait_ge(s_S2, c)
                    cc = slice(c * P, (c + 1) * P)
                    for g in range(SG):
                        mm = pe.matmul(ps[:, 0, g * P:(g + 1) * P], xbc[:, 8 + g, cc], xbc[:, 10 + g, cc], start=True, stop=True, skip_group_check=True)
                    for g in range(SG):
                        mm = pe.transpose(ps[:, 0, (SG + g) * P:(SG + g + 1) * P], xbc[:, 8 + g, cc], ident[:, :])
                    mm.then_inc(s_trB, 1)
                    for m in range(SI // P):
                        mm = pe.transpose(ps[:, 2 + m // 4, (m % 4) * P:(m % 4 + 1) * P], xbc[:, m, cc], ident[:, :])
                    mm.then_inc(s_tr, 1)
                    z_unit(2 * c + 1)
                    if c < TT - 1:
                        pe.wait_ge(s_Bev, c + 1)
                        pe.wait_ge(s_xdtw, c + 1)
                        for g in range(SG):
                            mm = pe.matmul(ps[:, 2 + g, :], ssd_B[:, g, :], xdtw[:, g * 512:(g + 1) * 512], start=True, stop=True)
                        mm.then_inc(s_st, 1)
                    pe.wait_ge(s_P, 2 * (c + 1))
                    pe.wait_ge(s_C, 2 * (c + 1))
                    if c:
                        pe.wait_ge(s_yev, c)
                    else:
                        pe.wait_ge(tile_out, 4 + 25 + XT)
                    for h in range(SH):
                        m = h // 2
                        dst = ps[(h % 2) * SHD:(h % 2 + 1) * SHD, 4 + m // 4, (m % 4) * P:(m % 4 + 1) * P]
                        if c:
                            pe.matmul(dst, ssd_state[:, h * SHD:(h + 1) * SHD], acum_rows[:, c % 2, h, :], start=True, stop=False, skip_group_check=True)
                        mm = pe.matmul(dst, xdt[:, h * SHD:(h + 1) * SHD], ssd_attn[:, c % 2, h, :], start=c == 0, stop=True, skip_group_check=True)
                    mm.then_inc(s_y, 1)
                    if c < TT - 1:
                        z_unit(2 * c + 2)
                z = NORMS["ssd"]
                n0 = n + NU["mix0"] - KT
                half = KT // SG
                for m in range(KT):
                    u, bank = n0 + m, GROUP_BANKS[m % 3]
                    if m >= 3:
                        pe.wait_ge(x_upd, XB["mix0"] + KT + m - 2)
                    pe.wait_ge(lo_ready, u + 1)
                    for k in range(KT):
                        if m == 0:
                            pe.wait_ge(opnd_ready, OPS["ssd"] + k + 1)
                        dst, st, en = ps[:, bank + k // half, :], k % half == 0, k % half == half - 1
                        wh, wl = w_hi[:, u % SLOTS, k * P:(k + 1) * P], w_lo[:, u % SLOTS, k * P:(k + 1) * P]
                        pe.matmul(dst, wh, y_hi[:, k, :], start=st, stop=False)
                        pe.matmul(dst, wh, y_lo[:, k, :], start=False, stop=False)
                        mm = pe.matmul(dst, wl, y_hi[:, k, :], start=False, stop=en)
                        if m == 2 and k == half - 1:
                            spread(z, [0, 1])
                    mm.then_inc(unit_used, 1)
                    if m == 1:
                        pe.wait_ge(sq_tree, 2 * SG)
                        for g in range(SG):
                            mm = sums(ysq[:, 4 * g, :], g * TT, 1)
                        mm.then_inc(ss_done, 1)

            def mix1(nxt):
                n = UB["mix1"]

                def latent_sums(rows, tiles, bank, c0):
                    for j in tiles:
                        for t in range(TT):
                            mm = pe.matmul(ps[:, bank, c0 + t:c0 + t + 1], sq[0:rows, j, t * P:(t + 1) * P], ones[0:rows, 0:1],
                                           start=j == tiles[0] and t == 0, stop=j == tiles[-1], skip_group_check=True)
                    return mm

                def latent_spread(bank, c0):
                    for t in range(TT):
                        mm = pe.matmul(ps[:, bank, t * P:(t + 1) * P], rs[:, 1, c0 + t:c0 + t + 1].to_broadcast([P, P]), ident[:, :],
                                       start=True, stop=True, skip_group_check=True)
                    return mm
                for t in range(4):
                    pe.wait_ge(x_upd, XB["mix1"] - 3 + (T1 + t) % 4)
                    pe.wait_ge(tile_out, T1 + t + 1)
                    if t == 0:
                        continue
                    if t == 1:
                        first_units(n, [4 + (T1 + u) % 4 for u in range(2)], "mix1")
                        continue
                    unit(n + t, 4 + (T1 + t) % 4, h_hi, h_lo, KT)
                    if t == 2:
                        pe.wait_ge(d_raw, 2)
                        latent_sums(P, (0, 1), 2, 0).then_inc(d_ss, 1)
                pe.wait_ge(d_rs, 1)
                latent_spread(0, 0).then_inc(d_bc, 1)
                pe.wait_ge(a_const, 2)
                pe.wait_ge(d_kx, 1)
                pe.matmul(ps[0:IDIM, 1, :], cmat[:, :], index_k_raw[0:IDIM, :], start=True, stop=True).then_inc(d_cen, 1)
                R = slice(IDIM, IDIM + IH)
                pe.wait_ge(tile_out, T1 + 4 + 4)
                for c in range(TT):
                    mm = pe.transpose(ps[:, 2, c * IH:(c + 1) * IH], index_k_raw[R, c * P:(c + 1) * P], ident[R, R])
                mm.then_inc(d_tr, 1)
                pe.wait_ge(d_raw, 3)
                pe.wait_ge(rb_ready, XNORM["mix1"] + 1)
                latent_sums(P, (2,), 3, 4)
                pe.wait_ge(d_sq, 1)
                latent_sums(IDIM, (3,), 3, 8).then_inc(d_ss, 1)
                pe.wait_ge(d_ql, 2)
                for u in range(6):
                    s = (n + 4 + u) % SLOTS
                    pe.wait_ge(lo_ready, n + 4 + u + 1)
                    for j in range(4):
                        t = 4 * u + j
                        pe.wait_ge(tile_out, T1 + 4 + t + 1)
                        dst = ps[:, 4 + (T1 + t) % 4, :]
                        for k in range(2):
                            c0 = k * 512 + j * P
                            wh, wl = w_hi[:, s, c0:c0 + P], w_lo[:, s, c0:c0 + P]
                            pe.matmul(dst, wh, q_latent_hi[:, k, :], start=k == 0, stop=False)
                            pe.matmul(dst, wh, q_latent_lo[:, k, :], start=False, stop=False)
                            mm = pe.matmul(dst, wl, q_latent_hi[:, k, :], start=False, stop=k == 1)
                        mm.then_inc(unit_used if j == 3 else d_tile, 1)
                    if u == 0:
                        pe.wait_ge(d_rs, 2)
                        pe.wait_ge(d_kc, 1)
                        latent_spread(1, 4)
                        latent_spread(3, 8).then_inc(d_bc, 1)
                    if u == 1:
                        pe.wait_ge(d_kv, 1)
                        for c in range(TT):
                            mm = pe.transpose(ps[:, 0, c * P:(c + 1) * P], kvT[:, c * P:(c + 1) * P], ident[:, :])
                        mm.then_inc(d_tr, 1)
                pe.wait_ge(d_dup, 16)
                for r in range((TT - 1) * IH):
                    b, h = r // IH + 1, r % IH
                    w = P * (b + 1)
                    R = slice((h % 2) * IDIM, (h % 2 + 1) * IDIM)
                    if r >= 4:
                        pe.wait_ge(d_relu, r - 3)
                    pe.matmul(ps[:, r % 4, 0:w], index_q[R, h // 2, b * P:(b + 1) * P], index_k[R, 0:w], start=True, stop=True).then_inc(d_ix, 1)
                pe.wait_ge(d_relu, (TT - 1) * IH)
                pe.wait_ge(tile_out, T1 + 4 + 4 + KT + AH)
                pe.wait_ge(uv_landed, 16)
                NR = TT * AH

                def p_turn(r):
                    b = r // AH
                    pe.wait_ge(a_nrm, r + 1)
                    if r >= 2:
                        pe.wait_ge(a_pt, r - 1)
                    for st in range(b + 1):
                        mm = pe.transpose(ps[:, 2 + r % 2, st * P:(st + 1) * P], probs[:, r % RING, st * P:(st + 1) * P], ident[:, :])
                    mm.then_inc(a_tr, 1)

                def latent(r):
                    b, g = r // AH, r // 4
                    pe.wait_ge(a_pt, r + 1)
                    if r % 4 == 0 and g >= 2:
                        pe.wait_ge(a_ol, g - 1)
                    for st in range(b + 1):
                        mm = pe.matmul(ps[:, 4 + g % 2, (r % 4) * P:(r % 4 + 1) * P], kvtok[:, st, :], probs_T[:, r % 2, st * P:(st + 1) * P],
                                       start=st == 0, stop=st == b, skip_group_check=True)
                    mm.then_inc(a_pv, 1)

                def values(g):
                    pe.wait_ge(a_ol, g + 1)
                    if g >= 4:
                        pe.wait_ge(a_o, g // 2 - 1)
                    for j in range(4):
                        h = (4 * g + j) % AH
                        m = h // 2
                        mm = pe.matmul(ps[(h % 2) * AV:(h % 2 + 1) * AV, 6 + m // 4, (m % 4) * P:(m % 4 + 1) * P], w_uv_sb[:, h, :],
                                       o_latent[:, g % 2, j * P:(j + 1) * P], start=True, stop=True, skip_group_check=True)
                    mm.then_inc(a_uv, 1)
                for r in range(NR + LAG + 3):
                    if r < NR:
                        b, h = r // AH, r % AH
                        w = P * (b + 1)
                        if h == 0:
                            pe.wait_ge(k_mask, b + 1)
                        if r >= 2:
                            pe.wait_ge(a_max, r - 1)
                        pe.matmul(ps[:, r % 2, 0:w], att_q[:, h, b * P:(b + 1) * P], kvT[:, 0:w], start=True, stop=False)
                        pe.matmul(ps[:, r % 2, 0:w], identr[:, :], att_mask[:, b, 0:w], start=False, stop=True).then_inc(a_log, 1)
                    if LAG <= r < NR + LAG:
                        p_turn(r - LAG)
                    if LAG + 1 <= r < NR + LAG + 1:
                        latent(r - LAG - 1)
                    if r >= LAG + 3 and (r - LAG - 3) % 4 == 3 and (r - LAG - 3) // 4 < NR // 4:
                        values((r - LAG - 3) // 4)
                n0 = n + NU["mix1"] - KT
                z = NORMS[nxt]
                for m in range(KT):
                    if m >= 4:
                        pe.wait_ge(x_upd, XB["mix1"] + m - 3)
                    unit(n0 + m, 4 + m % 4, o_hi, o_lo, KT, 0, ready_of(OPS["dsa"]) if m == 0 else None)

            pe.wait_ge(consts_ready, 3)
            pe.wait_ge(par_landed, 16 * 9)
            pe.transpose(ps[:, 0, 0:83], prow[0:83, 0, :], ident[0:83, 0:83]).then_inc(par_done, 1)
            pe.transpose(ps[:, 1, 0:48], prow[0:48, 1, :], ident[0:48, 0:48]).then_inc(par_done, 1)
            pe.wait_ge(x_landed, 16)
            for m in range(KT):
                if m >= 4:
                    pe.wait_ge(x_upd, m - 3)
                for t in range(TT):
                    mm = pe.transpose(ps[:, 4 + m % 4, t * P:(t + 1) * P], x_in[:, t, m * P:(m + 1) * P], ident[:, :])
                mm.then_inc(xt_done, 1)
            pe.wait_ge(l_landed, 32)
            pe.wait_ge(x_upd, KT)
            pe.matmul(ps[0:AH, 4, :], rel_bias_sb[:, :], bucket_sb[:, 0:TOK], start=True, stop=True)
            pe.matmul(ps[0:AH, 5, 0:P], rel_bias_sb[:, :], bucket_sb[:, TOK:LINE], start=True, stop=True).then_inc(l_mm, 1)
            for k, st in enumerate(STAGES):
                nxt = (STAGES + ["final"])[k + 1]
                if st.startswith("ffn"):
                    ffn(st, nxt)
                elif st == "mix0":
                    mix0(nxt)
                else:
                    mix1(nxt)
            sumsq_x("final")
            for t in range(TT):
                for c in range(2):
                    if 2 * t + c >= 4:
                        pe.wait_ge(fin_ready, 2 * t + c - 3)
                    for m in range(4):
                        mm = pe.transpose(ps[:, 4 + (2 * t + c) % 4, m * P:(m + 1) * P],
                                          x[:, 4 * c + m, t * P:(t + 1) * P], ident[:, :])
                    mm.then_inc(fin_t, 1)


_INS = ["x", "ffn_norm_g", "ffn_w_gate", "ffn_w_up", "ffn_w_down", "mix_norm_g", "final_norm_g",
        "hy_w_in", "gla_w_gate2", "gla_b_gate", "gla_norm_g", "ssd_conv_w", "ssd_conv_b", "ssd_dt_bias", "ssd_a_log",
        "ssd_d", "ssd_norm_g", "hy_w_out",
        "dsa_w_dq", "dsa_q_norm_g", "dsa_w_uq", "dsa_w_dkv", "dsa_kv_norm_g", "dsa_w_uv", "dsa_w_o",
        "idx_w_q", "idx_w_k", "idx_ln_g", "idx_ln_b", "idx_w_w", "rel_bias"]


def _CONSTS():
    import math
    import numpy as np

    dist = np.maximum(TOK - 1 - np.arange(LINE), 0)
    exact = REL_BUCKETS // 2
    large = exact + (np.log(np.maximum(dist, 1).astype(np.float32) / np.float32(exact))
                     / np.float32(math.log(REL_MAX_DIST / exact)) * np.float32(REL_BUCKETS - exact)).astype(np.int32)
    bucket = np.where(dist < exact, dist, np.minimum(large, REL_BUCKETS - 1))
    return {"bucket_onehot": (bucket[None, :] == np.arange(REL_BUCKETS)[:, None]).astype(np.float32)}


def kernel(**inputs):
    import numpy as np
    import concourse.bacc as bacc
    from concourse.bass_utils import run_bass_kernel_spmd

    nc = bacc.Bacc("TRN2", target_bir_lowering=False, num_devices=1)
    arrays, aps = {}, {}
    for name in _INS:
        arrays[f"in_{name}"] = np.ascontiguousarray(inputs[name])
        aps[name] = nc.dram_tensor(f"in_{name}", arrays[f"in_{name}"].shape, F32, kind="ExternalInput").ap()
    for name, value in _CONSTS().items():
        arrays[f"in_{name}"] = value
        aps[name] = nc.dram_tensor(f"in_{name}", value.shape, F32, kind="ExternalInput").ap()
    out = nc.dram_tensor("out", (1, TOK, D), F32, kind="ExternalOutput").ap()
    build_program(nc, aps, out)
    got = run_bass_kernel_spmd(nc, [arrays], core_ids=[0])
    return got.results[0]["out"]
```
